# Optimizing a Trainium2 kernel written in Bass

```python
import jax, jax.numpy as jnp
from jax import lax
import numpy as np

D_MODEL = 1024
BATCH = 1
SEQ = 1024
DEPTH = 1

N_MEM = 256
MEM_HEADS = 4
MEM_HEAD_DIM = D_MODEL // MEM_HEADS
D_MIX = D_MODEL
GLA_WIDTH = D_MIX // 2
GLA_HEADS = 4
GLA_DV = GLA_WIDTH // GLA_HEADS
GLA_DK = GLA_DV // 2
GLA_KEY_WIDTH = GLA_HEADS * GLA_DK
GLA_GATE_RANK = 16
GLA_GATE_NORMALIZER = 16.0
GLA_CHUNK = 64
GLA_NORM_EPS = 1e-5
RWKV_WIDTH = D_MIX - GLA_WIDTH
RWKV_HEAD = 64
RWKV_HEADS = RWKV_WIDTH // RWKV_HEAD
RWKV_DECAY_RANK = 64
RWKV_AAA_RANK = 64
RWKV_GATE_RANK = 128
RWKV_LN_EPS = 64e-5
D_FF = -(-8 * D_MODEL // (3 * 256)) * 256
NORM_EPS = 1e-6

GLA_COLS = (GLA_KEY_WIDTH, GLA_KEY_WIDTH, GLA_WIDTH, GLA_WIDTH, GLA_GATE_RANK)
RWKV_COLS = (RWKV_WIDTH, RWKV_WIDTH, RWKV_WIDTH, RWKV_DECAY_RANK, RWKV_AAA_RANK, RWKV_GATE_RANK)
N_GLA_COLS = sum(GLA_COLS)
N_RWKV_COLS = sum(RWKV_COLS)
D_IN_PROJ = N_GLA_COLS + N_RWKV_COLS

kernel_name = "hymba_gla_rwkv7_memory_block"

def _split(z, cols):
    idx = tuple(int(i) for i in np.cumsum(cols)[:-1])
    return jnp.split(z, idx, axis=-1)

def rms_norm(x, g, eps=NORM_EPS):
    xf = x.astype(jnp.float32)
    y = xf * lax.rsqrt(jnp.mean(xf * xf, axis=-1, keepdims=True) + eps)
    return (y * g.astype(jnp.float32)).astype(x.dtype)

def token_shift(z):
    return jnp.pad(z[:, :-1], ((0, 0), (1, 0), (0, 0)))

def gla_chunked(q, k, v, log_a):
    B, T, H, DK = q.shape
    DV = v.shape[-1]
    C = GLA_CHUNK
    N = T // C
    q, k, log_a = (t.reshape(B, N, C, H, DK) for t in (q, k, log_a))
    v = v.reshape(B, N, C, H, DV)
    b = jnp.cumsum(log_a, axis=2)
    b_last = b[:, :, -1:]
    q_dec = q * jnp.exp(b)
    k_inv = k * jnp.exp(-b)
    k_tail = k * jnp.exp(b_last - b)
    causal = jnp.tril(jnp.ones((C, C), dtype=bool))
    scores = jnp.einsum('bnchk,bnshk->bnhcs', q_dec, k_inv)
    scores = jnp.where(causal, scores, 0.0)
    o_intra = jnp.einsum('bnhcs,bnshv->bnchv', scores, v)
    d_state = jnp.einsum('bnshk,bnshv->bnhkv', k_tail, v)
    chunk_decay = jnp.exp(b_last[:, :, 0])

    def step(S, inp):
        dec, dS = inp
        return S * dec[..., None] + dS, S

    S0 = jnp.zeros((B, H, DK, DV), d_state.dtype)
    _, S_prev = lax.scan(step, S0, (jnp.moveaxis(chunk_decay, 1, 0), jnp.moveaxis(d_state, 1, 0)))
    S_prev = jnp.moveaxis(S_prev, 0, 1)
    o_inter = jnp.einsum('bnchk,bnhkv->bnchv', q_dec, S_prev)
    return (o_intra + o_inter).reshape(B, T, H, DV)

def gla_mixer(z, wa2, ba, norm_g):
    B, T, _ = z.shape
    f32 = jnp.float32
    q, k, v, g, a_lo = _split(z, GLA_COLS)
    log_a = jax.nn.log_sigmoid((a_lo @ wa2 + ba).astype(f32)) / GLA_GATE_NORMALIZER
    q = q.astype(f32).reshape(B, T, GLA_HEADS, GLA_DK) * (GLA_DK ** -0.5)
    k = k.astype(f32).reshape(B, T, GLA_HEADS, GLA_DK)
    v = v.astype(f32).reshape(B, T, GLA_HEADS, GLA_DV)
    log_a = log_a.reshape(B, T, GLA_HEADS, GLA_DK)
    o = gla_chunked(q, k, v, log_a)
    o = o * lax.rsqrt(jnp.mean(o * o, axis=-1, keepdims=True) + GLA_NORM_EPS) * norm_g.astype(f32)
    o = o * jax.nn.silu(g.astype(f32).reshape(B, T, GLA_HEADS, GLA_DV))
    return o.reshape(B, T, GLA_WIDTH).astype(z.dtype)

def rwkv7_scan(r, w, k, v, a, b):
    B, T, H, N = r.shape

    def step(S, inp):
        r_t, w_t, k_t, v_t, a_t, b_t = inp
        sa = jnp.einsum('bhij,bhj->bhi', S, a_t)
        S = S * w_t[:, :, None, :] + sa[..., None] * b_t[:, :, None, :] + v_t[..., None] * k_t[:, :, None, :]
        return S, jnp.einsum('bhij,bhj->bhi', S, r_t)

    xs = tuple(jnp.moveaxis(t.astype(jnp.float32), 1, 0) for t in (r, w, k, v, a, b))
    S0 = jnp.zeros((B, H, N, N), jnp.float32)
    _, y = lax.scan(step, S0, xs)
    return jnp.moveaxis(y, 0, 1)

def rwkv7_mixer(z, mu, w0, w2, a0, a2, g2, k_k, k_a, r_k, ln_g, ln_b):
    B, T, _ = z.shape
    H, N = RWKV_HEADS, RWKV_HEAD
    f32 = jnp.float32
    z = z + (token_shift(z) - z) * mu
    r, k, v, w_lo, a_lo, g_lo = _split(z, RWKV_COLS)
    w_raw = -jax.nn.softplus(-(w0 + jnp.tanh(w_lo) @ w2).astype(f32)) - 0.5
    w = jnp.exp(-jnp.exp(w_raw))
    a = jax.nn.sigmoid((a0 + a_lo @ a2).astype(f32))
    g = jax.nn.sigmoid(g_lo) @ g2
    k = k.astype(f32)
    kk = (k * k_k).reshape(B, T, H, N)
    kk = kk / jnp.maximum(jnp.sqrt(jnp.sum(kk * kk, axis=-1, keepdims=True)), 1e-12)
    k = k * (1.0 + (a - 1.0) * k_a)
    hd = lambda t: t.reshape(B, T, H, N)
    r_h, w_h, k_h, v_h, a_h = hd(r.astype(f32)), hd(w), hd(k), hd(v.astype(f32)), hd(a)
    y = rwkv7_scan(r_h, w_h, k_h, v_h, -kk, kk * a_h)
    mean = jnp.mean(y, axis=-1, keepdims=True)
    var = jnp.mean(jnp.square(y - mean), axis=-1, keepdims=True)
    y = (y - mean) * lax.rsqrt(var + RWKV_LN_EPS) * ln_g.reshape(H, N) + ln_b.reshape(H, N)
    bonus = jnp.sum(r_h * k_h * r_k, axis=-1, keepdims=True) * v_h
    y = (y + bonus).reshape(B, T, RWKV_WIDTH) * g.astype(f32)
    return y.astype(z.dtype)

def memory_cross_attention(h, mem_n, wq, wkv, wo):
    B, T, _ = h.shape
    M = mem_n.shape[1]
    q = (h @ wq).reshape(B, T, MEM_HEADS, MEM_HEAD_DIM)
    k, v = jnp.split(mem_n @ wkv, 2, axis=-1)
    k = k.reshape(B, M, MEM_HEADS, MEM_HEAD_DIM)
    v = v.reshape(B, M, MEM_HEADS, MEM_HEAD_DIM)
    s = jnp.einsum('bthd,bmhd->bhtm', q, k).astype(jnp.float32) * (MEM_HEAD_DIM ** -0.5)
    p = jax.nn.softmax(s, axis=-1).astype(v.dtype)
    o = jnp.einsum('bhtm,bmhd->bthd', p, v).reshape(B, T, D_MODEL)
    return o @ wo

def swiglu_ffn(h, w_gate_up, w_down):
    gate, up = jnp.split(h @ w_gate_up, 2, axis=-1)
    return (jax.nn.silu(gate) * up) @ w_down

def hybrid_layer(x, mem, norm_mix_g, w_in, gla_wa2, gla_ba, gla_norm_g, rwkv_mu, rwkv_w0, rwkv_w2,
                 rwkv_a0, rwkv_a2, rwkv_g2, rwkv_k_k, rwkv_k_a, rwkv_r_k, rwkv_ln_g, rwkv_ln_b, w_out,
                 norm_mem_x_g, norm_mem_g, wq_mem, wkv_mem, wo_mem, norm_ffn_g, w_gate_up, w_down):
    h = rms_norm(x, norm_mix_g)
    z = h @ w_in
    o_gla = gla_mixer(z[..., :N_GLA_COLS], gla_wa2, gla_ba, gla_norm_g)
    o_rwkv = rwkv7_mixer(z[..., N_GLA_COLS:], rwkv_mu, rwkv_w0, rwkv_w2, rwkv_a0, rwkv_a2, rwkv_g2,
                         rwkv_k_k, rwkv_k_a, rwkv_r_k, rwkv_ln_g, rwkv_ln_b)
    x = x + jnp.concatenate([o_gla, o_rwkv], axis=-1) @ w_out
    x = x + memory_cross_attention(rms_norm(x, norm_mem_x_g), rms_norm(mem, norm_mem_g), wq_mem, wkv_mem, wo_mem)
    x = x + swiglu_ffn(rms_norm(x, norm_ffn_g), w_gate_up, w_down)
    return x

def setup_inputs(seed: int = 0) -> dict:
    key = jax.random.key(seed)
    ks = iter(jax.random.split(key, 32))
    f32 = jnp.float32
    L = DEPTH

    def nrm(shape, scale):
        return jax.random.normal(next(ks), shape, f32) * scale

    def gain(shape):
        return 1.0 + nrm(shape, 0.02)

    return {
        "x": nrm((BATCH, SEQ, D_MODEL), 1.0),
        "mem": nrm((BATCH, N_MEM, D_MODEL), 1.0),
        "norm_mix_g": gain((L, D_MODEL)),
        "w_in": nrm((L, D_MODEL, D_IN_PROJ), D_MODEL ** -0.5),
        "gla_wa2": nrm((L, GLA_GATE_RANK, GLA_KEY_WIDTH), GLA_GATE_RANK ** -0.5),
        "gla_ba": nrm((L, GLA_KEY_WIDTH), 0.1),
        "gla_norm_g": gain((L, GLA_DV)),
        "rwkv_mu": jax.random.uniform(next(ks), (L, N_RWKV_COLS), f32),
        "rwkv_w0": jax.random.uniform(next(ks), (L, RWKV_WIDTH), f32, -6.0, -1.0),
        "rwkv_w2": nrm((L, RWKV_DECAY_RANK, RWKV_WIDTH), 0.5 * RWKV_DECAY_RANK ** -0.5),
        "rwkv_a0": nrm((L, RWKV_WIDTH), 0.1),
        "rwkv_a2": nrm((L, RWKV_AAA_RANK, RWKV_WIDTH), RWKV_AAA_RANK ** -0.5),
        "rwkv_g2": nrm((L, RWKV_GATE_RANK, RWKV_WIDTH), RWKV_GATE_RANK ** -0.5),
        "rwkv_k_k": 0.85 + nrm((L, RWKV_WIDTH), 0.02),
        "rwkv_k_a": 1.0 + nrm((L, RWKV_WIDTH), 0.02),
        "rwkv_r_k": nrm((L, RWKV_HEADS, RWKV_HEAD), 0.1),
        "rwkv_ln_g": gain((L, RWKV_WIDTH)),
        "rwkv_ln_b": nrm((L, RWKV_WIDTH), 0.02),
        "w_out": nrm((L, D_MIX, D_MODEL), D_MIX ** -0.5),
        "norm_mem_x_g": gain((L, D_MODEL)),
        "norm_mem_g": gain((L, D_MODEL)),
        "wq_mem": nrm((L, D_MODEL, D_MODEL), D_MODEL ** -0.5),
        "wkv_mem": nrm((L, D_MODEL, 2 * D_MODEL), D_MODEL ** -0.5),
        "wo_mem": nrm((L, D_MODEL, D_MODEL), D_MODEL ** -0.5),
        "norm_ffn_g": gain((L, D_MODEL)),
        "w_gate_up": nrm((L, D_MODEL, 2 * D_FF), D_MODEL ** -0.5),
        "w_down": nrm((L, D_FF, D_MODEL), D_FF ** -0.5),
        "norm_final_g": gain((D_MODEL,)),
    }

def reference(x, mem, norm_mix_g, w_in, gla_wa2, gla_ba, gla_norm_g, rwkv_mu, rwkv_w0, rwkv_w2,
              rwkv_a0, rwkv_a2, rwkv_g2, rwkv_k_k, rwkv_k_a, rwkv_r_k, rwkv_ln_g, rwkv_ln_b, w_out,
              norm_mem_x_g, norm_mem_g, wq_mem, wkv_mem, wo_mem, norm_ffn_g, w_gate_up, w_down,
              norm_final_g):
    for l in range(DEPTH):
        x = hybrid_layer(x, mem, norm_mix_g[l], w_in[l], gla_wa2[l], gla_ba[l], gla_norm_g[l], rwkv_mu[l],
                         rwkv_w0[l], rwkv_w2[l], rwkv_a0[l], rwkv_a2[l], rwkv_g2[l], rwkv_k_k[l], rwkv_k_a[l],
                         rwkv_r_k[l], rwkv_ln_g[l], rwkv_ln_b[l], w_out[l], norm_mem_x_g[l], norm_mem_g[l],
                         wq_mem[l], wkv_mem[l], wo_mem[l], norm_ffn_g[l], w_gate_up[l], w_down[l])
    return rms_norm(x, norm_final_g)


_drawn_inputs = setup_inputs


def setup_inputs(seed=0):
    import zlib

    import numpy as np

    out = dict(_drawn_inputs(seed))
    spreads = {}
    factors = {'gla_ba': 2.998,
     'gla_norm_g': 6.596,
     'rwkv_w2': 6.428,
     'rwkv_a0': 3.956,
     'rwkv_k_k': 7.672,
     'rwkv_k_a': 7.38,
     'rwkv_ln_g': 7.72,
     'rwkv_ln_b': 7.964,
     'norm_mem_x_g': 8.0,
     'norm_mem_g': 8.0,
     'norm_ffn_g': 4.331,
     'norm_final_g': 3.117}
    for name, (base, spread) in spreads.items():
        noise = np.random.default_rng([zlib.crc32(name.encode()), seed]).standard_normal(out[name].shape)
        drawn = base * np.exp(spread * noise) if base else spread * noise
        out[name] = __import__('jax').numpy.asarray(drawn.astype(out[name].dtype))
    for name, factor in factors.items():
        out[name] = (out[name] * factor).astype(out[name].dtype)
    return out
```

```python
from contextlib import ExitStack

import numpy as np

import concourse.bass as bass
from concourse import mybir

F32 = mybir.dt.float32
ALU = mybir.AluOpType
ACT = mybir.ActivationFunctionType

P = 128
D = 1024
KD = D // P
T = 1024
NC = T // P
HALF = 512
NH = T // HALF
M = 256
EPS = 1e-6
GH, GK, GV = 4, 64, 128
G_EPS = 1e-5
RANK = 16
G_COLS = 1552
RH, RN = 8, 64
RT = RH * RN // P
R_EPS = 64e-5
R_TILES = 14
AH, AD = 4, 256
FF = 2816
FT = FF // P

CONSTS = ["ident", "ones", "pair_ones", "cum_in", "cum_ex", "up_strict", "up_incl", "diag_up",
          "diag_lo", "merge16", "merge32", "merge64"]
PARAMS = [("norm_mix_g", KD), ("norm_mem_x_g", KD), ("norm_mem_g", KD), ("norm_ffn_g", KD),
          ("norm_final_g", KD), ("gla_norm_g", 1), ("rwkv_mu", R_TILES), ("rwkv_k_k", RT),
          ("rwkv_k_a", RT), ("rwkv_r_k", RT), ("rwkv_ln_g", RT), ("rwkv_ln_b", RT)]
ROWS = [("gla_ba", GH * GK), ("rwkv_w0", RH * RN), ("rwkv_a0", RH * RN)]


class Kept:

    def __init__(self):
        self.const, self.par, self.row = {}, {}, {}


def constants():
    s = np.arange(P)[:, None]
    t = np.arange(P)[None, :]
    mid = s <= P // 2 - 1
    same = lambda n: s // n == t // n
    return np.concatenate([np.asarray(m, np.float32) for m in (
        s == t, np.ones((P, P)), same(RN),
        (s <= t) * 1.0 - mid, (s < t) * 1.0 - mid,
        s < t, s <= t, (s < t) & same(16),
        (s > t) & same(16), (s > t) & same(32) & ~same(16), (s > t) & same(64) & ~same(32),
        (s > t) & ~same(64))], axis=1)


def at(steps, name, turn):
    return turn * len(steps) + steps.index(name) + 2


def before(steps, turn):
    return turn * len(steps) + 1


def tiles(nc, ctx, prefix):
    def sb(name, shape):
        return ctx.enter_context(nc.sbuf_tensor(f"{prefix}_{name}", shape, F32))

    def ps(name, shape):
        return ctx.enter_context(nc.psum_tensor(f"{prefix}_{name}", shape, F32))

    def sem(name):
        return ctx.enter_context(nc.semaphore(f"{prefix}_{name}"))
    return sb, ps, sem


def wide(scalars, n):
    return scalars.unsqueeze(2).to_broadcast([scalars.shape[0], scalars.shape[1], n])


def transpose_in(nc, k, name, src, dst, n_tok):
    nt = n_tok // P
    rows = src.rearrange("(c p) f -> c p f", p=P)
    with ExitStack() as ctx:
        sb, ps, sem = tiles(nc, ctx, name)
        tok = sb("tok", [P, 2, D])
        bank = ps("bank", [P, 2, KD, P])
        landed = [sem("landed0"), sem("landed1")]
        turned, copied = sem("turned"), sem("copied")
        with nc.Block() as block:
            @block.sync
            def _(sp):
                for c in range(nt):
                    if c >= 2:
                        sp.wait_ge(turned, c - 1)
                    sp.dma_start(tok[:, c % 2, :], rows[c]).then_inc(landed[c % 2], 16)

            @block.tensor
            def _(pe):
                for c in range(nt):
                    pe.wait_ge(landed[c % 2], 16 * (c // 2 + 1))
                    if c >= 2:
                        pe.wait_ge(copied, c - 1)
                    for f in range(KD):
                        mm = nc.tensor.transpose(bank[:, c % 2, f, :], tok[:, c % 2, f * P:(f + 1) * P],
                                                 k.const["ident"])
                    mm.then_inc(turned, 1)

            @block.vector
            def _(dve):
                for c in range(nt):
                    dve.wait_ge(turned, c + 1)
                    nc.vector.tensor_copy(dst[:, :, c * P:(c + 1) * P], bank[:, c % 2]).then_inc(copied, 1)


def rms_norm(nc, k, name, src, dst, gain, n_tok):
    w = min(HALF, n_tok)
    nh = n_tok // w
    with ExitStack() as ctx:
        sb, ps, sem = tiles(nc, ctx, name)
        sq = sb("sq", [P, 2, n_tok])
        root = sb("root", [P, n_tok])
        rstd = sb("rstd", [P, n_tok])
        total = ps("total", [P, nh, HALF])
        squared, summed, rooted, inverted, scaled = (sem(n) for n in ("squared", "summed", "rooted", "inverted",
                                                                      "scaled"))
        with nc.Block() as block:
            @block.scalar
            def _(act):
                for kt in range(KD):
                    if kt >= 2:
                        act.wait_ge(summed, kt - 1)
                    nc.scalar.activation(sq[:, kt % 2, :], src[:, kt, :], ACT.Square).then_inc(squared, 1)
                act.wait_ge(summed, KD)
                for h in range(nh):
                    mm = nc.scalar.activation(root[:, h * w:(h + 1) * w], total[:, h, 0:w], ACT.Sqrt,
                                              scale=1.0 / D, bias=k.eps[:, 0:1])
                mm.then_inc(rooted, 1)

            @block.tensor
            def _(pe):
                for kt in range(KD):
                    pe.wait_ge(squared, kt + 1)
                    for h in range(nh):
                        mm = nc.tensor.matmul(total[:, h, 0:w], k.const["ones"], sq[:, kt % 2, h * w:(h + 1) * w],
                                              start=(kt == 0), stop=(kt == KD - 1))
                    mm.then_inc(summed, 1)

            @block.vector
            def _(dve):
                dve.wait_ge(rooted, 1)
                nc.vector.reciprocal(rstd[:, :], root[:, :]).then_inc(inverted, 1)
                dve.wait_ge(inverted, 1)
                for kt in range(KD):
                    nc.vector.scalar_tensor_tensor(out=dst[:, kt, :], in0=src[:, kt, :], scalar=gain[:, kt:kt + 1],
                                                   in1=rstd[:, :], op0=ALU.mult, op1=ALU.mult)


def dense(nc, name, jobs, src, kt_n, drain, outs=1):
    with ExitStack() as ctx:
        own = tiles(nc, ctx, name)
        sb, ps, sem = own
        w = sb("w", [P, 2, outs, kt_n, P])
        bank = ps("bank", [P, 2, outs, NH, HALF])
        landed = [sem("landed0"), sem("landed1")]
        ready, free = sem("ready"), sem("banks_free")
        with nc.Block() as block:
            @block.sync
            def _(sp):
                base = 0
                for n, views in jobs:
                    cols = [v.rearrange("(kt p) (i u f) -> u i p kt f", p=P, u=2, f=P) for v in views]

                    def load(i, u):
                        for o in range(outs):
                            sp.dma_start(w[:, u, o], cols[o][u, i]).then_inc(landed[u], 16)

                    for u in range(2):
                        if base:
                            sp.wait_ge(ready, base + u - 1)
                        load(0, u)
                    if n > 2:
                        with sp.Fori(1, n // 2) as i:
                            for u in range(2):
                                sp.wait_ge(ready, 2 * i + (base + u - 1))
                                load(i, u)
                    base += n

            @block.tensor
            def _(pe):
                with pe.Fori(0, sum(n for n, _ in jobs) // 2) as i:
                    for u in range(2):
                        pe.wait_ge(landed[u], (i + 1) * (16 * outs))
                        pe.wait_ge(free, 2 * i + u + 1)
                        for o in range(outs):
                            for h in range(NH):
                                for kt in range(kt_n):
                                    mm = nc.tensor.matmul(bank[:, u, o, h, :], w[:, u, o, kt, :], src(kt, h),
                                                          start=(kt == 0), stop=(kt == kt_n - 1))
                        mm.then_inc(ready, 1)

            drain(block, own, bank, ready, free)


def halves(x):
    return x.rearrange("p (h t) -> p h t", h=NH)


def copy_out(nc, dst, first, n):
    out = dst[:, first:first + n, :].rearrange("p (i u) t -> p i u t", u=2)

    def drain(block, own, bank, ready, free):
        @block.scalar
        def _(act):
            act.sem_inc(free, 2)
            with act.Fori(0, n // 2) as i:
                for u in range(2):
                    act.wait_ge(ready, 2 * i + u + 1)
                    nc.scalar.copy(halves(out[:, i, u, :]), bank[:, u, 0]).then_inc(free, 1)
    return drain


def add_out(nc, dst):
    out = dst[:, :, :].rearrange("p (i u) t -> p i u t", u=2)

    def drain(block, own, bank, ready, free):
        @block.vector
        def _(dve):
            dve.sem_inc(free, 2)
            with dve.Fori(0, KD // 2) as i:
                for u in range(2):
                    dve.wait_ge(ready, 2 * i + u + 1)
                    x = halves(out[:, i, u, :])
                    nc.vector.tensor_tensor(x, x, bank[:, u, 0], ALU.add).then_inc(free, 1)
    return drain


def shift_mix_out(nc, dst, mu):
    out = dst[:, :, :].rearrange("p (i u) t -> p i u t", u=2)
    mus = mu.rearrange("p (i u) -> p i u", u=2)

    def drain(block, own, bank, ready, free):
        sb, _, sem = own
        raw = sb("raw", [P, 2, T + 1])
        diff = sb("diff", [P, 2, T])
        mu_of = sb("mu_of", [P, 2])
        zeroed, stored, mixed, subtracted = (sem(n) for n in ("zeroed", "stored", "mixed", "subtracted"))

        @block.scalar
        def _(act):
            act.sem_inc(free, 2)
            with act.Fori(0, R_TILES // 2) as i:
                for u in range(2):
                    act.wait_ge(ready, 2 * i + u + 1)
                    act.wait_ge(mixed, 2 * i + u + 1)
                    nc.scalar.copy(halves(raw[:, u, 1:T + 1]), bank[:, u, 0]).then_inc(free, 1)
                    nc.scalar.copy(mu_of[:, u:u + 1], mus[:, i, u:u + 1]).then_inc(stored, 1)

        @block.vector
        def _(dve):
            nc.vector.memset(raw[:, :, 0:1], 0.0).then_inc(zeroed, 1)
            dve.sem_inc(mixed, 2)
            dve.wait_ge(zeroed, 1)
            with dve.Fori(0, R_TILES // 2) as i:
                for u in range(2):
                    dve.wait_ge(stored, 2 * i + u + 1)
                    nc.vector.tensor_tensor(diff[:, u, :], raw[:, u, 0:T], raw[:, u, 1:T + 1],
                                            ALU.subtract).then_inc(subtracted, 1)
                    dve.wait_ge(subtracted, 2 * i + u + 1)
                    nc.vector.scalar_tensor_tensor(out=out[:, i, u, :], in0=diff[:, u, :], scalar=mu_of[:, u:u + 1],
                                                   in1=raw[:, u, 1:T + 1], op0=ALU.mult, op1=ALU.add).then_inc(mixed, 1)
    return drain


def gate_out(nc, dst):
    out = dst[:, :, :].rearrange("p (i u) t -> p i u t", u=2)

    def drain(block, own, bank, ready, free):
        sb, _, sem = own
        silu = sb("silu", [P, 2, T])
        activated = sem("activated")

        @block.scalar
        def _(act):
            with act.Fori(0, FT // 2) as i:
                for u in range(2):
                    act.wait_ge(ready, 2 * i + u + 1)
                    act.wait_ge(free, 2 * i + u + 1)
                    nc.scalar.activation(halves(silu[:, u, :]), bank[:, u, 0], ACT.Silu).then_inc(activated, 1)

        @block.vector
        def _(dve):
            dve.sem_inc(free, 2)
            with dve.Fori(0, FT // 2) as i:
                for u in range(2):
                    dve.wait_ge(activated, 2 * i + u + 1)
                    nc.vector.tensor_tensor(halves(out[:, i, u, :]), halves(silu[:, u, :]), bank[:, u, 1],
                                            ALU.mult).then_inc(free, 1)
    return drain


def token_major(nc, name, src, kt_n, w_dram, dst, n_tok, width):
    nt = n_tok // P
    with ExitStack() as ctx:
        sb, ps, sem = tiles(nc, ctx, name)
        w = sb("w", [P, 2, kt_n, HALF])
        bank = ps("bank", [P, 2, HALF])
        landed = [sem("landed0"), sem("landed1")]
        ready, copied = sem("ready"), sem("copied")
        nb = width // HALF
        cols = w_dram.rearrange("(kt p) (b f) -> b p kt f", p=P, f=HALF)
        with nc.Block() as block:
            @block.sync
            def _(sp):
                for b in range(nb):
                    sp.dma_start(w[:, b, :, :], cols[b]).then_inc(landed[b], 16)

            @block.tensor
            def _(pe):
                for b in range(nb):
                    pe.wait_ge(landed[b], 16)
                    for c in range(nt):
                        n = b * nt + c
                        if n >= 2:
                            pe.wait_ge(copied, n - 1)
                        for kt in range(kt_n):
                            mm = nc.tensor.matmul(bank[:, n % 2, :], src[:, kt, c * P:(c + 1) * P], w[:, b, kt, :],
                                                  start=(kt == 0), stop=(kt == kt_n - 1))
                        mm.then_inc(ready, 1)

            @block.vector
            def _(dve):
                for b in range(nb):
                    for c in range(nt):
                        n = b * nt + c
                        dve.wait_ge(ready, n + 1)
                        nc.vector.tensor_copy(dst[:, c, b * HALF:(b + 1) * HALF], bank[:, n % 2, :]).then_inc(copied, 1)


def finish(nc, k, name, src, out):
    rows = out.rearrange("(c p) f -> c p f", p=P)
    with ExitStack() as ctx:
        sb, ps, sem = tiles(nc, ctx, name)
        tok = sb("tok", [P, 2, KD, P])
        bank = ps("bank", [P, 2, KD, P])
        turned, copied = sem("turned"), sem("copied")
        written = [sem("written0"), sem("written1")]
        with nc.Block() as block:
            @block.tensor
            def _(pe):
                for c in range(NC):
                    if c >= 2:
                        pe.wait_ge(copied, c - 1)
                    for f in range(KD):
                        mm = nc.tensor.transpose(bank[:, c % 2, f, :], src[:, f, c * P:(c + 1) * P], k.const["ident"])
                    mm.then_inc(turned, 1)

            @block.vector
            def _(dve):
                for c in range(NC):
                    dve.wait_ge(turned, c + 1)
                    if c >= 2:
                        dve.wait_ge(written[c % 2], 16 * (c // 2))
                    nc.vector.tensor_copy(tok[:, c % 2], bank[:, c % 2]).then_inc(copied, 1)

            @block.sync
            def _(sp):
                for c in range(NC):
                    sp.wait_ge(copied, c + 1)
                    sp.dma_start(rows[c], tok[:, c % 2].rearrange("p k f -> p (k f)")).then_inc(written[c % 2], 16)
                for u in range(2):
                    sp.wait_ge(written[u], 16 * (NC // 2))


def gla(nc, k, q, key, gate, lo, vtok, wa2, og):
    pe_steps = ("logits", "cumsum", "turn_keys", "scores", "outputs", "state")
    act_steps = ("load_lo", "log_decays", "decay_up", "decay_down", "mid_factor", "keep_keys", "keep_outputs")
    dve_steps = ("relu", "decayed", "masked", "entered", "end_factor", "left")
    with ExitStack() as ctx:
        sb, ps, sem = tiles(nc, ctx, "gla")
        wa2_sb = sb("wa2", [RANK, GH * GK])
        lo_c = sb("lo_c", [RANK, P])
        neg = sb("neg", [P, GH * GK])
        mag = sb("mag", [P, 2, GH * GK])
        soft = sb("soft", [P, GH * GK])
        la = sb("la", [P, GH * GK])
        up = sb("up", [P, 2, P])
        down = sb("down", [P, 2, P])
        mid = sb("mid", [P, 2])
        last = sb("last", [P, 2])
        qd = sb("qd", [P, 2, P])
        ki = sb("ki", [P, 2, P])
        kt = sb("kt", [P, 2, P])
        sc = sb("sc", [P, GH, P])
        state = sb("state", [P, 2, GV])
        entry = sb("entry", [P, 2, GV])
        b = [ps(f"b{n}", [P, HALF]) for n in range(8)]
        pe_done, act_done, dve_done = sem("pe_done"), sem("act_done"), sem("dve_done")
        loaded, zeroed, scratch = sem("loaded"), sem("zeroed"), sem("scratch")
        sub = sem("sub")
        chunk = lambda x: x.rearrange("p h (c t) -> p c h t", t=P)
        cq, ck = chunk(q), chunk(key)
        clo = lo.rearrange("p (c t) -> p c t", t=P)
        cog = chunk(og)
        vcur = sb("vcur", [P, GH * GV])
        with nc.Block() as block:
            @block.sync
            def _(sp):
                sp.dma_start(wa2_sb[:, :], wa2).then_inc(loaded, 16)

            @block.tensor
            def _(pe):
                pe.wait_ge(loaded, 16)
                pe.sem_inc(pe_done, 1)
                with pe.Fori(0, NC) as c:
                    pe.wait_ge(act_done, at(act_steps, "load_lo", c))
                    nc.tensor.matmul(b[0][:, 0:GH * GK], k.ones_row[0:1, 0:P], k.row["gla_ba"], start=True, stop=False)
                    nc.tensor.matmul(b[0][:, 0:GH * GK], lo_c[:, :], wa2_sb[:, :],
                                     start=False, stop=True).then_inc(pe_done, 1)
                    pe.wait_ge(act_done, at(act_steps, "log_decays", c))
                    pe.wait_ge(dve_done, at(dve_steps, "relu", c))
                    for f in range(2):
                        mm = nc.tensor.matmul(b[1][:, f * 2 * P:(f + 1) * 2 * P], la[:, f * P:(f + 1) * P], k.cum,
                                              start=True, stop=True)
                    mm.then_inc(pe_done, 1)
                    pe.wait_ge(dve_done, at(dve_steps, "decayed", c))
                    for f in range(2):
                        mm = nc.tensor.transpose(b[2][:, f * P:(f + 1) * P], ki[:, f, :], k.const["ident"])
                    mm.then_inc(pe_done, 1)
                    for h in range(GH):
                        r = slice(GK * (h % 2), GK * (h % 2) + GK)
                        mm = nc.tensor.matmul(b[3 + 3 * (h % 2)][:, (h // 2) * P:(h // 2 + 1) * P], ki[r, h // 2, :], qd[r, h // 2, :],
                                              start=True, stop=True)
                    mm.then_inc(pe_done, 1)
                    pe.wait_ge(dve_done, at(dve_steps, "entered", c))
                    for h in range(GH):
                        r = slice(GK * (h % 2), GK * (h % 2) + GK)
                        o = b[4 + 3 * (h % 2)][:, (h // 2) * P:(h // 2 + 1) * P]
                        nc.tensor.matmul(o, vcur[:, h * GV:(h + 1) * GV], sc[:, h, :],
                                         start=True, stop=False)
                        mm = nc.tensor.matmul(o, entry[r, h // 2, :], qd[r, h // 2, :],
                                              start=False, stop=True)
                    mm.then_inc(pe_done, 1)
                    pe.wait_ge(act_done, at(act_steps, "keep_keys", c))
                    for h in range(GH):
                        r = slice(GK * (h % 2), GK * (h % 2) + GK)
                        mm = nc.tensor.matmul(b[5][r, (h // 2) * GV:(h // 2 + 1) * GV],
                                              kt[:, h // 2, GK * (h % 2):GK * (h % 2) + GK],
                                              vcur[:, h * GV:(h + 1) * GV], start=True, stop=True)
                    mm.then_inc(pe_done, 1)

            @block.scalar
            def _(act):
                act.sem_inc(act_done, 1)
                with act.Fori(0, NC) as c:
                    act.wait_ge(dve_done, before(dve_steps, c))
                    nc.scalar.copy(vcur[:, :], vtok[:, c, :])
                    nc.scalar.copy(lo_c[:, :], clo[:, c, :]).then_inc(act_done, 1)
                    act.wait_ge(pe_done, at(pe_steps, "logits", c))
                    nc.scalar.activation(mag[:, 0, :], b[0][:, 0:GH * GK], ACT.Abs).then_inc(sub, 1)
                    act.wait_ge(sub, 2 * c + 1)
                    nc.scalar.activation(mag[:, 1, :], mag[:, 0, :], ACT.Exp, scale=-1.0).then_inc(sub, 1)
                    act.wait_ge(sub, 2 * c + 2)
                    nc.scalar.activation(soft[:, :], mag[:, 1, :], ACT.Ln, bias=1.0).then_inc(act_done, 1)
                    act.wait_ge(pe_done, at(pe_steps, "cumsum", c))
                    cum = b[1][:, :].rearrange("p (f w t) -> p f w t", f=2, w=2)
                    nc.scalar.activation(up[:, :, :], cum[:, :, 0, :], ACT.Exp, scale=1.0 / 16).then_inc(act_done, 1)
                    nc.scalar.activation(down[:, :, :], cum[:, :, 0, :], ACT.Exp, scale=-1.0 / 16).then_inc(act_done, 1)
                    nc.scalar.activation(mid[:, :], cum[:, :, 1, 0], ACT.Exp, scale=-1.0 / 16).then_inc(act_done, 1)
                    act.wait_ge(pe_done, at(pe_steps, "turn_keys", c))
                    nc.scalar.copy(kt[:, :, :], b[2][:, 0:2 * P].rearrange("p (f t) -> p f t", f=2)).then_inc(act_done, 1)
                    act.wait_ge(pe_done, at(pe_steps, "outputs", c))
                    for e in range(2):
                        mm = nc.scalar.copy(cog[:, c, e:GH:2, :],
                                            b[4 + 3 * e][:, 0:2 * P].rearrange("p (h t) -> p h t", h=2))
                    mm.then_inc(act_done, 1)

            @block.vector
            def _(dve):
                nc.vector.memset(state[:, :, :], 0.0).then_inc(zeroed, 1)
                dve.wait_ge(zeroed, 1)
                dve.sem_inc(dve_done, 1)
                with dve.Fori(0, NC) as c:
                    dve.wait_ge(act_done, at(act_steps, "log_decays", c))
                    nc.vector.tensor_scalar(neg[:, :], b[0][:, 0:GH * GK], 0.0, None, ALU.min).then_inc(scratch, 1)
                    dve.wait_ge(scratch, 2 * c + 1)
                    nc.vector.tensor_tensor(la[:, :], neg[:, :], soft[:, :], ALU.subtract).then_inc(dve_done, 1)
                    dve.wait_ge(act_done, at(act_steps, "decay_down", c))
                    nc.vector.scalar_tensor_tensor(out=qd[:, :, :], in0=cq[:, c, :, :], scalar=GK ** -0.5,
                                                   in1=up[:, :, :], op0=ALU.mult, op1=ALU.mult)
                    nc.vector.tensor_tensor(ki[:, :, :], ck[:, c, :, :], down[:, :, :], ALU.mult).then_inc(dve_done, 1)
                    dve.wait_ge(pe_done, at(pe_steps, "scores", c))
                    for e in range(2):
                        mm = nc.vector.tensor_tensor(sc[:, e:GH:2, :],
                                                     b[3 + 3 * e][:, 0:2 * P].rearrange("p (h t) -> p h t", h=2),
                                                     k.const["up_incl"].unsqueeze(1).to_broadcast([P, 2, P]), ALU.mult)
                    mm.then_inc(dve_done, 1)
                    dve.wait_ge(act_done, at(act_steps, "mid_factor", c))
                    nc.vector.tensor_tensor(entry[:, :, :], state[:, :, :], wide(mid[:, :], GV),
                                            ALU.mult).then_inc(dve_done, 1)
                    dve.wait_ge(pe_done, at(pe_steps, "state", c))
                    nc.vector.tensor_tensor(entry[:, :, :], entry[:, :, :],
                                            b[5][:, 0:2 * GV].rearrange("p (f v) -> p f v", f=2),
                                            ALU.add).then_inc(dve_done, 1)
                    dve.wait_ge(dve_done, at(dve_steps, "end_factor", c))
                    nc.vector.tensor_copy(last[:, :], up[:, :, P - 1]).then_inc(scratch, 1)
                    dve.wait_ge(scratch, 2 * c + 2)
                    dve.wait_ge(act_done, at(act_steps, "keep_outputs", c))
                    nc.vector.tensor_tensor(state[:, :, :], entry[:, :, :], wide(last[:, :], GV),
                                            ALU.mult).then_inc(dve_done, 1)
                    dve.wait_ge(dve_done, at(dve_steps, "left", c))

    with ExitStack() as ctx:
        sb, ps, sem = tiles(nc, ctx, "gla_norm")
        sq = sb("sq", [P, 2, T])
        root = sb("root", [P, 2, T])
        rstd = sb("rstd", [P, 2, T])
        silu = sb("silu", [P, 2, T])
        total = ps("total", [P, 2, NH, HALF])
        squared, summed, rooted, scaled, silus = (sem(n) for n in ("squared", "summed", "rooted", "scaled", "silus"))
        with nc.Block() as block:
            @block.scalar
            def _(act):
                for h in range(GH):
                    u = h % 2
                    if h >= 2:
                        act.wait_ge(scaled, 3 * (h - 1))
                    nc.scalar.activation(sq[:, u, :], og[:, h, :], ACT.Square).then_inc(squared, 1)
                    nc.scalar.activation(silu[:, u, :], gate[:, h, :], ACT.Silu).then_inc(silus, 1)
                    act.wait_ge(summed, h + 1)
                    nc.scalar.activation(halves(root[:, u, :]), total[:, u], ACT.Sqrt, scale=1.0 / GV,
                                         bias=k.eps[:, 1:2]).then_inc(rooted, 1)

            @block.tensor
            def _(pe):
                for h in range(GH):
                    pe.wait_ge(squared, h + 1)
                    for n in range(NH):
                        mm = nc.tensor.matmul(total[:, h % 2, n, :], k.const["ones"],
                                              sq[:, h % 2, n * HALF:(n + 1) * HALF], start=True, stop=True)
                    mm.then_inc(summed, 1)

            @block.vector
            def _(dve):
                for h in range(GH):
                    u = h % 2
                    dve.wait_ge(rooted, h + 1)
                    nc.vector.reciprocal(rstd[:, u, :], root[:, u, :]).then_inc(scaled, 1)
                    dve.wait_ge(scaled, 3 * h + 1)
                    nc.vector.scalar_tensor_tensor(out=og[:, h, :], in0=og[:, h, :], scalar=k.par["gla_norm_g"][:, 0:1],
                                                   in1=rstd[:, u, :], op0=ALU.mult, op1=ALU.mult).then_inc(scaled, 1)
                    dve.wait_ge(scaled, 3 * h + 2)
                    dve.wait_ge(silus, h + 1)
                    nc.vector.tensor_tensor(og[:, h, :], og[:, h, :], silu[:, u, :], ALU.mult).then_inc(scaled, 1)


RP = ("decay_logits", "rate_logits", "gates", "key_norms", "turn_values", "cumsum", "bonus", "turn_abk",
      "gram_a", "gram_b", "chunk_h", "sq_a", "sq_b", "quad_a", "quad_b", "oct_a", "oct_b", "dec_a", "dec_b",
      "turn_a", "turn_b", "join0_a", "join0_b", "left0_a", "left0_b", "join1_a", "join1_b", "left1_a", "left1_b",
      "join2_a", "join2_b", "left2_a", "left2_b", "removal", "removed", "state", "outputs", "means", "variances")
RA = ("loras", "decays", "rates", "gates", "key_roots", "keep_values", "up", "down", "up_ex", "mid", "bonus", "keep_a",
      "keep_b", "keep_k", "keep_strict_a", "keep_strict_b", "keep_h",
      "sq_a", "sq_b", "quad_a", "quad_b", "oct_a", "oct_b", "turn_a", "turn_b", "join0_a", "join0_b", "join1_a",
      "join1_b", "join2_a", "join2_b", "keep_w", "keep_u", "keep_y", "centred_sq", "roots")
RV = ("raw_kk", "raw_sq", "root_max", "inv_norm", "kk", "rate_k", "k_gain", "key", "b_vec", "key_r", "bonus_rk", "ab", "kr",
      "strict_a", "masked_ak_a", "masked_rk_a", "strict_b", "masked_ak_b", "masked_rk_b",
      "quad_a", "quad_b", "oct_a", "oct_b", "dec_a", "dec_b",
      "left0_a", "leftT0_a", "left0_b", "leftT0_b", "left1_a", "leftT1_a", "left1_b", "leftT1_b", "left2_a", "left2_b",
      "entered", "state_sum", "state", "centred", "inv_std", "normed", "gained", "bonus_v", "with_bias", "with_bonus",
      "written")
RG = ("diag_a", "plus_a", "merges_a", "diag_b", "plus_b", "merges_b")


def rwkv(nc, k, z, w2, a2, g2):
    with ExitStack() as ctx:
        sb, ps, sem = tiles(nc, ctx, "rwkv")
        w2_sb, a2_sb, g2_sb = sb("w2", [P, HALF]), sb("a2", [P, HALF]), sb("g2", [P, HALF])
        lora = sb("lora", [P, 2, P])
        sig_w = sb("sig_w", [P, HALF])
        f4 = lambda n: sb(n, [P, RT, P])
        rate, gates, kk, t1, t2, key, up, down, upx = (f4(n) for n in (
            "rate", "gates", "kk", "t1", "t2", "key", "up", "down", "upx"))
        bonus, y = f4("bonus"), f4("y")
        ar = sb("ar", [P, RT, 2, P])
        bt, kt = f4("bt"), f4("kt")
        mid = sb("mid", [P, RT])
        tok = {n: sb(f"tok_{n}", [P, RH * RN]) for n in "abkv"}
        m8 = lambda n: sb(n, [P, RH, P])
        nmat, merge, rb, ak, rk = m8("nmat"), sb("merge", [P, 3, RH, P]), m8("rb"), m8("ak"), m8("rk")
        strict = m8("strict")
        d1, d1t, x2, x2t, x8t = m8("d1"), m8("d1t"), m8("x2"), m8("x2t"), m8("x8t")
        xp = sb("xp", [P, RH, 2, P])
        h_sb, u_sb = sb("h", [P, RH, RN]), sb("u", [P, RH, RN])
        wt = sb("wt", [P, RT, P])
        state, entry = sb("state", [P, RT, RN]), sb("entry", [P, RT, RN])
        bank = ps("bank", [P, 8, HALF])
        pe_done, act_done, dve_done, pool_done = (sem(n) for n in ("pe_done", "act_done", "dve_done", "pool_done"))
        loaded, zeroed = sem("loaded"), sem("zeroed")
        cz = z[:, :, :].rearrange("p f (c t) -> p c f t", t=P)
        c = k.const
        heads = {"a": range(0, RH // 2), "b": range(RH // 2, RH)}
        hs = {"a": slice(0, RH // 2), "b": slice(RH // 2, RH)}

        def rows(h):
            return slice(RN * (h % 2), RN * (h % 2) + RN)

        def masks(x, n):
            return x.unsqueeze(1).to_broadcast([P, n, P])

        def flat(b):
            return bank[:, b, :].rearrange("p (h t) -> p h t", t=P)

        def by_parity(x, g):
            return x[:, hs[g], :].rearrange("p (n e) t -> p e n t", e=2)

        first = {"a": 0, "b": 3}
        p4, p4t, q, p5, p5t, p6, p6t, p7 = x2, x2t, x8t, d1, d1t, x2, x2t, d1
        chain = [(p4, p4t), (p5, p5t), (p6, p6t), (p7, None)]

        with nc.Block() as block:
            @block.sync
            def _(sp):
                sp.dma_start(w2_sb[0:64, :], w2).then_inc(loaded, 16)
                sp.dma_start(a2_sb[64:128, :], a2).then_inc(loaded, 16)
                sp.dma_start(g2_sb[:, :], g2).then_inc(loaded, 16)

            @block.tensor
            def _(pe):
                mmul = nc.tensor.matmul
                pe.wait_ge(loaded, 48)
                pe.sem_inc(pe_done, 1)
                with pe.Fori(0, NC) as i:
                    def act(name):
                        pe.wait_ge(act_done, at(RA, name, i))

                    def dve(name):
                        pe.wait_ge(dve_done, at(RV, name, i))

                    act("loras")
                    mmul(bank[:, 0, :], k.ones_row[0:1, 0:P], k.row["rwkv_w0"], start=True, stop=False)
                    mmul(bank[:, 0, :], lora[0:64, 0, :], w2_sb[0:64, :], start=False, stop=True).then_inc(pe_done, 1)
                    for f in range(RT):
                        s = slice(f * P, (f + 1) * P)
                        mmul(bank[:, 1, s], k.row["rwkv_a0"][:, s], k.ones_row[0:1, 0:P], start=True, stop=False)
                        mm = mmul(bank[:, 1, s], a2_sb[64:128, s], lora[64:128, 0, :], start=False, stop=True)
                    mm.then_inc(pe_done, 1)
                    for f in range(RT):
                        s = slice(f * P, (f + 1) * P)
                        mm = mmul(bank[:, 2, s], g2_sb[:, s], lora[:, 1, :], start=True, stop=True)
                    mm.then_inc(pe_done, 1)
                    dve("raw_sq")
                    mmul(bank[:, 3, :], c["pair_ones"], t1[:, :, :].rearrange("p f t -> p (f t)"),
                         start=True, stop=True).then_inc(pe_done, 1)
                    for f in range(RT):
                        mm = nc.tensor.transpose(bank[:, 4, f * P:(f + 1) * P], y[:, f, :], c["ident"])
                    mm.then_inc(pe_done, 1)
                    act("decays")
                    for f in range(RT):
                        mm = mmul(bank[:, 5 + f // 2, (f % 2) * 2 * P:(f % 2 + 1) * 2 * P], sig_w[:, f * P:(f + 1) * P],
                                  k.cum_w[:, :], start=True, stop=True)
                    mm.then_inc(pe_done, 1)
                    dve("bonus_rk")
                    mmul(bank[:, 7, :], c["pair_ones"], t1[:, :, :].rearrange("p f t -> p (f t)"),
                         start=True, stop=True).then_inc(pe_done, 1)
                    dve("kr")
                    act("rates")
                    act("gates")
                    for n, src in enumerate((ar[:, :, 0, :], bt, kt)):
                        for f in range(RT):
                            mm = nc.tensor.transpose(bank[:, n, f * P:(f + 1) * P], src[:, f, :], c["ident"])
                    mm.then_inc(pe_done, 1)
                    for g, b0 in (("a", 2), ("b", 0)):
                        if g == "a":
                            act("keep_k")
                        else:
                            dve("masked_rk_a")
                            act("keep_strict_a")
                        for n, h in enumerate(heads[g]):
                            r, e = rows(h), h % 2
                            a_r = ar[r, h // 2, :, :].rearrange("p w t -> p (w t)")
                            s = slice((n // 2) * 2 * P, (n // 2 + 1) * 2 * P)
                            mmul(bank[:, b0 + e, s], bt[r, h // 2, :], a_r, start=True, stop=True)
                            mmul(bank[:, b0 + 2 + e, s], kt[r, h // 2, :], a_r, start=True, stop=True)
                            mm = mmul(bank[:, b0 + 4 + e, (n // 2) * P:(n // 2 + 1) * P], ar[r, h // 2, 0, :],
                                      bt[r, h // 2, :], start=True, stop=True)
                        mm.then_inc(pe_done, 1)
                    act("keep_values")
                    dve("masked_rk_b")
                    for h in range(RH):
                        mm = mmul(bank[:, 7, h * RN:(h + 1) * RN], ak[:, h, :], tok["v"][:, h * RN:(h + 1) * RN],
                                  start=True, stop=True)
                    mm.then_inc(pe_done, 1)
                    for g in "ab":
                        b0 = first[g]
                        pe.wait_ge(pool_done, at(RG, "diag_" + g, i))
                        for n, h in enumerate(heads[g]):
                            s = slice(n * P, (n + 1) * P)
                            mmul(bank[:, b0, s], d1t[:, h, :], d1[:, h, :], start=True, stop=True)
                            mm = mmul(bank[:, b0 + 2, s], d1[:, h, :], d1t[:, h, :], start=True, stop=True)
                        mm.then_inc(pe_done, 1)
                    for g in "ab":
                        b0 = first[g]
                        act("sq_" + g)
                        pe.wait_ge(pool_done, at(RG, "plus_" + g, i))
                        for n, h in enumerate(heads[g]):
                            s = slice((n % 2) * 2 * P, (n % 2 + 1) * 2 * P)
                            mmul(bank[:, b0 + n // 2, s], x2t[:, h, :], xp[:, h, :, :].rearrange("p w t -> p (w t)"),
                                 start=True, stop=True)
                            mm = mmul(bank[:, b0 + 2, n * P:(n + 1) * P], x2[:, h, :], x2t[:, h, :],
                                      start=True, stop=True)
                        mm.then_inc(pe_done, 1)
                    for g in "ab":
                        b0 = first[g]
                        act("quad_" + g)
                        dve("quad_" + g)
                        for n, h in enumerate(heads[g]):
                            s = slice(n * P, (n + 1) * P)
                            mmul(bank[:, b0, s], d1t[:, h, :], xp[:, h, 1, :], start=True, stop=True)
                            mm = mmul(bank[:, b0 + 1, s], xp[:, h, 0, :], d1t[:, h, :], start=True, stop=True)
                        mm.then_inc(pe_done, 1)
                    for g in "ab":
                        b0 = first[g]
                        act("oct_" + g)
                        dve("oct_" + g)
                        for n, h in enumerate(heads[g]):
                            mm = mmul(bank[:, b0 + 2, n * P:(n + 1) * P], x8t[:, h, :], d1[:, h, :],
                                      start=True, stop=True)
                        mm.then_inc(pe_done, 1)
                    for g in "ab":
                        b0 = first[g]
                        dve("dec_" + g)
                        for n, h in enumerate(heads[g]):
                            mm = nc.tensor.transpose(bank[:, b0, n * P:(n + 1) * P], p4[:, h, :], c["ident"])
                        mm.then_inc(pe_done, 1)
                    for lv in range(3):
                        pm, pmt = chain[lv]
                        for g in "ab":
                            b0 = first[g]
                            if lv == 0:
                                pe.wait_ge(pool_done, at(RG, "merges_" + g, i))
                            else:
                                dve(f"leftT{lv - 1}_{g}")
                            for n, h in enumerate(heads[g]):
                                mm = mmul(bank[:, b0 + 1, n * P:(n + 1) * P], merge[:, lv, h, :], pm[:, h, :],
                                          start=True, stop=True)
                            mm.then_inc(pe_done, 1)
                        for g in "ab":
                            b0 = first[g]
                            act(f"join{lv}_{g}")
                            for n, h in enumerate(heads[g]):
                                s = slice(n * P, (n + 1) * P)
                                mm = mmul(bank[:, b0 + 2, s], pmt[:, h, :], q[:, h, :], start=True, stop=True)
                                if lv < 2:
                                    mm = mmul(bank[:, b0, s], q[:, h, :], pmt[:, h, :], start=True, stop=True)
                            mm.then_inc(pe_done, 1)
                    dve("left2_b")
                    act("keep_h")
                    for h in range(RH):
                        mm = mmul(bank[rows(h), 6, (h // 2) * P:(h // 2 + 1) * P], tok["a"][:, h * RN:(h + 1) * RN],
                                  p7[:, h, :], start=True, stop=True)
                    mm.then_inc(pe_done, 1)
                    act("keep_w")
                    dve("entered")
                    for h in range(RH):
                        o = bank[:, 6 + h % 2, (h // 2) * RN:(h // 2 + 1) * RN]
                        mmul(o, p7[:, h, :], h_sb[:, h, :], start=True, stop=False)
                        mm = mmul(o, wt[rows(h), h // 2, :], entry[rows(h), h // 2, :],
                                  start=False, stop=True)
                    mm.then_inc(pe_done, 1)
                    act("keep_u")
                    for h in range(RH):
                        o = bank[rows(h), 0, (h // 2) * RN:(h // 2 + 1) * RN]
                        s = slice(h * RN, (h + 1) * RN)
                        mmul(o, tok["k"][:, s], tok["v"][:, s], start=True, stop=False)
                        mm = mmul(o, tok["b"][:, s], u_sb[:, h, :], start=False, stop=True)
                    mm.then_inc(pe_done, 1)
                    for h in range(RH):
                        o = bank[rows(h), 1, (h // 2) * P:(h // 2 + 1) * P]
                        mmul(o, entry[rows(h), h // 2, :], ar[rows(h), h // 2, 1, :], start=True, stop=False)
                        mmul(o, tok["v"][:, h * RN:(h + 1) * RN], rk[:, h, :], start=False, stop=False)
                        mm = mmul(o, u_sb[:, h, :], rb[:, h, :], start=False, stop=True)
                    mm.then_inc(pe_done, 1)
                    act("keep_y")
                    mmul(bank[:, 2, :], c["pair_ones"], y[:, :, :].rearrange("p f t -> p (f t)"),
                         start=True, stop=True).then_inc(pe_done, 1)
                    act("centred_sq")
                    mmul(bank[:, 3, :], c["pair_ones"], t1[:, :, :].rearrange("p f t -> p (f t)"),
                         start=True, stop=True).then_inc(pe_done, 1)

            @block.scalar
            def _(act):
                done = lambda ins: ins.then_inc(act_done, 1)
                act.sem_inc(act_done, 1)
                with act.Fori(0, NC) as i:
                    def pe(name):
                        act.wait_ge(pe_done, at(RP, name, i))

                    def own(name):
                        act.wait_ge(act_done, at(RA, name, i))

                    act.wait_ge(dve_done, before(RV, i))
                    nc.scalar.activation(lora[0:64, 0, :], cz[0:64, i, 12, :], ACT.Tanh)
                    nc.scalar.copy(lora[64:128, 0, :], cz[64:128, i, 12, :])
                    nc.scalar.copy(y[:, :, :], cz[:, i, 8:12, :])
                    done(nc.scalar.activation(lora[:, 1, :], cz[:, i, 13, :], ACT.Sigmoid))
                    pe("decay_logits")
                    done(nc.scalar.activation(sig_w[:, :], bank[:, 0, :], ACT.Sigmoid))
                    pe("rate_logits")
                    done(nc.scalar.activation(rate[:, :, :], flat(1), ACT.Sigmoid))
                    pe("gates")
                    done(nc.scalar.copy(gates[:, :, :], flat(2)))
                    pe("key_norms")
                    done(nc.scalar.activation(t2[:, :, :], flat(3), ACT.Sqrt))
                    pe("turn_values")
                    done(nc.scalar.copy(tok["v"][:, :], bank[:, 4, :]))
                    pe("cumsum")
                    cum = bank[:, 5:7, :].rearrange("p b (f w t) -> p (b f) w t", f=2, w=2)
                    done(nc.scalar.activation(up[:, :, :], cum[:, :, 0, :], ACT.Exp))
                    done(nc.scalar.activation(down[:, :, :], cum[:, :, 0, :], ACT.Exp, scale=-1.0))
                    done(nc.scalar.activation(upx[:, :, :], cum[:, :, 1, :], ACT.Exp))
                    done(nc.scalar.activation(mid[:, :], cum[:, :, 1, 0], ACT.Exp, scale=-1.0))
                    pe("bonus")
                    done(nc.scalar.copy(bonus[:, :, :], flat(7)))
                    pe("turn_abk")
                    done(nc.scalar.copy(tok["a"][:, :], bank[:, 0, :]))
                    done(nc.scalar.copy(tok["b"][:, :], bank[:, 1, :]))
                    done(nc.scalar.copy(tok["k"][:, :], bank[:, 2, :]))
                    for g, nb in (("a", 6), ("b", 4)):
                        pe("gram_" + g)
                        done(nc.scalar.copy(by_parity(nmat, g), bank[:, nb:nb + 2, 0:2 * P].rearrange(
                            "p e (n t) -> p e n t", t=P)))
                    pe("chunk_h")
                    done(nc.scalar.copy(h_sb[:, :, :], bank[:, 7, :].rearrange("p (h n) -> p h n", n=RN)))
                    for g in "ab":
                        pe("sq_" + g)
                        nc.scalar.copy(xp[:, hs[g], 0, :], flat(first[g]))
                        nc.scalar.copy(x2[:, hs[g], :], flat(first[g]))
                        done(nc.scalar.copy(x2t[:, hs[g], :], flat(first[g] + 2)))
                    for g in "ab":
                        pe("quad_" + g)
                        b0 = first[g]
                        quad = bank[:, b0:b0 + 2, :].rearrange("p b (f w t) -> p (b f) w t", f=2, w=2)
                        nc.scalar.copy(xp[:, hs[g], 0, :], quad[:, :, 0, :])
                        done(nc.scalar.copy(d1t[:, hs[g], :], flat(b0 + 2)))
                    for g in "ab":
                        pe("oct_" + g)
                        done(nc.scalar.copy(x8t[:, hs[g], :], flat(first[g] + 1)))
                    for g in "ab":
                        pe("turn_" + g)
                        done(nc.scalar.copy(p4t[:, hs[g], :], flat(first[g])))
                    for lv in range(3):
                        for g in "ab":
                            pe(f"join{lv}_{g}")
                            done(nc.scalar.copy(q[:, hs[g], :], flat(first[g] + 1)))
                    pe("removal")
                    done(nc.scalar.copy(wt[:, :, :], flat(6)))
                    pe("removed")
                    done(nc.scalar.copy(u_sb[:, :, :].rearrange("p (n e) i -> p e n i", e=2),
                                        bank[:, 6:8, 0:RT * RN].rearrange("p e (n i) -> p e n i", i=RN)))
                    pe("outputs")
                    done(nc.scalar.copy(y[:, :, :], flat(1)))
                    act.wait_ge(dve_done, at(RV, "centred", i))
                    done(nc.scalar.activation(t1[:, :, :], y[:, :, :], ACT.Square))
                    pe("variances")
                    done(nc.scalar.activation(t2[:, :, :], flat(3), ACT.Sqrt, scale=1.0 / RN, bias=k.eps[:, 2:3]))

            @block.gpsimd
            def _(pool):
                nc.gpsimd.memset(state[:, :, :], 0.0).then_inc(zeroed, 1)
                pool.sem_inc(pool_done, 1)
                with pool.Fori(0, NC) as i:
                    for g, nb in (("a", 7), ("b", 4)):
                        pool.wait_ge(dve_done, at(RV, "strict_" + g, i))
                        nc.gpsimd.tensor_tensor(d1[:, hs[g], :], strict[:, hs[g], :], masks(c["diag_up"], 4), ALU.mult)
                        pool.wait_ge(act_done, at(RA, "keep_strict_" + g, i))
                        nc.gpsimd.tensor_tensor(d1t[:, hs[g], :], nmat[:, hs[g], :], masks(c["diag_lo"], 4),
                                                ALU.mult).then_inc(pool_done, 1)
                        pool.wait_ge(pool_done, at(RG, "diag_" + g, i))
                        nc.gpsimd.tensor_tensor(xp[:, hs[g], 1, :], d1[:, hs[g], :], masks(c["ident"], 4),
                                                ALU.add).then_inc(pool_done, 1)
                        for lv, name in enumerate(("merge16", "merge32", "merge64")):
                            mm = nc.gpsimd.tensor_tensor(merge[:, lv, hs[g], :], nmat[:, hs[g], :], masks(c[name], 4),
                                                         ALU.mult)
                        mm.then_inc(pool_done, 1)

            @block.vector
            def _(dve):
                done = lambda ins: ins.then_inc(dve_done, 1)
                tt, stt = nc.vector.tensor_tensor, nc.vector.scalar_tensor_tensor
                par = k.par
                dve.wait_ge(zeroed, 1)
                dve.sem_inc(dve_done, 1)
                with dve.Fori(0, NC) as i:
                    def pe(name):
                        dve.wait_ge(pe_done, at(RP, name, i))

                    def act(name):
                        dve.wait_ge(act_done, at(RA, name, i))

                    def own(name):
                        dve.wait_ge(dve_done, at(RV, name, i))

                    r_in, k_in, v_in = (cz[:, i, n:n + RT, :] for n in (0, 4, 8))
                    done(tt(kk[:, :, :], k_in, wide(par["rwkv_k_k"], P), ALU.mult))
                    own("raw_kk")
                    done(tt(t1[:, :, :], kk[:, :, :], kk[:, :, :], ALU.mult))
                    act("key_roots")
                    done(nc.vector.tensor_scalar(t2[:, :, :], t2[:, :, :], 1e-12, None, ALU.max))
                    own("root_max")
                    done(nc.vector.reciprocal(t2[:, :, :], t2[:, :, :]))
                    own("inv_norm")
                    done(tt(kk[:, :, :], kk[:, :, :], t2[:, :, :], ALU.mult))
                    act("rates")
                    done(stt(out=key[:, :, :], in0=rate[:, :, :], scalar=-1.0, in1=k_in, op0=ALU.add, op1=ALU.mult))
                    own("rate_k")
                    done(tt(key[:, :, :], key[:, :, :], wide(par["rwkv_k_a"], P), ALU.mult))
                    own("k_gain")
                    done(tt(key[:, :, :], key[:, :, :], k_in, ALU.add))
                    own("key")
                    done(tt(rate[:, :, :], rate[:, :, :], kk[:, :, :], ALU.mult))
                    pe("key_norms")
                    done(tt(t2[:, :, :], key[:, :, :], r_in, ALU.mult))
                    own("key_r")
                    done(tt(t1[:, :, :], t2[:, :, :], wide(par["rwkv_r_k"], P), ALU.mult))
                    act("up_ex")
                    stt(out=ar[:, :, 0, :], in0=kk[:, :, :], scalar=-1.0, in1=upx[:, :, :], op0=ALU.mult, op1=ALU.mult)
                    done(tt(bt[:, :, :], rate[:, :, :], down[:, :, :], ALU.mult))
                    tt(ar[:, :, 1, :], r_in, up[:, :, :], ALU.mult)
                    done(tt(kt[:, :, :], key[:, :, :], down[:, :, :], ALU.mult))
                    for g, b0 in (("a", 2), ("b", 0)):
                        pe("gram_" + g)
                        nr = bank[:, b0:b0 + 2, :].rearrange("p e (n w t) -> p e n w t", n=2, w=2)
                        akrk = bank[:, b0 + 2:b0 + 4, :].rearrange("p e (n w t) -> p e n w t", n=2, w=2)

                        def mask(dst, src, w, name):
                            for e in range(2):
                                ins = tt(by_parity(dst, g)[:, e], src[:, e, :, w, :], masks(c[name], 2), ALU.mult)
                            return ins

                        done(mask(strict, nr, 0, "up_strict"))
                        mask(rb, nr, 1, "up_incl")
                        done(mask(ak, akrk, 0, "up_strict"))
                        done(mask(rk, akrk, 1, "up_incl"))
                    for g in "ab":
                        act("quad_" + g)
                        b0 = first[g]
                        quad = bank[:, b0:b0 + 2, :].rearrange("p b (f w t) -> p (b f) w t", f=2, w=2)
                        done(tt(xp[:, hs[g], 1, :], quad[:, :, 1, :], xp[:, hs[g], 1, :], ALU.add))
                    for g in "ab":
                        pe("oct_" + g)
                        done(tt(d1[:, hs[g], :], flat(first[g]), xp[:, hs[g], 1, :], ALU.add))
                    for g in "ab":
                        pe("dec_" + g)
                        done(tt(p4[:, hs[g], :], flat(first[g] + 2), d1[:, hs[g], :], ALU.add))
                    for lv in range(3):
                        (pm, pmt), (pn, pnt) = chain[lv], chain[lv + 1]
                        for g in "ab":
                            pe(f"left{lv}_{g}")
                            done(tt(pn[:, hs[g], :], flat(first[g] + 2), pm[:, hs[g], :], ALU.add))
                            if lv < 2:
                                done(tt(pnt[:, hs[g], :], flat(first[g]), pmt[:, hs[g], :], ALU.add))
                    done(tt(entry[:, :, :], state[:, :, :], wide(mid[:, :], RN), ALU.mult))
                    pe("state")
                    done(tt(state[:, :, :], entry[:, :, :], bank[:, 0, 0:RT * RN].rearrange("p (f n) -> p f n", n=RN),
                            ALU.add))
                    own("state_sum")
                    done(tt(state[:, :, :], state[:, :, :], wide(up[:, :, P - 1], RN), ALU.mult))
                    pe("means")
                    done(stt(out=y[:, :, :], in0=flat(2), scalar=-1.0 / RN, in1=y[:, :, :], op0=ALU.mult, op1=ALU.add))
                    act("roots")
                    done(nc.vector.reciprocal(t2[:, :, :], t2[:, :, :]))
                    own("inv_std")
                    done(tt(y[:, :, :], y[:, :, :], t2[:, :, :], ALU.mult))
                    own("normed")
                    done(tt(y[:, :, :], y[:, :, :], wide(par["rwkv_ln_g"], P), ALU.mult))
                    done(tt(bonus[:, :, :], bonus[:, :, :], v_in, ALU.mult))
                    own("bonus_v")
                    done(tt(y[:, :, :], y[:, :, :], wide(par["rwkv_ln_b"], P), ALU.add))
                    own("with_bias")
                    done(tt(y[:, :, :], y[:, :, :], bonus[:, :, :], ALU.add))
                    own("with_bonus")
                    done(tt(r_in, y[:, :, :], gates[:, :, :], ALU.mult))


def block_kernel(nc, x, mem, w_in, gla_wa2, rwkv_w2, rwkv_a2, rwkv_g2, w_out, wq_mem, wkv_mem, wo_mem, w_gate_up,
                 w_down, consts, params, rows, out):
    k = Kept()
    n_par = sum(n for _, n in PARAMS)
    n_row = sum(n for _, n in ROWS)
    keep = ExitStack()

    def hold(stack, name, shape, side="left"):
        return stack.enter_context(nc.sbuf_tensor(name, shape, F32, side=side))

    with keep:
        con = hold(keep, "consts", [P, len(CONSTS) * P])
        par = hold(keep, "params", [P, n_par])
        row = hold(keep, "rows", [1, n_row])
        k.cum_w = hold(keep, "cum_w", [P, 2 * P])
        k.eps = hold(keep, "eps", [P, 3])
        for n, name in enumerate(CONSTS):
            k.const[name] = con[:, n * P:(n + 1) * P]
        first = CONSTS.index("cum_in") * P
        k.cum = con[:, first:first + 2 * P]
        k.ones_row = k.const["ones"][0:1, :]
        at_col = 0
        for name, n in PARAMS:
            k.par[name] = par[:, at_col:at_col + n]
            at_col += n
        at_col = 0
        for name, n in ROWS:
            k.row[name] = row[0:1, at_col:at_col + n]
            at_col += n
        loaded = keep.enter_context(nc.semaphore("consts_loaded"))
        with nc.Block() as block:
            @block.sync
            def _(sp):
                sp.dma_start(con[:, :], consts).then_inc(loaded, 16)
                sp.dma_start(par[:, :], params).then_inc(loaded, 16)
                sp.dma_start(row[:, :], rows).then_inc(loaded, 16)

            @block.vector
            def _(dve):
                for n, e in enumerate((EPS, G_EPS, R_EPS)):
                    nc.vector.memset(k.eps[:, n:n + 1], e)

            @block.scalar
            def _(act):
                act.wait_ge(loaded, 48)
                nc.scalar.mul(k.cum_w[:, :], k.cum, -float(np.exp(-0.5)))

        xs = ExitStack()
        h_stack = ExitStack()
        og_stack = ExitStack()
        z_stack = ExitStack()
        gl = ExitStack()
        og = hold(og_stack, "og", [P, GH, T])
        z = hold(z_stack, "rwkv_z", [P, R_TILES, T])
        hT = hold(h_stack, "hT", [P, KD, T], "right")
        xT = hold(xs, "xT_first", [P, KD, T])
        transpose_in(nc, k, "x_in", x, xT, T)
        rms_norm(nc, k, "norm_mix", xT, hT, k.par["norm_mix_g"], T)
        xs.close()
        full = lambda t: (lambda kt, h: t[:, kt, h * HALF:(h + 1) * HALF])

        qk = hold(gl, "gla_qk", [P, 4, T])
        gate = hold(gl, "gla_gate", [P, 4, T])
        vtok = hold(gl, "gla_v", [P, NC, GH * GV])
        lo = hold(gl, "gla_lo", [RANK, T])
        dense(nc, "proj_qk", [(4, [w_in[:, 0:512]])], full(hT), KD, copy_out(nc, qk, 0, 4))
        dense(nc, "proj_gate", [(4, [w_in[:, 1024:1536]])], full(hT), KD, copy_out(nc, gate, 0, 4))
        token_major(nc, "proj_v", hT, KD, w_in[:, 512:1024], vtok, T, GH * GV)
        low_rank(nc, "proj_lo", w_in[:, 1536:G_COLS], hT, lo)
        gla(nc, k, qk[:, 0:2, :], qk[:, 2:4, :], gate, lo[:, :], vtok, gla_wa2, og)
        gl.close()

        dense(nc, "proj_rwkv", [(R_TILES, [w_in[:, G_COLS:]])], full(hT), KD, shift_mix_out(nc, z, k.par["rwkv_mu"]))
        h_stack.close()
        rwkv(nc, k, z, rwkv_w2, rwkv_a2, rwkv_g2)

        xs = ExitStack()
        xT = hold(xs, "xT", [P, KD, T], "right")
        transpose_in(nc, k, "x_again", x, xT, T)
        both = lambda kt, h: (og[:, kt, :] if kt < GH else z[:, kt - GH, :])[:, h * HALF:(h + 1) * HALF]
        dense(nc, "proj_out", [(KD, [w_out])], both, KD, add_out(nc, xT))
        z_stack.close()
        og_stack.close()

        with ExitStack() as st:
            kT = hold(st, "mem_k", [P, KD, M])
            vm = hold(st, "mem_v", [P, M // P, D])
            with ExitStack() as s2:
                mT = hold(s2, "memT", [P, KD, M])
                mh = hold(s2, "mem_h", [P, KD, M])
                transpose_in(nc, k, "mem_in", mem, mT, M)
                rms_norm(nc, k, "norm_mem", mT, mh, k.par["norm_mem_g"], M)
                memory_keys(nc, "mem_keys", wkv_mem[:, 0:D], mh, kT)
                token_major(nc, "mem_values", mh, KD, wkv_mem[:, D:2 * D], vm, M, D)
            q_sb = hold(st, "q_sb", [P, KD, T])
            o_sb = hold(st, "o_sb", [P, KD, T])
            rms_norm(nc, k, "norm_mem_x", xT, o_sb, k.par["norm_mem_x_g"], T)
            dense(nc, "proj_q", [(KD, [wq_mem])], full(o_sb), KD, copy_out(nc, q_sb, 0, KD))
            attention(nc, k, q_sb, kT, vm, o_sb)
            dense(nc, "proj_o", [(KD, [wo_mem])], full(o_sb), KD, add_out(nc, xT))

        with ExitStack() as st:
            act_sb = hold(st, "ffn_act", [P, FT, T])
            with ExitStack() as s2:
                h2 = hold(s2, "ffn_h", [P, KD, T])
                rms_norm(nc, k, "norm_ffn", xT, h2, k.par["norm_ffn_g"], T)
                dense(nc, "gate_up", [(FT, [w_gate_up[:, 0:FF], w_gate_up[:, FF:2 * FF]])], full(h2), KD,
                      gate_out(nc, act_sb), outs=2)
            dense(nc, "down", [(KD, [w_down])], full(act_sb), FT, add_out(nc, xT))
        with ExitStack() as st:
            yT = hold(st, "yT", [P, KD, T])
            rms_norm(nc, k, "norm_final", xT, yT, k.par["norm_final_g"], T)
            finish(nc, k, "store", yT, out)
        xs.close()


def low_rank(nc, name, w_dram, src, dst):
    with ExitStack() as ctx:
        sb, ps, sem = tiles(nc, ctx, name)
        w = sb("w", [P, KD, RANK])
        bank = ps("bank", [RANK, NH, HALF])
        landed, ready = sem("landed"), sem("ready")
        with nc.Block() as block:
            @block.sync
            def _(sp):
                sp.dma_start(w[:, :, :], w_dram.rearrange("(kt p) f -> p kt f", p=P)).then_inc(landed, 16)

            @block.tensor
            def _(pe):
                pe.wait_ge(landed, 16)
                for h in range(NH):
                    for kt in range(KD):
                        mm = nc.tensor.matmul(bank[:, h, :], w[:, kt, :], src[:, kt, h * HALF:(h + 1) * HALF],
                                              start=(kt == 0), stop=(kt == KD - 1))
                mm.then_inc(ready, 1)

            @block.vector
            def _(dve):
                dve.wait_ge(ready, 1)
                nc.vector.tensor_copy(halves(dst[:, :]), bank[:, :, :])


def memory_keys(nc, name, w_dram, src, dst):
    with ExitStack() as ctx:
        sb, ps, sem = tiles(nc, ctx, name)
        w = sb("w", [P, 2, KD, HALF])
        bank = ps("bank", [P, 2, HALF])
        landed = [sem("landed0"), sem("landed1")]
        ready, copied = sem("ready"), sem("copied")
        cols = w_dram.rearrange("(kt p) (b f) -> b p kt f", p=P, f=HALF)
        with nc.Block() as block:
            @block.sync
            def _(sp):
                for b in range(2):
                    sp.dma_start(w[:, b], cols[b]).then_inc(landed[b], 16)

            @block.tensor
            def _(pe):
                for f in range(KD):
                    b, s = f // 4, slice((f % 4) * P, (f % 4 + 1) * P)
                    pe.wait_ge(landed[b], 16)
                    if f >= 2:
                        pe.wait_ge(copied, f - 1)
                    for kt in range(KD):
                        mm = nc.tensor.matmul(bank[:, f % 2, 0:M], w[:, b, kt, s], src[:, kt, :],
                                              start=(kt == 0), stop=(kt == KD - 1))
                    mm.then_inc(ready, 1)

            @block.vector
            def _(dve):
                for f in range(KD):
                    dve.wait_ge(ready, f + 1)
                    nc.vector.tensor_copy(dst[:, f, :], bank[:, f % 2, 0:M]).then_inc(copied, 1)


def attention(nc, k, q_sb, kT, vm, o_sb):
    scale = float(AD) ** -0.5
    pe_steps = ("scores", "turned", "outputs")
    act_steps = ("q_copied", "exp", "p_copied", "o_copied")
    dve_steps = ("max", "neg_max", "inverse", "probs")
    with ExitStack() as ctx:
        sb, ps, sem = tiles(nc, ctx, "attn")
        q_c = sb("q_c", [P, KD, P])
        top, bias, total, inv = (sb(n, [P, AH]) for n in ("top", "bias", "total", "inv"))
        e = sb("e", [P, AH, M])
        pT = sb("pT", [P, AH, 2, P])
        bank = ps("bank", [P, 6, HALF])
        pe_done, act_done, dve_done = sem("pe_done"), sem("act_done"), sem("dve_done")
        cq = q_sb[:, :, :].rearrange("p f (c t) -> p c f t", t=P)
        co = o_sb[:, :, :].rearrange("p f (c t) -> p c f t", t=P)
        s_ps = bank[:, 0:2, :].rearrange("p b (h m) -> p (b h) m", m=M)
        with nc.Block() as block:
            @block.tensor
            def _(pe):
                pe.sem_inc(pe_done, 1)
                with pe.Fori(0, NC) as c:
                    pe.wait_ge(act_done, at(act_steps, "q_copied", c))
                    for h in range(AH):
                        for d in range(2):
                            mm = nc.tensor.matmul(bank[:, h // 2, (h % 2) * M:(h % 2 + 1) * M], q_c[:, 2 * h + d, :],
                                                  kT[:, 2 * h + d, :], start=(d == 0), stop=(d == 1))
                    mm.then_inc(pe_done, 1)
                    pe.wait_ge(dve_done, at(dve_steps, "probs", c))
                    for h in range(AH):
                        for m in range(2):
                            mm = nc.tensor.transpose(bank[:, 2 + h // 2, ((h % 2) * 2 + m) * P:((h % 2) * 2 + m + 1) * P],
                                                     e[:, h, m * P:(m + 1) * P], k.const["ident"])
                    mm.then_inc(pe_done, 1)
                    pe.wait_ge(act_done, at(act_steps, "p_copied", c))
                    for f in range(KD):
                        for m in range(2):
                            mm = nc.tensor.matmul(bank[:, 4 + f // 4, (f % 4) * P:(f % 4 + 1) * P],
                                                  vm[:, m, f * P:(f + 1) * P], pT[:, f // 2, m, :],
                                                  start=(m == 0), stop=(m == 1))
                    mm.then_inc(pe_done, 1)

            @block.scalar
            def _(act):
                act.sem_inc(act_done, 1)
                with act.Fori(0, NC) as c:
                    act.wait_ge(pe_done, before(pe_steps, c))
                    nc.scalar.copy(q_c[:, :, :], cq[:, c, :, :]).then_inc(act_done, 1)
                    act.wait_ge(dve_done, at(dve_steps, "neg_max", c))
                    for h in range(AH):
                        mm = nc.scalar.activation(e[:, h, :], s_ps[:, h, :], ACT.Exp, bias=bias[:, h:h + 1],
                                                  scale=scale, accum_out=total[:, h:h + 1])
                    mm.then_inc(act_done, 1)
                    act.wait_ge(pe_done, at(pe_steps, "turned", c))
                    nc.scalar.copy(pT[:, :, :, :].rearrange("p h m t -> p (h m t)"),
                                   bank[:, 2:4, :].rearrange("p b t -> p (b t)")).then_inc(act_done, 1)
                    act.wait_ge(pe_done, at(pe_steps, "outputs", c))
                    nc.scalar.copy(co[:, c, :, :], bank[:, 4:6, :].rearrange("p b (f t) -> p (b f) t", t=P))\
                        .then_inc(act_done, 1)

            @block.vector
            def _(dve):
                dve.sem_inc(dve_done, 1)
                with dve.Fori(0, NC) as c:
                    dve.wait_ge(pe_done, at(pe_steps, "scores", c))
                    nc.vector.tensor_reduce(top[:, :], s_ps, mybir.AxisListType.X, ALU.max).then_inc(dve_done, 1)
                    dve.wait_ge(dve_done, at(dve_steps, "max", c))
                    nc.vector.tensor_scalar(bias[:, :], top[:, :], -scale, None, ALU.mult).then_inc(dve_done, 1)
                    dve.wait_ge(act_done, at(act_steps, "exp", c))
                    nc.vector.reciprocal(inv[:, :], total[:, :]).then_inc(dve_done, 1)
                    dve.wait_ge(dve_done, at(dve_steps, "inverse", c))
                    nc.vector.tensor_tensor(e[:, :, :], e[:, :, :], wide(inv[:, :], M), ALU.mult).then_inc(dve_done, 1)


WEIGHTS = ["w_in", "gla_wa2", "rwkv_w2", "rwkv_a2", "rwkv_g2", "w_out", "wq_mem", "wkv_mem", "wo_mem", "w_gate_up",
           "w_down"]


def kernel(**inputs):
    import concourse.bacc as bacc
    from concourse.bass_utils import run_bass_kernel_spmd

    nc = bacc.Bacc("TRN2", target_bir_lowering=False, num_devices=1)
    a = {name: np.ascontiguousarray(value) for name, value in inputs.items()}
    arrays = {"x": a["x"][0], "mem": a["mem"][0]}
    arrays.update({name: a[name][0] for name in WEIGHTS})
    arrays["consts"] = constants()
    arrays["params"] = np.concatenate([a[name].reshape(n, P).T for name, n in PARAMS], axis=1)
    arrays["rows"] = np.concatenate([a[name].reshape(1, n) for name, n in ROWS], axis=1)
    arrays = {name: np.ascontiguousarray(value) for name, value in arrays.items()}
    args = [nc.dram_tensor(f"in_{name}", value.shape, F32, kind="ExternalInput").ap()
            for name, value in arrays.items()]
    args.append(nc.dram_tensor("out_0", (T, D), F32, kind="ExternalOutput").ap())
    block_kernel(nc, *args)
    r = run_bass_kernel_spmd(nc, [{f"in_{name}": value for name, value in arrays.items()}], core_ids=[0])
    return r.results[0]["out_0"].reshape(1, T, D)
```

```python
from contextlib import ExitStack

import numpy as np

import concourse.bass as bass
from concourse import mybir

F32 = mybir.dt.float32
F32R = mybir.dt.float32r
ALU = mybir.AluOpType
ACT = mybir.ActivationFunctionType

P = 128
D = 1024
KD = D // P
T = 1024
NC = T // P
HALF = 512
NH = T // HALF
M = 256
EPS = 1e-6
GH, GK, GV = 4, 64, 128
G_EPS = 1e-5
RANK = 16
G_COLS = 1552
RH, RN = 8, 64
RT = RH * RN // P
R_EPS = 64e-5
R_TILES = 14
AH, AD = 4, 256
FF = 2816
FT = FF // P
FF_GROUPS = (8, 8, 6)

CONSTS = ["ident", "ones", "pair_ones", "cum_in", "cum_ex", "diag_up", "up_incl", "up_strict",
          "up_incl_2", "diag_lo", "merge16", "merge32", "merge64"]
PARAMS = [("norm_mix_g", KD), ("norm_mem_x_g", KD), ("norm_mem_g", KD), ("norm_ffn_g", KD),
          ("norm_final_g", KD), ("gla_norm_g", 1), ("rwkv_mu", R_TILES), ("rwkv_k_k", RT),
          ("rwkv_k_a", RT), ("rwkv_a0", RT), ("rwkv_r_k", RT), ("rwkv_ln_g", RT), ("rwkv_ln_b", RT)]
ROWS = [("gla_ba", GH * GK), ("rwkv_w0", RH * RN)]


class Kept:

    def __init__(self):
        self.const, self.par, self.row = {}, {}, {}


def constants():
    s = np.arange(P)[:, None]
    t = np.arange(P)[None, :]
    mid = s <= P // 2 - 1
    same = lambda n: s // n == t // n
    return np.concatenate([np.asarray(m, np.float32) for m in (
        s == t, np.ones((P, P)), same(RN),
        (s <= t) * 1.0 - mid, (s < t) * 1.0 - mid,
        (s < t) & same(16), s <= t, s < t, s <= t,
        (s > t) & same(16), (s > t) & same(32) & ~same(16), (s > t) & same(64) & ~same(32),
        (s > t) & ~same(64))], axis=1)


def at(steps, name, turn):
    return turn * len(steps) + steps.index(name) + 2


def before(steps, turn):
    return turn * len(steps) + 1


PAST = []


def tiles(nc, ctx, prefix):
    def sb(name, shape):
        return ctx.enter_context(nc.sbuf_tensor(f"{prefix}_{name}", shape, F32))

    def ps(name, shape):
        return ctx.enter_context(nc.psum_tensor(f"{prefix}_{name}", shape, F32))

    def sem(name):
        s = ctx.enter_context(nc.semaphore(f"{prefix}_{name}"))
        PAST.append(s)
        return s
    return sb, ps, sem


def clear_semaphores(nc, used):
    with nc.Block() as block:
        @block.sync
        def _(sp):
            for s in used:
                sp.sem_clear(s)
    used.clear()


def wide(scalars, n):
    return scalars.unsqueeze(2).to_broadcast([scalars.shape[0], scalars.shape[1], n])


def transpose_in(nc, k, name, src, dst, n_tok, to_split=()):
    nt = n_tok // P
    rows = src.rearrange("(c p) f -> c p f", p=P)
    with ExitStack() as ctx:
        sb, ps, sem = tiles(nc, ctx, name)
        tok = sb("tok", [P, 2, D])
        bank = ps("bank", [P, 2, KD, P])
        landed = [sem("landed0"), sem("landed1")]
        turned, copied = sem("turned"), sem("copied")
        rounded = sem("rounded")
        with nc.Block() as block:
            if to_split:
                @block.scalar
                def _(act):
                    for x_full, hi, _ in to_split:
                        nc.scalar.copy(hi, x_full).then_inc(rounded, 1)

                @block.gpsimd
                def _(pool):
                    for n, (x_full, hi, lo) in enumerate(to_split):
                        pool.wait_ge(rounded, n + 1)
                        nc.gpsimd.tensor_tensor(lo, x_full, hi.bitcast(F32), ALU.subtract)

            @block.sync
            def _(sp):
                for c in range(nt):
                    if c >= 2:
                        sp.wait_ge(turned, c - 1)
                    sp.dma_start(tok[:, c % 2, :], rows[c]).then_inc(landed[c % 2], 16)

            @block.tensor
            def _(pe):
                for c in range(nt):
                    pe.wait_ge(landed[c % 2], 16 * (c // 2 + 1))
                    if c >= 2:
                        pe.wait_ge(copied, c - 1)
                    for f in range(KD):
                        mm = nc.tensor.transpose(bank[:, c % 2, f, :], tok[:, c % 2, f * P:(f + 1) * P],
                                                 k.const["ident"])
                    mm.then_inc(turned, 1)

            @block.vector
            def _(dve):
                for c in range(nt):
                    dve.wait_ge(turned, c + 1)
                    nc.vector.tensor_copy(dst[:, :, c * P:(c + 1) * P], bank[:, c % 2]).then_inc(copied, 1)


def rms_norm(nc, k, name, src, dst, gain, n_tok):
    parts = isinstance(dst, tuple)
    w = min(HALF, n_tok)
    nh = n_tok // w
    with ExitStack() as ctx:
        sb, ps, sem = tiles(nc, ctx, name)
        sq = sb("sq", [P, 2, n_tok])
        root = sb("root", [P, n_tok])
        rstd = sb("rstd", [P, n_tok])
        total = ps("total", [P, nh, HALF])
        squared, summed, rooted, inverted, scaled = (sem(n) for n in ("squared", "summed", "rooted", "inverted",
                                                                      "scaled"))
        rounded, split = sem("rounded"), sem("split")
        full = sb("full", [P, 2, n_tok]) if parts else None
        with nc.Block() as block:
            @block.scalar
            def _(act):
                for kt in range(KD):
                    if kt >= 2:
                        act.wait_ge(summed, kt - 1)
                    nc.scalar.activation(sq[:, kt % 2, :], src[:, kt, :], ACT.Square).then_inc(squared, 1)
                act.wait_ge(summed, KD)
                for h in range(nh):
                    mm = nc.scalar.activation(root[:, h * w:(h + 1) * w], total[:, h, 0:w], ACT.Sqrt,
                                              scale=1.0 / D, bias=k.eps[:, 0:1])
                mm.then_inc(rooted, 1)
                if parts:
                    for kt in range(KD):
                        act.wait_ge(scaled, kt + 1)
                        nc.scalar.copy(dst[0][:, kt, :], full[:, kt % 2, :]).then_inc(rounded, 1)

            if parts:
                @block.gpsimd
                def _(pool):
                    for kt in range(KD):
                        pool.wait_ge(rounded, kt + 1)
                        nc.gpsimd.tensor_tensor(dst[1][:, kt, :], full[:, kt % 2, :], dst[0][:, kt, :].bitcast(F32),
                                                ALU.subtract).then_inc(split, 1)

            @block.tensor
            def _(pe):
                for kt in range(KD):
                    pe.wait_ge(squared, kt + 1)
                    for h in range(nh):
                        mm = nc.tensor.matmul(total[:, h, 0:w], k.const["ones"], sq[:, kt % 2, h * w:(h + 1) * w],
                                              start=(kt == 0), stop=(kt == KD - 1))
                    mm.then_inc(summed, 1)

            @block.vector
            def _(dve):
                dve.wait_ge(rooted, 1)
                nc.vector.reciprocal(rstd[:, :], root[:, :]).then_inc(inverted, 1)
                dve.wait_ge(inverted, 1)
                for kt in range(KD):
                    if parts and kt >= 2:
                        dve.wait_ge(split, kt - 1)
                    nc.vector.scalar_tensor_tensor(out=full[:, kt % 2, :] if parts else dst[:, kt, :],
                                                   in0=src[:, kt, :], scalar=gain[:, kt:kt + 1], in1=rstd[:, :],
                                                   op0=ALU.mult, op1=ALU.mult).then_inc(scaled, 1)


def turns(eng, n, body):
    if n >= 2:
        with eng.Fori(0, n // 2) as i:
            body(i, 0)
            body(i, 1)
    if n % 2:
        body(n // 2, 0)


def turns_ahead(eng, n, prepare, body):
    prepare(0, 0)
    loops = (n - 1) // 2
    if loops:
        with eng.Fori(0, loops) as i:
            prepare(i, 1)
            body(i, 0)
            prepare(i + 1, 0)
            body(i, 1)
    if n % 2 == 0:
        prepare(loops, 1)
    body(loops, 0)
    if n % 2 == 0:
        body(loops, 1)


def dense(nc, name, jobs, src, kt_n, drain):
    steps = sum(n for n, _ in jobs)
    with ExitStack() as ctx:
        own = tiles(nc, ctx, name)
        sb, ps, sem = own
        w = sb("w", [P, 2, kt_n, P])
        w_hi = ctx.enter_context(nc.sbuf_tensor(name + "_w_hi", [P, 2, kt_n, P], F32R))
        w_lo = ctx.enter_context(nc.sbuf_tensor(name + "_w_lo", [P, 2, kt_n, P], F32R))
        bank = ps("bank", [P, 2, NH, HALF])
        landed = [sem("landed0"), sem("landed1")]
        rounded, split = sem("rounded"), sem("split")
        ready, free, used = sem("ready"), sem("banks_free"), sem("weights_used")
        act_drain, dve_drain, prologue = drain(own, bank, ready, free)
        with nc.Block() as block:
            @block.sync
            def _(sp):
                base = 0
                for n, view in jobs:
                    if isinstance(view, tuple):
                        m, f0 = view
                        even = m.rearrange("(kt p) (u i f) -> u i p kt f", p=P, u=2, f=P)[:, f0:f0 + n // 2]
                    else:
                        cols = view.rearrange("(kt p) (s f) -> s p kt f", p=P, f=P)
                        even = cols[0:n // 2 * 2].rearrange("(i u) p kt f -> u i p kt f", u=2)

                    def load(i, u):
                        tile = cols[2 * i] if isinstance(i, int) and n % 2 and 2 * i + u == n - 1 else even[u, i]
                        sp.dma_start(w[:, u], tile).then_inc(landed[u], 16)

                    for u in range(2):
                        if base:
                            sp.wait_ge(split, base + u - 1)
                        load(0, u)
                    if n > 3:
                        with sp.Fori(1, n // 2) as i:
                            for u in range(2):
                                sp.wait_ge(split, 2 * i + (base + u - 1))
                                load(i, u)
                    if n % 2:
                        sp.wait_ge(split, base + n - 2)
                        load(n // 2, 0)
                    base += n

            @block.tensor
            def _(pe):
                def products(i, u):
                    pe.wait_ge(split, 2 * i + u + 1)
                    pe.wait_ge(free, 2 * i + u + 1)
                    for h in range(NH):
                        for kt in range(kt_n):
                            hi, lo = src(kt, h)
                            for n, (a, b) in enumerate(((w_hi, hi), (w_hi, lo), (w_lo, hi))):
                                mm = nc.tensor.matmul(bank[:, u, h, :], a[:, u, kt, :], b,
                                                      start=(kt == 0 and n == 0), stop=(kt == kt_n - 1 and n == 2))
                    mm.then_inc(ready, 1)

                turns(pe, steps, products)

            @block.scalar
            def _(act):
                def round_weights(i, u):
                    act.wait_ge(landed[u], (i + 1) * 16)
                    act.wait_ge(used, 2 * i + u + 1)
                    nc.scalar.copy(w_hi[:, u], w[:, u]).then_inc(rounded, 1)

                act.sem_inc(used, 2)
                if prologue:
                    prologue(act)
                turns_ahead(act, steps, round_weights, act_drain or (lambda i, u: None))

            @block.gpsimd
            def _(pool):
                def rest(i, u):
                    pool.wait_ge(rounded, 2 * i + u + 1)
                    nc.gpsimd.tensor_tensor(w_lo[:, u], w[:, u], w_hi[:, u].bitcast(F32), ALU.subtract).then_inc(split, 1)

                turns(pool, steps, rest)

            @block.vector
            def _(dve):
                def step(i, u):
                    dve.wait_ge(ready, 2 * i + u + 1)
                    dve.sem_inc(used, 1)
                    if dve_drain:
                        dve_drain(i, u)

                dve.sem_inc(free, 2)
                turns(dve, steps, step)


def halves(x):
    return x.rearrange("p (h t) -> p h t", h=NH)


class Steps:

    def __init__(self, x, n):
        self.x, self.n = x, n
        self.pairs = x[:, 0:n // 2 * 2].rearrange("p (i u) t -> p i u t", u=2)

    def __call__(self, i, u):
        if isinstance(i, int):
            return self.x[:, 2 * i + u, :]
        return self.pairs[:, i, u, :]


def copy_out(nc, dst, n):
    out = Steps(dst, n)

    def drain(own, bank, ready, free):
        def act_step(i, u):
            nc.scalar.wait_ge(ready, 2 * i + u + 1)
            nc.scalar.copy(halves(out(i, u)), bank[:, u]).then_inc(free, 1)
        return act_step, None, None
    return drain


def add_out(nc, dst):
    out = Steps(dst, KD)

    def drain(own, bank, ready, free):
        def dve_step(i, u):
            x = halves(out(i, u))
            nc.vector.tensor_tensor(x, x, bank[:, u], ALU.add).then_inc(free, 1)
        return None, dve_step, None
    return drain


def shift_mix_out(nc, dst, mu):
    out = Steps(dst, R_TILES)
    mus = Steps(mu.unsqueeze(2), R_TILES)

    def drain(own, bank, ready, free):
        sb, _, sem = own
        raw = sb("raw", [P, 2, T + 1])
        diff = sb("diff", [P, 2, T])
        mu_of = sb("mu_of", [P, 2])
        zeroed, stored, mixed, subtracted = (sem(n) for n in ("zeroed", "stored", "mixed", "subtracted"))

        def prologue(act):
            act.sem_inc(mixed, 2)
            nc.scalar.mul(raw[:, :, 0:1], mu[:, 0:2].unsqueeze(2), 0.0).then_inc(zeroed, 1)

        def act_step(i, u):
            nc.scalar.wait_ge(ready, 2 * i + u + 1)
            nc.scalar.wait_ge(mixed, 2 * i + u + 1)
            nc.scalar.copy(halves(raw[:, u, 1:T + 1]), bank[:, u]).then_inc(free, 1)
            nc.scalar.copy(mu_of[:, u:u + 1], mus(i, u)).then_inc(stored, 1)

        def dve_step(i, u):
            nc.vector.wait_ge(stored, 2 * i + u + 1)
            nc.vector.tensor_tensor(diff[:, u, :], raw[:, u, 0:T], raw[:, u, 1:T + 1],
                                    ALU.subtract).then_inc(subtracted, 1)
            nc.vector.wait_ge(subtracted, 2 * i + u + 1)
            nc.vector.scalar_tensor_tensor(out=out(i, u), in0=diff[:, u, :], scalar=mu_of[:, u:u + 1],
                                           in1=raw[:, u, 1:T + 1], op0=ALU.mult, op1=ALU.add).then_inc(mixed, 1)
        return act_step, dve_step, prologue
    return drain


def gate_out(nc, hi, lo):
    def drain(own, bank, ready, free):
        sb, _, sem = own
        silu, prod = sb("silu", [P, T]), sb("prod", [P, T])
        activated, gated, rounded, kept = sem("activated"), sem("gated"), sem("act_rounded"), sem("kept")

        def prologue(act):
            act.sem_inc(kept, 1)

        def act_step(i, u):
            if u == 0:
                nc.scalar.wait_ge(ready, 2 * i + 1)
                nc.scalar.wait_ge(kept, i + 1)
                nc.scalar.activation(halves(silu[:, :]), bank[:, 0], ACT.Silu).then_inc(activated, 1)
            else:
                nc.scalar.wait_ge(gated, i + 1)
                nc.scalar.copy(hi[:, i, :], prod[:, :]).then_inc(rounded, 1)

        def dve_step(i, u):
            if u == 0:
                nc.vector.wait_ge(activated, i + 1)
                nc.vector.sem_inc(free, 1)
            else:
                nc.vector.tensor_tensor(halves(prod[:, :]), halves(silu[:, :]), bank[:, 1], ALU.mult).then_inc(gated, 1)
                nc.vector.wait_ge(gated, i + 1)
                nc.vector.sem_inc(free, 1)
                nc.vector.wait_ge(rounded, i + 1)
                nc.vector.tensor_tensor(lo[:, i, :], prod[:, :], hi[:, i, :].bitcast(F32),
                                        ALU.subtract).then_inc(kept, 1)
        return act_step, dve_step, prologue
    return drain


def token_major(nc, name, src, kt_n, w_dram, dst, n_tok, width):
    nt = n_tok // P
    parts = isinstance(src, tuple)
    nb = width // HALF
    with ExitStack() as ctx:
        sb, ps, sem = tiles(nc, ctx, name)
        w = sb("w", [P, nb, kt_n, HALF])
        if parts:
            w_hi = ctx.enter_context(nc.sbuf_tensor(name + "_w_hi", [P, nb, kt_n, HALF], F32R))
            w_lo = ctx.enter_context(nc.sbuf_tensor(name + "_w_lo", [P, nb, kt_n, HALF], F32R))
            pairs = ((src[0], w_hi), (src[1], w_hi), (src[0], w_lo))
        else:
            pairs = ((src, w),)
        bank = ps("bank", [P, 2, HALF])
        landed = [sem(f"landed{n}") for n in range(kt_n)]
        ready, copied, rounded, split = sem("ready"), sem("copied"), sem("rounded"), sem("split")
        rows = w_dram.rearrange("(kt p) (b f) -> kt p b f", p=P, f=HALF)
        with nc.Block() as block:
            @block.sync
            def _(sp):
                for kt in range(kt_n):
                    sp.dma_start(w[:, :, kt, :], rows[kt]).then_inc(landed[kt], 16)

            @block.tensor
            def _(pe):
                for b in range(nb):
                    for c in range(nt):
                        n = b * nt + c
                        if n >= 2:
                            pe.wait_ge(copied, n - 1)
                        for kt in range(kt_n):
                            if parts and n == 0:
                                pe.wait_ge(split, kt + 1)
                            elif n == 0:
                                pe.wait_ge(landed[kt], 16)
                            for m, (x, y) in enumerate(pairs):
                                mm = nc.tensor.matmul(bank[:, n % 2, :], x[:, kt, c * P:(c + 1) * P], y[:, b, kt, :],
                                                      start=(kt == 0 and m == 0),
                                                      stop=(kt == kt_n - 1 and m == len(pairs) - 1))
                        mm.then_inc(ready, 1)

            if parts:
                @block.scalar
                def _(act):
                    for kt in range(kt_n):
                        act.wait_ge(landed[kt], 16)
                        nc.scalar.copy(w_hi[:, :, kt, :], w[:, :, kt, :]).then_inc(rounded, 1)

                @block.gpsimd
                def _(pool):
                    for kt in range(kt_n):
                        pool.wait_ge(rounded, kt + 1)
                        nc.gpsimd.tensor_tensor(w_lo[:, :, kt, :], w[:, :, kt, :], w_hi[:, :, kt, :].bitcast(F32),
                                                ALU.subtract).then_inc(split, 1)

            @block.vector
            def _(dve):
                for b in range(nb):
                    for c in range(nt):
                        n = b * nt + c
                        dve.wait_ge(ready, n + 1)
                        nc.vector.tensor_copy(dst[:, c, b * HALF:(b + 1) * HALF], bank[:, n % 2, :]).then_inc(copied, 1)


def finish(nc, k, name, src, out):
    rows = out.rearrange("(c p) f -> c p f", p=P)
    with ExitStack() as ctx:
        sb, ps, sem = tiles(nc, ctx, name)
        tok = sb("tok", [P, 2, KD, P])
        bank = ps("bank", [P, 2, KD, P])
        turned, copied = sem("turned"), sem("copied")
        written = [sem("written0"), sem("written1")]
        with nc.Block() as block:
            @block.tensor
            def _(pe):
                for c in range(NC):
                    if c >= 2:
                        pe.wait_ge(copied, c - 1)
                    for f in range(KD):
                        mm = nc.tensor.transpose(bank[:, c % 2, f, :], src[:, f, c * P:(c + 1) * P], k.const["ident"])
                    mm.then_inc(turned, 1)

            @block.vector
            def _(dve):
                for c in range(NC):
                    dve.wait_ge(turned, c + 1)
                    if c >= 2:
                        dve.wait_ge(written[c % 2], 16 * (c // 2))
                    nc.vector.tensor_copy(tok[:, c % 2], bank[:, c % 2]).then_inc(copied, 1)

            @block.sync
            def _(sp):
                for c in range(NC):
                    sp.wait_ge(copied, c + 1)
                    sp.dma_start(rows[c], tok[:, c % 2].rearrange("p k f -> p (k f)")).then_inc(written[c % 2], 16)
                for u in range(2):
                    sp.wait_ge(written[u], 16 * (NC // 2))


def gla(nc, k, q, key, gate, lo, vtok, wa2, og):
    pe_steps = ("logits", "cumsum", "turn_keys", "scores", "outputs", "state")
    act_steps = ("load_lo", "log_decays", "decay_up", "decay_down", "mid_factor", "keep_keys", "keep_outputs")
    dve_steps = ("relu", "decayed", "masked", "entered", "end_factor", "left")
    with ExitStack() as ctx:
        sb, ps, sem = tiles(nc, ctx, "gla")
        wa2_sb = sb("wa2", [RANK, GH * GK])
        lo_c = sb("lo_c", [RANK, P])
        neg = sb("neg", [P, GH * GK])
        mag = sb("mag", [P, 2, GH * GK])
        soft = sb("soft", [P, GH * GK])
        la = sb("la", [P, GH * GK])
        up = sb("up", [P, 2, P])
        down = sb("down", [P, 2, P])
        mid = sb("mid", [P, 2])
        last = sb("last", [P, 2])
        qd = sb("qd", [P, 2, P])
        ki = sb("ki", [P, 2, P])
        kt = sb("kt", [P, 2, P])
        sc = sb("sc", [P, GH, P])
        state = sb("state", [P, 2, GV])
        entry = sb("entry", [P, 2, GV])
        b = [ps(f"b{n}", [P, HALF]) for n in range(8)]
        pe_done, act_done, dve_done = sem("pe_done"), sem("act_done"), sem("dve_done")
        loaded, zeroed, scratch = sem("loaded"), sem("zeroed"), sem("scratch")
        sub = sem("sub")
        chunk = lambda x: x.rearrange("p h (c t) -> p c h t", t=P)
        cq, ck = chunk(q), chunk(key)
        clo = lo.rearrange("p (c t) -> p c t", t=P)
        cog = chunk(og)
        vcur = sb("vcur", [P, GH * GV])
        with nc.Block() as block:
            @block.sync
            def _(sp):
                sp.dma_start(wa2_sb[:, :], wa2).then_inc(loaded, 16)

            @block.tensor
            def _(pe):
                pe.wait_ge(loaded, 16)
                pe.sem_inc(pe_done, 1)
                with pe.Fori(0, NC) as c:
                    pe.wait_ge(act_done, at(act_steps, "load_lo", c))
                    nc.tensor.matmul(b[0][:, 0:GH * GK], k.ones_row[0:1, 0:P], k.row["gla_ba"], start=True, stop=False)
                    nc.tensor.matmul(b[0][:, 0:GH * GK], lo_c[:, :], wa2_sb[:, :],
                                     start=False, stop=True).then_inc(pe_done, 1)
                    pe.wait_ge(act_done, at(act_steps, "log_decays", c))
                    pe.wait_ge(dve_done, at(dve_steps, "relu", c))
                    for f in range(2):
                        mm = nc.tensor.matmul(b[1][:, f * 2 * P:(f + 1) * 2 * P], la[:, f * P:(f + 1) * P], k.cum,
                                              start=True, stop=True)
                    mm.then_inc(pe_done, 1)
                    pe.wait_ge(dve_done, at(dve_steps, "decayed", c))
                    for f in range(2):
                        mm = nc.tensor.transpose(b[2][:, f * P:(f + 1) * P], ki[:, f, :], k.const["ident"])
                    mm.then_inc(pe_done, 1)
                    for h in range(GH):
                        r = slice(GK * (h % 2), GK * (h % 2) + GK)
                        mm = nc.tensor.matmul(b[3 + 3 * (h % 2)][:, (h // 2) * P:(h // 2 + 1) * P], ki[r, h // 2, :], qd[r, h // 2, :],
                                              start=True, stop=True)
                    mm.then_inc(pe_done, 1)
                    pe.wait_ge(dve_done, at(dve_steps, "entered", c))
                    for h in range(GH):
                        r = slice(GK * (h % 2), GK * (h % 2) + GK)
                        o = b[4 + 3 * (h % 2)][:, (h // 2) * P:(h // 2 + 1) * P]
                        nc.tensor.matmul(o, vcur[:, h * GV:(h + 1) * GV], sc[:, h, :],
                                         start=True, stop=False)
                        mm = nc.tensor.matmul(o, entry[r, h // 2, :], qd[r, h // 2, :],
                                              start=False, stop=True)
                    mm.then_inc(pe_done, 1)
                    pe.wait_ge(act_done, at(act_steps, "keep_keys", c))
                    for h in range(GH):
                        r = slice(GK * (h % 2), GK * (h % 2) + GK)
                        mm = nc.tensor.matmul(b[5][r, (h // 2) * GV:(h // 2 + 1) * GV],
                                              kt[:, h // 2, GK * (h % 2):GK * (h % 2) + GK],
                                              vcur[:, h * GV:(h + 1) * GV], start=True, stop=True)
                    mm.then_inc(pe_done, 1)

            @block.scalar
            def _(act):
                act.sem_inc(act_done, 1)
                with act.Fori(0, NC) as c:
                    act.wait_ge(dve_done, before(dve_steps, c))
                    nc.scalar.copy(vcur[:, :], vtok[:, c, :])
                    nc.scalar.copy(lo_c[:, :], clo[:, c, :]).then_inc(act_done, 1)
                    act.wait_ge(pe_done, at(pe_steps, "logits", c))
                    nc.scalar.activation(mag[:, 0, :], b[0][:, 0:GH * GK], ACT.Abs).then_inc(sub, 1)
                    act.wait_ge(sub, 2 * c + 1)
                    nc.scalar.activation(mag[:, 1, :], mag[:, 0, :], ACT.Exp, scale=-1.0).then_inc(sub, 1)
                    act.wait_ge(sub, 2 * c + 2)
                    nc.scalar.activation(soft[:, :], mag[:, 1, :], ACT.Ln, bias=1.0).then_inc(act_done, 1)
                    act.wait_ge(pe_done, at(pe_steps, "cumsum", c))
                    cum = b[1][:, :].rearrange("p (f w t) -> p f w t", f=2, w=2)
                    nc.scalar.activation(up[:, :, :], cum[:, :, 0, :], ACT.Exp, scale=1.0 / 16).then_inc(act_done, 1)
                    nc.scalar.activation(down[:, :, :], cum[:, :, 0, :], ACT.Exp, scale=-1.0 / 16).then_inc(act_done, 1)
                    nc.scalar.activation(mid[:, :], cum[:, :, 1, 0], ACT.Exp, scale=-1.0 / 16).then_inc(act_done, 1)
                    act.wait_ge(pe_done, at(pe_steps, "turn_keys", c))
                    nc.scalar.copy(kt[:, :, :], b[2][:, 0:2 * P].rearrange("p (f t) -> p f t", f=2)).then_inc(act_done, 1)
                    act.wait_ge(pe_done, at(pe_steps, "outputs", c))
                    for e in range(2):
                        mm = nc.scalar.copy(cog[:, c, e:GH:2, :],
                                            b[4 + 3 * e][:, 0:2 * P].rearrange("p (h t) -> p h t", h=2))
                    mm.then_inc(act_done, 1)

            @block.vector
            def _(dve):
                nc.vector.memset(state[:, :, :], 0.0).then_inc(zeroed, 1)
                dve.wait_ge(zeroed, 1)
                dve.sem_inc(dve_done, 1)
                with dve.Fori(0, NC) as c:
                    dve.wait_ge(act_done, at(act_steps, "log_decays", c))
                    nc.vector.tensor_scalar(neg[:, :], b[0][:, 0:GH * GK], 0.0, None, ALU.min).then_inc(scratch, 1)
                    dve.wait_ge(scratch, 2 * c + 1)
                    nc.vector.tensor_tensor(la[:, :], neg[:, :], soft[:, :], ALU.subtract).then_inc(dve_done, 1)
                    dve.wait_ge(act_done, at(act_steps, "decay_down", c))
                    nc.vector.scalar_tensor_tensor(out=qd[:, :, :], in0=cq[:, c, :, :], scalar=GK ** -0.5,
                                                   in1=up[:, :, :], op0=ALU.mult, op1=ALU.mult)
                    nc.vector.tensor_tensor(ki[:, :, :], ck[:, c, :, :], down[:, :, :], ALU.mult).then_inc(dve_done, 1)
                    dve.wait_ge(pe_done, at(pe_steps, "scores", c))
                    for e in range(2):
                        mm = nc.vector.tensor_tensor(sc[:, e:GH:2, :],
                                                     b[3 + 3 * e][:, 0:2 * P].rearrange("p (h t) -> p h t", h=2),
                                                     k.const["up_incl"].unsqueeze(1).to_broadcast([P, 2, P]), ALU.mult)
                    mm.then_inc(dve_done, 1)
                    dve.wait_ge(act_done, at(act_steps, "mid_factor", c))
                    nc.vector.tensor_tensor(entry[:, :, :], state[:, :, :], wide(mid[:, :], GV),
                                            ALU.mult).then_inc(dve_done, 1)
                    dve.wait_ge(pe_done, at(pe_steps, "state", c))
                    nc.vector.tensor_tensor(entry[:, :, :], entry[:, :, :],
                                            b[5][:, 0:2 * GV].rearrange("p (f v) -> p f v", f=2),
                                            ALU.add).then_inc(dve_done, 1)
                    dve.wait_ge(dve_done, at(dve_steps, "end_factor", c))
                    nc.vector.tensor_copy(last[:, :], up[:, :, P - 1]).then_inc(scratch, 1)
                    dve.wait_ge(scratch, 2 * c + 2)
                    dve.wait_ge(act_done, at(act_steps, "keep_outputs", c))
                    nc.vector.tensor_tensor(state[:, :, :], entry[:, :, :], wide(last[:, :], GV),
                                            ALU.mult).then_inc(dve_done, 1)
                    dve.wait_ge(dve_done, at(dve_steps, "left", c))

    with ExitStack() as ctx:
        sb, ps, sem = tiles(nc, ctx, "gla_norm")
        sq = sb("sq", [P, 2, T])
        root = sb("root", [P, 2, T])
        rstd = sb("rstd", [P, 2, T])
        silu = sb("silu", [P, 2, T])
        total = ps("total", [P, 2, NH, HALF])
        squared, summed, rooted, scaled, silus = (sem(n) for n in ("squared", "summed", "rooted", "scaled", "silus"))
        with nc.Block() as block:
            @block.scalar
            def _(act):
                for h in range(GH):
                    u = h % 2
                    if h >= 2:
                        act.wait_ge(scaled, 3 * (h - 1))
                    nc.scalar.activation(sq[:, u, :], og[:, h, :], ACT.Square).then_inc(squared, 1)
                    nc.scalar.activation(silu[:, u, :], gate[:, h, :], ACT.Silu).then_inc(silus, 1)
                    act.wait_ge(summed, h + 1)
                    nc.scalar.activation(halves(root[:, u, :]), total[:, u], ACT.Sqrt, scale=1.0 / GV,
                                         bias=k.eps[:, 1:2]).then_inc(rooted, 1)

            @block.tensor
            def _(pe):
                for h in range(GH):
                    pe.wait_ge(squared, h + 1)
                    for n in range(NH):
                        mm = nc.tensor.matmul(total[:, h % 2, n, :], k.const["ones"],
                                              sq[:, h % 2, n * HALF:(n + 1) * HALF], start=True, stop=True)
                    mm.then_inc(summed, 1)

            @block.vector
            def _(dve):
                for h in range(GH):
                    u = h % 2
                    dve.wait_ge(rooted, h + 1)
                    nc.vector.reciprocal(rstd[:, u, :], root[:, u, :]).then_inc(scaled, 1)
                    dve.wait_ge(scaled, 3 * h + 1)
                    nc.vector.scalar_tensor_tensor(out=og[:, h, :], in0=og[:, h, :], scalar=k.par["gla_norm_g"][:, 0:1],
                                                   in1=rstd[:, u, :], op0=ALU.mult, op1=ALU.mult).then_inc(scaled, 1)
                    dve.wait_ge(scaled, 3 * h + 2)
                    dve.wait_ge(silus, h + 1)
                    nc.vector.tensor_tensor(og[:, h, :], og[:, h, :], silu[:, u, :], ALU.mult).then_inc(scaled, 1)


PREP_PE = ("decay_logits", "rate_logits", "gates", "key_norms", "turn_v", "cumsum", "bonus", "turn_a", "turn_b",
           "turn_k")
PREP_ACT = ("loras", "decays", "rates", "gates", "key_roots", "keep_v", "down", "ends", "up", "bonus", "keep_a",
            "keep_b", "keep_k")
PREP_DVE = ("raw_kk", "raw_sq", "decay_bias", "rate_bias", "root_max", "inv_norm", "kk", "rate_k", "k_gain", "key",
            "b_vec", "key_r", "bonus_rk", "k_decayed", "decayed")
CORE_PE = ("gram_n", "gram0", "gram1", "gram2", "gram3", "sq_a", "sq_b", "quad_a", "quad_b", "oct_a", "oct_b",
           "dec_a", "dec_b", "turn_a", "turn_b", "join0_a", "join0_b", "left0_a", "left0_b", "join1_a", "join1_b",
           "left1_a", "left1_b", "join2_a", "join2_b", "left2_a", "left2_b", "removal", "chunk_h", "removed", "state",
           "outputs")
CORE_ACT = ("keep_n", "sq_a", "sq_b", "quad_a", "quad_b", "oct_a", "oct_b", "turn_a", "turn_b", "join0_a", "join0_b",
            "join1_a", "join1_b", "join2_a", "join2_b", "keep_w", "keep_u", "keep_y")
CORE_DVE = ("gram0", "gram1", "gram2", "gram3", "quad_a", "quad_b", "oct_a", "oct_b", "dec_a", "dec_b",
            "left0_a", "leftT0_a", "left0_b", "leftT0_b", "left1_a", "leftT1_a", "left1_b", "leftT1_b", "entered",
            "left2_a", "left2_b", "keep_h", "state_sum", "state")
CORE_POOL = ("diag_a", "plus_a", "diag_b", "plus_b", "merges_a", "merges_b")
CLOSE_PE = ("means", "variances")
CLOSE_ACT = ("centred_sq", "roots")
CLOSE_DVE = ("centred", "inv_std", "normed", "gained", "bonus_v", "with_bias", "with_bonus", "written")


class RwkvTiles:

    def __init__(self, nc, ctx, z):
        sb, ps, sem = tiles(nc, ctx, "rwkv")
        pair = lambda n, s: [sb(f"{n}{u}", s) for u in range(2)]
        self.z = z[:, :, :].rearrange("p f (c t) -> p c f t", t=P)
        self.w2, self.a2, self.g2 = sb("w2", [P, HALF]), sb("a2", [P, HALF]), sb("g2", [P, HALF])
        self.w0 = sb("w0", [P, HALF])
        self.lora = sb("lora", [P, 2, P])
        self.sig_w = sb("sig_w", [P, HALF])
        self.rate, self.kk, self.t1, self.t2, self.key = (sb(n, [P, RT, P]) for n in ("rate", "kk", "t1", "t2", "key"))
        self.gates, self.bonus = pair("gates", [P, RT, P]), pair("bonus", [P, RT, P])
        self.ar = pair("ar", [P, RT, 2, P])
        self.bt, self.kt = pair("bt", [P, RT, P]), pair("kt", [P, RT, P])
        self.mid, self.last = pair("mid", [P, RT]), pair("last", [P, RT])
        self.tok = {n: pair(f"tok_{n}", [P, RH * RN]) for n in "abkv"}
        self.gm = sb("gm", [P, RH, 4, P])
        self.nmat = sb("nmat", [P, RH, P])
        self.merge = sb("merge", [P, 2, RH, P])
        self.d1t, self.x2, self.x2t = (sb(n, [P, RH, P]) for n in ("d1t", "x2", "x2t"))
        self.xp = sb("xp", [P, RH, 2, P])
        self.hu = sb("hu", [P, RH, RN])
        self.wt = sb("wt", [P, RT, P])
        self.state, self.entry = sb("state", [P, RT, RN]), sb("entry", [P, RT, RN])
        self.d1, self.rb, self.ak, self.rk = (self.gm[:, :, n, :] for n in range(4))
        self.y, self.ysq, self.yroot = sb("y", [P, RT, P]), sb("ysq", [P, RT, P]), sb("yroot", [P, RT, P])
        self.bank = ps("bank", [P, 8, HALF])
        self.prep_pe, self.prep_act, self.prep_dve = sem("prep_pe"), sem("prep_act"), sem("prep_dve")
        self.core_pe, self.core_act, self.core_dve = sem("core_pe"), sem("core_act"), sem("core_dve")
        self.core_pool = sem("core_pool")
        self.close_pe, self.close_act, self.close_dve = sem("close_pe"), sem("close_act"), sem("close_dve")
        self.loaded, self.zeroed = sem("loaded"), sem("zeroed")

    def flat(self, b):
        return self.bank[:, b, :].rearrange("p (h t) -> p h t", t=P)


HEADS = {"a": range(0, RH // 2), "b": range(RH // 2, RH)}
HS = {"a": slice(0, RH // 2), "b": slice(RH // 2, RH)}
GROUP_BANK = {"a": 0, "b": 3}


def rows(h):
    return slice(RN * (h % 2), RN * (h % 2) + RN)


def masks(x, n):
    return x.unsqueeze(1).to_broadcast([P, n, x.shape[1]])


def merge_chain(t):
    return [(t.x2, t.x2t), (t.d1, t.d1t), (t.x2, t.x2t), (t.d1, None)], t.xp[:, :, 0, :]


def over_chunks(eng, prepare, core, close):
    prepare(0, 0)
    core(0, 0, (1, 1), None)
    with eng.Fori(0, (NC - 2) // 2) as j:
        core(2 * j + 1, 1, (2 * j + 2, 0), (2 * j, 0))
        core(2 * j + 2, 0, (2 * j + 3, 1), (2 * j + 1, 1))
    core(NC - 1, 1, None, (NC - 2, 0))
    close(NC - 1, 1)


def rwkv_tensor(nc, pe, k, t):
    mm, bank, const = nc.tensor.matmul, t.bank, k.const

    def flat2(x):
        return x.rearrange("p f t -> p (f t)")

    def logits(c, b):
        pe.wait_ge(t.prep_act, at(PREP_ACT, "loras", c))
        mm(bank[:, 6, :], t.lora[:, 0, :], t.w2[:, :], start=True, stop=True).then_inc(t.prep_pe, 1)
        for f in range(RT):
            s = slice(f * P, (f + 1) * P)
            ins = mm(bank[:, 7, s], t.a2[:, s], t.lora[:, 0, :], start=True, stop=True)
        ins.then_inc(t.prep_pe, 1)

    def gates(c, b):
        pe.wait_ge(t.prep_dve, at(PREP_DVE, "decay_bias", c))
        for f in range(RT):
            s = slice(f * P, (f + 1) * P)
            ins = mm(bank[:, 6, s], t.g2[:, s], t.lora[:, 1, :], start=True, stop=True)
        ins.then_inc(t.prep_pe, 1)
        pe.wait_ge(t.prep_dve, at(PREP_DVE, "rate_bias", c))
        mm(bank[:, 7, :], const["pair_ones"], flat2(t.t1[:, :, :]), start=True, stop=True).then_inc(t.prep_pe, 1)

    def turn_v(c, b):
        pe.wait_ge(t.prep_act, at(PREP_ACT, "gates", c))
        for f in range(RT):
            ins = nc.tensor.transpose(bank[:, 6, f * P:(f + 1) * P], t.key[:, f, :], const["ident"])
        ins.then_inc(t.prep_pe, 1)

    def cumsum(c, b):
        pe.wait_ge(t.prep_act, at(PREP_ACT, "keep_v", c))
        for f in range(RT):
            ins = mm(bank[:, 6 + f // 2, (f % 2) * 2 * P:(f % 2 + 1) * 2 * P], t.sig_w[:, f * P:(f + 1) * P],
                     k.cum_w[:, :], start=True, stop=True)
        ins.then_inc(t.prep_pe, 1)

    def bonus(c, b):
        pe.wait_ge(t.prep_act, at(PREP_ACT, "up", c))
        pe.wait_ge(t.prep_dve, at(PREP_DVE, "bonus_rk", c))
        mm(bank[:, 6, :], const["pair_ones"], flat2(t.t1[:, :, :]), start=True, stop=True).then_inc(t.prep_pe, 1)

    def turn_a(c, b):
        pe.wait_ge(t.prep_dve, at(PREP_DVE, "decayed", c))
        for f in range(RT):
            ins = nc.tensor.transpose(bank[:, 7, f * P:(f + 1) * P], t.ar[b][:, f, 0, :], const["ident"])
        ins.then_inc(t.prep_pe, 1)

    def turn_bk(c, b):
        for n, x, last_read in ((6, t.bt[b], "bonus"), (7, t.kt[b], "keep_a")):
            pe.wait_ge(t.prep_act, at(PREP_ACT, last_read, c))
            for f in range(RT):
                ins = nc.tensor.transpose(bank[:, n, f * P:(f + 1) * P], x[:, f, :], const["ident"])
            ins.then_inc(t.prep_pe, 1)

    def prepare(c, b):
        for stage in (logits, gates, turn_v, cumsum, bonus, turn_a, turn_bk):
            stage(c, b)

    def means(c, b):
        pe.wait_ge(t.core_act, at(CORE_ACT, "keep_y", c))
        mm(bank[:, 6, :], const["pair_ones"], flat2(t.y[:, :, :]), start=True, stop=True).then_inc(t.close_pe, 1)

    def variances(c, b):
        pe.wait_ge(t.close_act, at(CLOSE_ACT, "centred_sq", c))
        mm(bank[:, 7, :], const["pair_ones"], flat2(t.ysq[:, :, :]), start=True, stop=True).then_inc(t.close_pe, 1)

    def close(c, b):
        means(c, b)
        variances(c, b)

    def core(c, b, nxt, prev):
        ar, bt, kt = t.ar[b], t.bt[b], t.kt[b]
        tok = {n: x[b] for n, x in t.tok.items()}
        chain, q = merge_chain(t)

        def act(name):
            pe.wait_ge(t.core_act, at(CORE_ACT, name, c))

        def dve(name):
            pe.wait_ge(t.core_dve, at(CORE_DVE, name, c))

        def done(ins):
            ins.then_inc(t.core_pe, 1)

        pe.wait_ge(t.prep_dve, at(PREP_DVE, "decayed", c))
        for h in range(RH):
            ins = mm(bank[:, 4 + h % 2, (h // 2) * P:(h // 2 + 1) * P], ar[rows(h), h // 2, 0, :], bt[rows(h), h // 2, :],
                     start=True, stop=True)
        done(ins)
        pe.wait_ge(t.prep_act, at(PREP_ACT, "keep_k", c))
        if prev:
            pe.wait_ge(t.core_dve, before(CORE_DVE, c))
            means(*prev)
        for n in range(RH // 2):
            b0 = 2 * n % 6
            if n == 2:
                act("keep_n")
            if n == 3:
                dve("gram0")
            for w, x in enumerate((bt, kt)):
                for h in (2 * n, 2 * n + 1):
                    ins = mm(bank[:, b0 + h % 2, w * 2 * P:(w + 1) * 2 * P], x[rows(h), n, :],
                             ar[rows(h), n, :, :].rearrange("p w t -> p (w t)"), start=True, stop=True)
            done(ins)
        if prev:
            variances(*prev)
        for g in "ab":
            b0 = GROUP_BANK[g]
            dve("gram3" if g == "a" else "gram2")
            pe.wait_ge(t.core_pool, at(CORE_POOL, "diag_" + g, c))
            for n, h in enumerate(HEADS[g]):
                s = slice(n * P, (n + 1) * P)
                mm(bank[:, b0, s], t.d1t[:, h, :], t.d1[:, h, :], start=True, stop=True)
                ins = mm(bank[:, b0 + 2, s], t.d1[:, h, :], t.d1t[:, h, :], start=True, stop=True)
            done(ins)
        if nxt:
            if prev:
                pe.wait_ge(t.close_act, at(CLOSE_ACT, "roots", prev[0]))
            logits(*nxt)
        for g in "ab":
            b0 = GROUP_BANK[g]
            act("sq_" + g)
            pe.wait_ge(t.core_pool, at(CORE_POOL, "plus_" + g, c))
            for n, h in enumerate(HEADS[g]):
                s = slice((n % 2) * 2 * P, (n % 2 + 1) * 2 * P)
                mm(bank[:, b0 + n // 2, s], t.x2t[:, h, :], t.xp[:, h, :, :].rearrange("p w t -> p (w t)"),
                   start=True, stop=True)
                ins = mm(bank[:, b0 + 2, n * P:(n + 1) * P], t.x2[:, h, :], t.x2t[:, h, :], start=True, stop=True)
            done(ins)
        if nxt:
            gates(*nxt)
        for g in "ab":
            b0 = GROUP_BANK[g]
            act("quad_" + g)
            dve("quad_" + g)
            for n, h in enumerate(HEADS[g]):
                s = slice(n * P, (n + 1) * P)
                mm(bank[:, b0, s], t.d1t[:, h, :], t.xp[:, h, 1, :], start=True, stop=True)
                ins = mm(bank[:, b0 + 1, s], t.xp[:, h, 0, :], t.d1t[:, h, :], start=True, stop=True)
            done(ins)
        if nxt:
            turn_v(*nxt)
        for g in "ab":
            b0 = GROUP_BANK[g]
            act("oct_" + g)
            dve("oct_" + g)
            for n, h in enumerate(HEADS[g]):
                ins = mm(bank[:, b0 + 2, n * P:(n + 1) * P], t.d1t[:, h, :], t.d1[:, h, :], start=True, stop=True)
            done(ins)
        if nxt:
            cumsum(*nxt)
        for g in "ab":
            b0 = GROUP_BANK[g]
            dve("dec_" + g)
            for n, h in enumerate(HEADS[g]):
                ins = nc.tensor.transpose(bank[:, b0, n * P:(n + 1) * P], t.x2[:, h, :], const["ident"])
            done(ins)
        for lv in range(3):
            pm, pmt = chain[lv]
            for g in "ab":
                b0 = GROUP_BANK[g]
                if lv == 0:
                    pe.wait_ge(t.core_pool, at(CORE_POOL, "merges_" + g, c))
                else:
                    dve(f"leftT{lv - 1}_{g}")
                for n, h in enumerate(HEADS[g]):
                    m = t.merge[:, lv, h, :] if lv < 2 else t.nmat[:, h, :]
                    ins = mm(bank[:, b0 + 1, n * P:(n + 1) * P], m, pm[:, h, :], start=True, stop=True)
                done(ins)
            if nxt and lv == 0:
                bonus(*nxt)
            for g in "ab":
                b0 = GROUP_BANK[g]
                act(f"join{lv}_{g}")
                for n, h in enumerate(HEADS[g]):
                    s = slice(n * P, (n + 1) * P)
                    ins = mm(bank[:, b0 + 2, s], pmt[:, h, :], q[:, h, :], start=True, stop=True)
                    if lv < 2:
                        ins = mm(bank[:, b0, s], q[:, h, :], pmt[:, h, :], start=True, stop=True)
                done(ins)
        p7 = chain[3][0]
        dve("left2_b")
        for h in range(RH):
            ins = mm(bank[rows(h), 0, (h // 2) * P:(h // 2 + 1) * P], tok["a"][:, h * RN:(h + 1) * RN], p7[:, h, :],
                     start=True, stop=True)
        done(ins)
        for h in range(RH):
            s = slice(h * RN, (h + 1) * RN)
            ins = mm(bank[:, 1, s], t.ak[:, h, :], tok["v"][:, s], start=True, stop=True)
        done(ins)
        if nxt:
            turn_a(*nxt)
        act("keep_w")
        dve("keep_h")
        for h in range(RH):
            o = bank[:, 3 + h % 2, (h // 2) * RN:(h // 2 + 1) * RN]
            mm(o, p7[:, h, :], t.hu[:, h, :], start=True, stop=False)
            ins = mm(o, t.wt[rows(h), h // 2, :], t.entry[rows(h), h // 2, :], start=False, stop=True)
        done(ins)
        if nxt:
            turn_bk(*nxt)
        act("keep_u")
        for h in range(RH):
            o = bank[rows(h), 0, (h // 2) * RN:(h // 2 + 1) * RN]
            s = slice(h * RN, (h + 1) * RN)
            mm(o, tok["k"][:, s], tok["v"][:, s], start=True, stop=False)
            ins = mm(o, tok["b"][:, s], t.hu[:, h, :], start=False, stop=True)
        done(ins)
        for h in range(RH):
            o = bank[rows(h), 1, (h // 2) * P:(h // 2 + 1) * P]
            mm(o, t.entry[rows(h), h // 2, :], ar[rows(h), h // 2, 1, :], start=True, stop=False)
            mm(o, tok["v"][:, h * RN:(h + 1) * RN], t.rk[:, h, :], start=False, stop=False)
            ins = mm(o, t.hu[:, h, :], t.rb[:, h, :], start=False, stop=True)
        done(ins)

    pe.wait_ge(t.loaded, 64)
    pe.wait_ge(t.zeroed, 1)
    pe.sem_inc(t.prep_pe, 1)
    pe.sem_inc(t.core_pe, 1)
    pe.sem_inc(t.close_pe, 1)
    over_chunks(pe, prepare, core, close)


def rwkv_scalar(nc, act, k, t):
    bank, copy, fn = t.bank, nc.scalar.copy, nc.scalar.activation

    def pe_prep(c, name):
        act.wait_ge(t.prep_pe, at(PREP_PE, name, c))

    def done(ins):
        ins.then_inc(t.prep_act, 1)

    def loras(c, b):
        act.wait_ge(t.prep_dve, before(PREP_DVE, c))
        fn(t.lora[0:64, 0, :], t.z[0:64, c, 12, :], ACT.Tanh)
        copy(t.lora[64:128, 0, :], t.z[64:128, c, 12, :])
        copy(t.key[:, :, :], t.z[:, c, 8:12, :])
        done(fn(t.lora[:, 1, :], t.z[:, c, 13, :], ACT.Sigmoid))

    def sigmoids(c, b):
        act.wait_ge(t.prep_dve, at(PREP_DVE, "decay_bias", c))
        done(fn(t.sig_w[:, :], t.sig_w[:, :], ACT.Sigmoid))
        act.wait_ge(t.prep_dve, at(PREP_DVE, "rate_bias", c))
        done(fn(t.rate[:, :, :], t.rate[:, :, :], ACT.Sigmoid))

    def gates(c, b):
        pe_prep(c, "gates")
        if not (isinstance(c, int) and c < 2):
            act.wait_ge(t.close_dve, before(CLOSE_DVE, c - 1))
        done(copy(t.gates[b][:, :, :], t.flat(6)))
        pe_prep(c, "key_norms")
        done(fn(t.t2[:, :, :], t.flat(7), ACT.Sqrt))

    def keep_v(c, b):
        pe_prep(c, "turn_v")
        done(copy(t.tok["v"][b][:, :], bank[:, 6, :]))

    def decays(c, b):
        pe_prep(c, "cumsum")
        cum = bank[:, 6:8, :].rearrange("p b (f w t) -> p (b f) w t", f=2, w=2)
        done(fn(t.bt[b][:, :, :], cum[:, :, 0, :], ACT.Exp, scale=-1.0))
        fn(t.mid[b][:, :], cum[:, :, 1, 0], ACT.Exp, scale=-1.0)
        done(fn(t.last[b][:, :], cum[:, :, 0, P - 1], ACT.Exp))
        fn(t.ar[b][:, :, 0, :], cum[:, :, 1, :], ACT.Exp)
        done(fn(t.ar[b][:, :, 1, :], cum[:, :, 0, :], ACT.Exp))

    def bonus(c, b):
        pe_prep(c, "bonus")
        done(copy(t.bonus[b][:, :, :], t.flat(6)))

    def keep_a(c, b):
        pe_prep(c, "turn_a")
        done(copy(t.tok["a"][b][:, :], bank[:, 7, :]))

    def keep_bk(c, b):
        pe_prep(c, "turn_b")
        done(copy(t.tok["b"][b][:, :], bank[:, 6, :]))
        pe_prep(c, "turn_k")
        done(copy(t.tok["k"][b][:, :], bank[:, 7, :]))

    def prepare(c, b):
        for stage in (loras, sigmoids, gates, keep_v, decays, bonus, keep_a, keep_bk):
            stage(c, b)

    def squares(c, b):
        act.wait_ge(t.close_dve, at(CLOSE_DVE, "centred", c))
        fn(t.ysq[:, :, :], t.y[:, :, :], ACT.Square).then_inc(t.close_act, 1)

    def roots(c, b):
        act.wait_ge(t.close_pe, at(CLOSE_PE, "variances", c))
        fn(t.yroot[:, :, :], t.flat(7), ACT.Sqrt, scale=1.0 / RN, bias=k.eps[:, 2:3]).then_inc(t.close_act, 1)

    def close(c, b):
        squares(c, b)
        roots(c, b)

    def core(c, b, nxt, prev):
        chain, q = merge_chain(t)

        def pe(name):
            act.wait_ge(t.core_pe, at(CORE_PE, name, c))

        def done(ins):
            ins.then_inc(t.core_act, 1)

        pe("gram_n")
        done(copy(t.nmat[:, :, :].rearrange("p (n e) t -> p e n t", e=2),
                  bank[:, 4:6, :].rearrange("p e (n t) -> p e n t", t=P)))
        if nxt:
            loras(*nxt)
        if prev:
            squares(*prev)
            roots(*prev)
        for g in "ab":
            b0 = GROUP_BANK[g]
            pe("sq_" + g)
            copy(t.xp[:, HS[g], 0, :], t.flat(b0))
            copy(t.x2[:, HS[g], :], t.flat(b0))
            done(copy(t.x2t[:, HS[g], :], t.flat(b0 + 2)))
        if nxt:
            sigmoids(*nxt)
        for g in "ab":
            b0 = GROUP_BANK[g]
            pe("quad_" + g)
            quad = bank[:, b0:b0 + 2, :].rearrange("p b (f w t) -> p (b f) w t", f=2, w=2)
            copy(t.xp[:, HS[g], 0, :], quad[:, :, 0, :])
            done(copy(t.d1t[:, HS[g], :], t.flat(b0 + 2)))
        if nxt:
            gates(*nxt)
        for g in "ab":
            pe("oct_" + g)
            done(copy(t.d1t[:, HS[g], :], t.flat(GROUP_BANK[g] + 1)))
        if nxt:
            keep_v(*nxt)
            decays(*nxt)
        for g in "ab":
            pe("turn_" + g)
            done(copy(t.x2t[:, HS[g], :], t.flat(GROUP_BANK[g])))
        for lv in range(3):
            for g in "ab":
                pe(f"join{lv}_{g}")
                done(copy(q[:, HS[g], :], t.flat(GROUP_BANK[g] + 1)))
            if nxt and lv == 0:
                bonus(*nxt)
        pe("removal")
        done(copy(t.wt[:, :, :], t.flat(0)))
        if nxt:
            keep_a(*nxt)
        pe("removed")
        done(copy(t.hu[:, :, :].rearrange("p (n e) i -> p e n i", e=2),
                  bank[:, 3:5, 0:RT * RN].rearrange("p e (n i) -> p e n i", i=RN)))
        if nxt:
            keep_bk(*nxt)
        pe("outputs")
        act.wait_ge(t.close_dve, before(CLOSE_DVE, c))
        done(copy(t.y[:, :, :], t.flat(1)))

    act.sem_inc(t.prep_act, 1)
    act.sem_inc(t.core_act, 1)
    act.sem_inc(t.close_act, 1)
    over_chunks(act, prepare, core, close)


def rwkv_gpsimd(nc, pool, k, t):
    tt, const = nc.gpsimd.tensor_tensor, k.const

    def core(c, b, nxt, prev):
        def done(ins):
            ins.then_inc(t.core_pool, 1)

        pool.wait_ge(t.core_act, at(CORE_ACT, "keep_n", c))
        for g, last_pair in (("a", "gram1"), ("b", "gram3")):
            done(tt(t.d1t[:, HS[g], :], t.nmat[:, HS[g], :], masks(const["diag_lo"], 4), ALU.mult))
            pool.wait_ge(t.core_dve, at(CORE_DVE, last_pair, c))
            done(tt(t.xp[:, HS[g], 1, :], t.d1[:, HS[g], :], masks(const["ident"], 4), ALU.add))
        for g in "ab":
            tt(t.merge[:, 0, HS[g], :], t.nmat[:, HS[g], :], masks(const["merge16"], 4), ALU.mult)
            tt(t.merge[:, 1, HS[g], :], t.nmat[:, HS[g], :], masks(const["merge32"], 4), ALU.mult)
            done(tt(t.nmat[:, HS[g], :], t.nmat[:, HS[g], :], masks(const["merge64"], 4), ALU.mult))

    pool.sem_inc(t.core_pool, 1)
    over_chunks(pool, lambda c, b: None, core, lambda c, b: None)


def rwkv_vector(nc, dve, k, t):
    tt, stt, recip = nc.vector.tensor_tensor, nc.vector.scalar_tensor_tensor, nc.vector.reciprocal
    bank, par, const = t.bank, k.par, k.const

    def own(c, name):
        dve.wait_ge(t.prep_dve, at(PREP_DVE, name, c))

    def act_prep(c, name):
        dve.wait_ge(t.prep_act, at(PREP_ACT, name, c))

    def done(ins):
        ins.then_inc(t.prep_dve, 1)

    def squares(c, b):
        done(tt(t.kk[:, :, :], t.z[:, c, 4:8, :], wide(par["rwkv_k_k"], P), ALU.mult))
        own(c, "raw_kk")
        done(tt(t.t1[:, :, :], t.kk[:, :, :], t.kk[:, :, :], ALU.mult))

    def biases(c, b):
        dve.wait_ge(t.prep_pe, at(PREP_PE, "decay_logits", c))
        done(tt(t.sig_w[:, :], bank[:, 6, :], t.w0[:, :], ALU.add))
        dve.wait_ge(t.prep_pe, at(PREP_PE, "rate_logits", c))
        done(tt(t.rate[:, :, :], t.flat(7), wide(par["rwkv_a0"], P), ALU.add))

    def keys(c, b):
        k_in = t.z[:, c, 4:8, :]
        act_prep(c, "key_roots")
        done(nc.vector.tensor_scalar(t.t2[:, :, :], t.t2[:, :, :], 1e-12, None, ALU.max))
        own(c, "root_max")
        done(recip(t.t2[:, :, :], t.t2[:, :, :]))
        own(c, "inv_norm")
        done(tt(t.kk[:, :, :], t.kk[:, :, :], t.t2[:, :, :], ALU.mult))
        dve.wait_ge(t.prep_pe, at(PREP_PE, "turn_v", c))
        done(stt(out=t.key[:, :, :], in0=t.rate[:, :, :], scalar=-1.0, in1=k_in, op0=ALU.add, op1=ALU.mult))
        own(c, "rate_k")
        done(tt(t.key[:, :, :], t.key[:, :, :], wide(par["rwkv_k_a"], P), ALU.mult))
        own(c, "k_gain")
        done(tt(t.key[:, :, :], t.key[:, :, :], k_in, ALU.add))
        own(c, "key")
        done(tt(t.rate[:, :, :], t.rate[:, :, :], t.kk[:, :, :], ALU.mult))
        done(tt(t.t2[:, :, :], t.key[:, :, :], t.z[:, c, 0:4, :], ALU.mult))
        own(c, "key_r")
        done(tt(t.t1[:, :, :], t.t2[:, :, :], wide(par["rwkv_r_k"], P), ALU.mult))

    def decays(c, b):
        ar, bt, kt = t.ar[b], t.bt[b], t.kt[b]
        act_prep(c, "up")
        done(tt(kt[:, :, :], t.key[:, :, :], bt[:, :, :], ALU.mult))
        tt(bt[:, :, :], t.rate[:, :, :], bt[:, :, :], ALU.mult)
        stt(out=ar[:, :, 0, :], in0=t.kk[:, :, :], scalar=-1.0, in1=ar[:, :, 0, :], op0=ALU.mult, op1=ALU.mult)
        done(tt(ar[:, :, 1, :], t.z[:, c, 0:4, :], ar[:, :, 1, :], ALU.mult))

    def prepare(c, b):
        for stage in (squares, biases, keys, decays):
            stage(c, b)

    def centre(c, b):
        dve.wait_ge(t.close_pe, at(CLOSE_PE, "means", c))
        stt(out=t.y[:, :, :], in0=t.flat(6), scalar=-1.0 / RN, in1=t.y[:, :, :], op0=ALU.mult,
            op1=ALU.add).then_inc(t.close_dve, 1)

    def finish_y(c, b):
        def own(name):
            dve.wait_ge(t.close_dve, at(CLOSE_DVE, name, c))

        def done(ins):
            ins.then_inc(t.close_dve, 1)

        y = t.y[:, :, :]
        dve.wait_ge(t.close_act, at(CLOSE_ACT, "roots", c))
        done(recip(t.yroot[:, :, :], t.yroot[:, :, :]))
        own("inv_std")
        done(tt(y, y, t.yroot[:, :, :], ALU.mult))
        own("normed")
        done(tt(y, y, wide(par["rwkv_ln_g"], P), ALU.mult))
        done(tt(t.bonus[b][:, :, :], t.bonus[b][:, :, :], t.z[:, c, 8:12, :], ALU.mult))
        own("bonus_v")
        done(tt(y, y, wide(par["rwkv_ln_b"], P), ALU.add))
        own("with_bias")
        done(tt(y, y, t.bonus[b][:, :, :], ALU.add))
        own("with_bonus")
        done(tt(t.z[:, c, 0:4, :], y, t.gates[b][:, :, :], ALU.mult))

    def close(c, b):
        centre(c, b)
        finish_y(c, b)

    def core(c, b, nxt, prev):
        chain, _ = merge_chain(t)

        def pe(name):
            dve.wait_ge(t.core_pe, at(CORE_PE, name, c))

        def done(ins):
            ins.then_inc(t.core_dve, 1)

        if prev:
            centre(*prev)
        for n in range(RH // 2):
            pe(f"gram{n}")
            b0 = 2 * n % 6
            done(tt(t.gm[:, 2 * n:2 * n + 2, :, :].rearrange("p h w t -> p h (w t)"), bank[:, b0:b0 + 2, :],
                    masks(k.gram_masks, 2), ALU.mult))
        if nxt:
            squares(*nxt)
        if prev:
            finish_y(*prev)
        if nxt:
            biases(*nxt)
        for g in "ab":
            dve.wait_ge(t.core_act, at(CORE_ACT, "quad_" + g, c))
            b0 = GROUP_BANK[g]
            quad = bank[:, b0:b0 + 2, :].rearrange("p b (f w t) -> p (b f) w t", f=2, w=2)
            done(tt(t.xp[:, HS[g], 1, :], quad[:, :, 1, :], t.xp[:, HS[g], 1, :], ALU.add))
        for g in "ab":
            pe("oct_" + g)
            done(tt(t.d1[:, HS[g], :], t.flat(GROUP_BANK[g]), t.xp[:, HS[g], 1, :], ALU.add))
        for g in "ab":
            pe("dec_" + g)
            done(tt(t.x2[:, HS[g], :], t.flat(GROUP_BANK[g] + 2), t.d1[:, HS[g], :], ALU.add))
        if nxt:
            keys(*nxt)
        for lv in range(3):
            (pm, pmt), (pn, pnt) = chain[lv], chain[lv + 1]
            if lv == 2:
                dve.wait_ge(t.core_dve, before(CORE_DVE, c))
                done(tt(t.entry[:, :, :], t.state[:, :, :], wide(t.mid[b][:, :], RN), ALU.mult))
            for g in "ab":
                pe(f"left{lv}_{g}")
                done(tt(pn[:, HS[g], :], t.flat(GROUP_BANK[g] + 2), pm[:, HS[g], :], ALU.add))
                if lv < 2:
                    done(tt(pnt[:, HS[g], :], t.flat(GROUP_BANK[g]), pmt[:, HS[g], :], ALU.add))
            if nxt and lv == 0:
                decays(*nxt)
        pe("chunk_h")
        done(nc.vector.tensor_copy(t.hu[:, :, :].rearrange("p h n -> p (h n)"), bank[:, 1, :]))
        pe("state")
        done(tt(t.state[:, :, :], t.entry[:, :, :], bank[:, 0, 0:RT * RN].rearrange("p (f n) -> p f n", n=RN), ALU.add))
        dve.wait_ge(t.core_dve, at(CORE_DVE, "state_sum", c))
        done(tt(t.state[:, :, :], t.state[:, :, :], wide(t.last[b][:, :], RN), ALU.mult))

    nc.vector.memset(t.state[:, :, :], 0.0)
    nc.vector.memset(t.a2[0:64, :], 0.0)
    nc.vector.memset(t.w2[64:128, :], 0.0).then_inc(t.zeroed, 1)
    dve.wait_ge(t.zeroed, 1)
    dve.wait_ge(t.loaded, 64)
    dve.sem_inc(t.prep_dve, 1)
    dve.sem_inc(t.core_dve, 1)
    dve.sem_inc(t.close_dve, 1)
    over_chunks(dve, prepare, core, close)


def rwkv(nc, k, z, w2, a2, g2, w0):
    with ExitStack() as ctx:
        t = RwkvTiles(nc, ctx, z)
        with nc.Block() as block:
            @block.sync
            def _(sp):
                sp.dma_start(t.w2[0:64, :], w2).then_inc(t.loaded, 16)
                sp.dma_start(t.a2[64:128, :], a2).then_inc(t.loaded, 16)
                sp.dma_start(t.g2[:, :], g2).then_inc(t.loaded, 16)
                sp.dma_start(t.w0[:, :], w0.to_broadcast([P, HALF])).then_inc(t.loaded, 16)

            @block.tensor
            def _(pe):
                rwkv_tensor(nc, pe, k, t)

            @block.scalar
            def _(act):
                rwkv_scalar(nc, act, k, t)

            @block.gpsimd
            def _(pool):
                rwkv_gpsimd(nc, pool, k, t)

            @block.vector
            def _(dve):
                rwkv_vector(nc, dve, k, t)


def block_kernel(nc, x, mem, w_in, gla_wa2, rwkv_w2, rwkv_a2, rwkv_g2, w_out, wq_mem, wkv_mem, wo_mem, w_gate_up,
                 w_down, consts, params, rows, out):
    k = Kept()
    n_par = sum(n for _, n in PARAMS)
    n_row = sum(n for _, n in ROWS)
    keep = ExitStack()

    def hold(stack, name, shape, side="left"):
        return stack.enter_context(nc.sbuf_tensor(name, shape, F32, side=side))

    with keep:
        con = hold(keep, "consts", [P, len(CONSTS) * P])
        par = hold(keep, "params", [P, n_par])
        row = hold(keep, "rows", [1, n_row])
        k.cum_w = hold(keep, "cum_w", [P, 2 * P])
        k.eps = hold(keep, "eps", [P, 3])
        for n, name in enumerate(CONSTS):
            k.const[name] = con[:, n * P:(n + 1) * P]
        first = CONSTS.index("cum_in") * P
        k.cum = con[:, first:first + 2 * P]
        first = CONSTS.index("diag_up") * P
        k.gram_masks = con[:, first:first + 4 * P]
        k.ones_row = k.const["ones"][0:1, :]
        at_col = 0
        for name, n in PARAMS:
            k.par[name] = par[:, at_col:at_col + n]
            at_col += n
        at_col = 0
        for name, n in ROWS:
            k.row[name] = row[0:1, at_col:at_col + n]
            at_col += n
        loaded = keep.enter_context(nc.semaphore("consts_loaded"))
        with nc.Block() as block:
            @block.sync
            def _(sp):
                sp.dma_start(con[:, :], consts).then_inc(loaded, 16)
                sp.dma_start(par[:, :], params).then_inc(loaded, 16)
                sp.dma_start(row[:, :], rows).then_inc(loaded, 16)

            @block.vector
            def _(dve):
                for n, e in enumerate((EPS, G_EPS, R_EPS)):
                    nc.vector.memset(k.eps[:, n:n + 1], e)

            @block.scalar
            def _(act):
                act.wait_ge(loaded, 48)
                nc.scalar.mul(k.cum_w[:, :], k.cum, -float(np.exp(-0.5)))

        def parts(stack, name, n, side="left"):
            return tuple(stack.enter_context(nc.sbuf_tensor(f"{name}_{p}", [P, n, T], F32R, side=side))
                         for p in ("hi", "lo"))

        def moving(pair):
            return lambda kt, h: tuple(x[:, kt, h * HALF:(h + 1) * HALF] for x in pair)

        early = ExitStack()
        h_stack = ExitStack()
        og = hold(early, "og", [P, GH, T])
        h = parts(h_stack, "h", KD, "right")
        with ExitStack() as st:
            x_first = hold(st, "x_first", [P, KD, T])
            transpose_in(nc, k, "x_in", x, x_first, T)
            rms_norm(nc, k, "norm_mix", x_first, h, k.par["norm_mix_g"], T)

        with ExitStack() as gl:
            gz = hold(gl, "gla_z", [P, 9, T])
            vtok = hold(gl, "gla_v", [P, NC, GH * GV])
            dense(nc, "proj_gla", [(4, w_in[:, 0:512]), (5, w_in[:, 1024:1536 + P])], moving(h), KD, copy_out(nc, gz, 9))
            token_major(nc, "proj_v", h, KD, w_in[:, 512:1024], vtok, T, GH * GV)
            gla(nc, k, gz[:, 0:2, :], gz[:, 2:4, :], gz[:, 4:8, :], gz[0:RANK, 8, :], vtok, gla_wa2, og)

        z = hold(early, "rwkv_z", [P, R_TILES, T])
        dense(nc, "proj_rwkv", [(R_TILES, w_in[:, G_COLS:])], moving(h), KD, shift_mix_out(nc, z, k.par["rwkv_mu"]))
        h_stack.close()
        rwkv(nc, k, z, rwkv_w2, rwkv_a2, rwkv_g2, rows[:, GH * GK:])

        late = ExitStack()
        xT = hold(late, "xT", [P, KD, T], "right")
        with ExitStack() as st:
            mix = parts(st, "mix", KD)
            halves_of = [og[:, n, :] for n in range(GH)] + [z[:, n, :] for n in range(RT)]
            transpose_in(nc, k, "x_again", x, xT, T,
                         [(v, mix[0][:, n, :], mix[1][:, n, :]) for n, v in enumerate(halves_of)])
            dense(nc, "proj_out", [(KD, w_out)], moving(mix), KD, add_out(nc, xT))
        early.close()

        with ExitStack() as st:
            kT = hold(st, "mem_k", [P, KD, M])
            vm = hold(st, "mem_v", [P, M // P, D])
            with ExitStack() as s2:
                mT = hold(s2, "memT", [P, KD, M])
                mh = hold(s2, "mem_h", [P, KD, M])
                transpose_in(nc, k, "mem_in", mem, mT, M)
                rms_norm(nc, k, "norm_mem", mT, mh, k.par["norm_mem_g"], M)
                memory_keys(nc, "mem_keys", wkv_mem[:, 0:D], mh, kT)
                token_major(nc, "mem_values", mh, KD, wkv_mem[:, D:2 * D], vm, M, D)
            q_sb = hold(st, "q_sb", [P, KD, T])
            a = parts(st, "attn_io", KD)
            rms_norm(nc, k, "norm_mem_x", xT, a, k.par["norm_mem_x_g"], T)
            dense(nc, "proj_q", [(KD, wq_mem)], moving(a), KD, copy_out(nc, q_sb, KD))
            attention(nc, k, q_sb, kT, vm, a)
            dense(nc, "proj_o", [(KD, wo_mem)], moving(a), KD, add_out(nc, xT))

        clear_semaphores(nc, PAST)
        with ExitStack() as st:
            f = parts(st, "ffn_h", KD)
            rms_norm(nc, k, "norm_ffn", xT, f, k.par["norm_ffn_g"], T)
            first = 0
            for n, width in enumerate(FF_GROUPS):
                with ExitStack() as s2:
                    hidden = parts(s2, f"ffn_act{n}", width)
                    cols = slice(first * P, (first + width) * P)
                    dense(nc, f"gate_up{n}", [(2 * width, (w_gate_up, first))], moving(f), KD,
                          gate_out(nc, *hidden))
                    dense(nc, f"down{n}", [(KD, w_down[cols, :])], moving(hidden), width, add_out(nc, xT))
                first += width
        with ExitStack() as st:
            yT = hold(st, "yT", [P, KD, T])
            rms_norm(nc, k, "norm_final", xT, yT, k.par["norm_final_g"], T)
            finish(nc, k, "store", yT, out)
        late.close()


def memory_keys(nc, name, w_dram, src, dst):
    with ExitStack() as ctx:
        sb, ps, sem = tiles(nc, ctx, name)
        w = sb("w", [P, 2, KD, HALF])
        bank = ps("bank", [P, 2, HALF])
        landed = [sem("landed0"), sem("landed1")]
        ready, copied = sem("ready"), sem("copied")
        cols = w_dram.rearrange("(kt p) (b f) -> b p kt f", p=P, f=HALF)
        with nc.Block() as block:
            @block.sync
            def _(sp):
                for b in range(2):
                    sp.dma_start(w[:, b], cols[b]).then_inc(landed[b], 16)

            @block.tensor
            def _(pe):
                for f in range(KD):
                    b, s = f // 4, slice((f % 4) * P, (f % 4 + 1) * P)
                    pe.wait_ge(landed[b], 16)
                    if f >= 2:
                        pe.wait_ge(copied, f - 1)
                    for kt in range(KD):
                        mm = nc.tensor.matmul(bank[:, f % 2, 0:M], w[:, b, kt, s], src[:, kt, :],
                                              start=(kt == 0), stop=(kt == KD - 1))
                    mm.then_inc(ready, 1)

            @block.vector
            def _(dve):
                for f in range(KD):
                    dve.wait_ge(ready, f + 1)
                    nc.vector.tensor_copy(dst[:, f, :], bank[:, f % 2, 0:M]).then_inc(copied, 1)


def attention(nc, k, q_sb, kT, vm, o_sb):
    scale = float(AD) ** -0.5
    pe_steps = ("scores", "turned", "outputs")
    act_steps = ("q_copied", "exp", "p_copied", "o_copied")
    dve_steps = ("max", "neg_max", "inverse", "probs", "o_rest")
    with ExitStack() as ctx:
        sb, ps, sem = tiles(nc, ctx, "attn")
        q_c = sb("q_c", [P, KD, P])
        top, bias, total, inv = (sb(n, [P, AH]) for n in ("top", "bias", "total", "inv"))
        e = sb("e", [P, AH, M])
        pT = sb("pT", [P, AH, 2, P])
        bank = ps("bank", [P, 6, HALF])
        pe_done, act_done, dve_done = sem("pe_done"), sem("act_done"), sem("dve_done")
        cq = q_sb[:, :, :].rearrange("p f (c t) -> p c f t", t=P)
        co, co_lo = (x[:, :, :].rearrange("p f (c t) -> p c f t", t=P) for x in o_sb)
        s_ps = bank[:, 0:2, :].rearrange("p b (h m) -> p (b h) m", m=M)
        with nc.Block() as block:
            @block.tensor
            def _(pe):
                pe.sem_inc(pe_done, 1)
                with pe.Fori(0, NC) as c:
                    pe.wait_ge(act_done, at(act_steps, "q_copied", c))
                    for h in range(AH):
                        for d in range(2):
                            mm = nc.tensor.matmul(bank[:, h // 2, (h % 2) * M:(h % 2 + 1) * M], q_c[:, 2 * h + d, :],
                                                  kT[:, 2 * h + d, :], start=(d == 0), stop=(d == 1))
                    mm.then_inc(pe_done, 1)
                    pe.wait_ge(dve_done, at(dve_steps, "probs", c))
                    for h in range(AH):
                        for m in range(2):
                            mm = nc.tensor.transpose(bank[:, 2 + h // 2, ((h % 2) * 2 + m) * P:((h % 2) * 2 + m + 1) * P],
                                                     e[:, h, m * P:(m + 1) * P], k.const["ident"])
                    mm.then_inc(pe_done, 1)
                    pe.wait_ge(act_done, at(act_steps, "p_copied", c))
                    pe.wait_ge(dve_done, before(dve_steps, c))
                    for f in range(KD):
                        for m in range(2):
                            mm = nc.tensor.matmul(bank[:, 4 + f // 4, (f % 4) * P:(f % 4 + 1) * P],
                                                  vm[:, m, f * P:(f + 1) * P], pT[:, f // 2, m, :],
                                                  start=(m == 0), stop=(m == 1))
                    mm.then_inc(pe_done, 1)

            @block.scalar
            def _(act):
                act.sem_inc(act_done, 1)
                with act.Fori(0, NC) as c:
                    act.wait_ge(pe_done, before(pe_steps, c))
                    nc.scalar.copy(q_c[:, :, :], cq[:, c, :, :]).then_inc(act_done, 1)
                    act.wait_ge(dve_done, at(dve_steps, "neg_max", c))
                    for h in range(AH):
                        mm = nc.scalar.activation(e[:, h, :], s_ps[:, h, :], ACT.Exp, bias=bias[:, h:h + 1],
                                                  scale=scale, accum_out=total[:, h:h + 1])
                    mm.then_inc(act_done, 1)
                    act.wait_ge(pe_done, at(pe_steps, "turned", c))
                    nc.scalar.copy(pT[:, :, :, :].rearrange("p h m t -> p (h m t)"),
                                   bank[:, 2:4, :].rearrange("p b t -> p (b t)")).then_inc(act_done, 1)
                    act.wait_ge(pe_done, at(pe_steps, "outputs", c))
                    nc.scalar.copy(co[:, c, :, :], bank[:, 4:6, :].rearrange("p b (f t) -> p (b f) t", t=P))\
                        .then_inc(act_done, 1)

            @block.vector
            def _(dve):
                dve.sem_inc(dve_done, 1)
                with dve.Fori(0, NC) as c:
                    dve.wait_ge(pe_done, at(pe_steps, "scores", c))
                    nc.vector.tensor_reduce(top[:, :], s_ps, mybir.AxisListType.X, ALU.max).then_inc(dve_done, 1)
                    dve.wait_ge(dve_done, at(dve_steps, "max", c))
                    nc.vector.tensor_scalar(bias[:, :], top[:, :], -scale, None, ALU.mult).then_inc(dve_done, 1)
                    dve.wait_ge(act_done, at(act_steps, "exp", c))
                    nc.vector.reciprocal(inv[:, :], total[:, :]).then_inc(dve_done, 1)
                    dve.wait_ge(dve_done, at(dve_steps, "inverse", c))
                    nc.vector.tensor_tensor(e[:, :, :], e[:, :, :], wide(inv[:, :], M), ALU.mult).then_inc(dve_done, 1)
                    dve.wait_ge(act_done, at(act_steps, "o_copied", c))
                    nc.vector.tensor_tensor(co_lo[:, c, :, :], bank[:, 4:6, :].rearrange("p b (f t) -> p (b f) t", t=P),
                                            co[:, c, :, :].bitcast(F32), ALU.subtract).then_inc(dve_done, 1)


WEIGHTS = ["w_in", "gla_wa2", "rwkv_w2", "rwkv_a2", "rwkv_g2", "w_out", "wq_mem", "wkv_mem", "wo_mem", "w_gate_up",
           "w_down"]


def kernel(**inputs):
    import concourse.bacc as bacc
    from concourse.bass_utils import run_bass_kernel_spmd

    nc = bacc.Bacc("TRN2", target_bir_lowering=False, num_devices=1)
    a = {name: np.ascontiguousarray(value) for name, value in inputs.items()}
    arrays = {"x": a["x"][0], "mem": a["mem"][0]}
    arrays.update({name: a[name][0] for name in WEIGHTS})
    arrays["consts"] = constants()
    arrays["params"] = np.concatenate([a[name].reshape(n, P).T for name, n in PARAMS], axis=1)
    arrays["rows"] = np.concatenate([a[name].reshape(1, n) for name, n in ROWS], axis=1)
    arrays = {name: np.ascontiguousarray(value) for name, value in arrays.items()}
    args = [nc.dram_tensor(f"in_{name}", value.shape, F32, kind="ExternalInput").ap()
            for name, value in arrays.items()]
    args.append(nc.dram_tensor("out_0", (T, D), F32, kind="ExternalOutput").ap())
    block_kernel(nc, *args)
    r = run_bass_kernel_spmd(nc, [{f"in_{name}": value for name, value in arrays.items()}], core_ids=[0])
    return r.results[0]["out_0"].reshape(1, T, D)
```

```python
from contextlib import ExitStack

import numpy as np

import concourse.bass as bass
from concourse import mybir

F32 = mybir.dt.float32
F32R = mybir.dt.float32r
ALU = mybir.AluOpType
ACT = mybir.ActivationFunctionType

P = 128
D = 1024
KD = D // P
T = 1024
NC = T // P
HALF = 512
NH = T // HALF
M = 256
EPS = 1e-6
GH, GK, GV = 4, 64, 128
G_EPS = 1e-5
RANK = 16
G_COLS = 1552
RH, RN = 8, 64
RT = RH * RN // P
R_EPS = 64e-5
R_TILES = 14
AH, AD = 4, 256
FF = 2816
FT = FF // P
FF_GROUPS = (8, 8, 6)

MERGES = (2, 4, 8, 16, 32, 64)
CONSTS = ["ident", "ones", "pair_ones", "cum_in", "cum_ex", "diag_up", "up_incl", "up_strict",
          "up_incl_2"] + [f"merge{n}" for n in MERGES]
PARAMS = [("norm_mix_g", KD), ("norm_mem_x_g", KD), ("norm_mem_g", KD), ("norm_ffn_g", KD),
          ("norm_final_g", KD), ("gla_norm_g", 1), ("rwkv_mu", R_TILES), ("rwkv_k_k", RT),
          ("rwkv_k_a", RT), ("rwkv_a0", RT), ("rwkv_r_k", RT), ("rwkv_ln_g", RT), ("rwkv_ln_b", RT)]
ROWS = [("gla_ba", GH * GK), ("rwkv_w0", RH * RN)]


class Kept:

    def __init__(self):
        self.const, self.par, self.row = {}, {}, {}


def constants():
    s = np.arange(P)[:, None]
    t = np.arange(P)[None, :]
    mid = s <= P // 2 - 1
    same = lambda n: s // n == t // n
    return np.concatenate([np.asarray(m, np.float32) for m in (
        s == t, np.ones((P, P)), same(RN),
        (s <= t) * 1.0 - mid, (s < t) * 1.0 - mid,
        (s < t) & same(2), s <= t, s < t, s <= t,
        *((s > t) & same(2 * n) & ~same(n) for n in MERGES))], axis=1)


def at(steps, name, turn):
    return turn * len(steps) + steps.index(name) + 2


def before(steps, turn):
    return turn * len(steps) + 1


PAST = []


def tiles(nc, ctx, prefix):
    def sb(name, shape):
        return ctx.enter_context(nc.sbuf_tensor(f"{prefix}_{name}", shape, F32))

    def ps(name, shape):
        return ctx.enter_context(nc.psum_tensor(f"{prefix}_{name}", shape, F32))

    def sem(name):
        s = ctx.enter_context(nc.semaphore(f"{prefix}_{name}"))
        PAST.append(s)
        return s
    return sb, ps, sem


def clear_semaphores(nc, used):
    with nc.Block() as block:
        @block.sync
        def _(sp):
            for s in used:
                sp.sem_clear(s)
    used.clear()


def wide(scalars, n):
    return scalars.unsqueeze(2).to_broadcast([scalars.shape[0], scalars.shape[1], n])


def split_tiles(nc, name, tiles_of, weights):
    with ExitStack() as ctx:
        _, _, sem = tiles(nc, ctx, name)
        rounded = sem("rounded")
        with nc.Block() as block:
            @block.sync
            def _(sp):
                weights.start_loading(sp)

            @block.scalar
            def _(act):
                for n, (x, hi, _) in enumerate(tiles_of):
                    if n == len(tiles_of) // 2:
                        weights.start_rounding(act)
                    nc.scalar.copy(hi, x).then_inc(rounded, 1)

            def rest(eng, engine, which):
                for n in which:
                    x, hi, lo = tiles_of[n]
                    eng.wait_ge(rounded, n + 1)
                    engine.tensor_tensor(lo, x, hi.bitcast(F32), ALU.subtract)

            @block.vector
            def _(dve):
                rest(dve, nc.vector, range(2, len(tiles_of)))

            @block.gpsimd
            def _(pool):
                rest(pool, nc.gpsimd, range(0, 2))
                weights.start_splitting(pool)


def first_norm(nc, k, name, src, gain, parts, rstd, rstd_tok, room, weights):
    nt = src.shape[0] // P
    rows = src.rearrange("(c p) f -> c p f", p=P)
    hi, lo = parts
    with ExitStack() as ctx:
        sb, ps, sem = tiles(nc, ctx, name)
        tok, sq = room[:, 0:3, :], room[:, 3, :]
        full = room[:, 4:6, :].rearrange("p u (f t) -> p u f t", t=P)
        total, root = sb("total", [P, nt]), sb("root", [P, nt])
        diag = room[:, 6, 0:nt * P].rearrange("p (c t) -> p c t", t=P)
        bank = ps("bank", [P, 2, KD, P])
        spread = ps("spread", [P, nt, P])
        landed = [sem(f"landed{n}") for n in range(3)]
        turned, gained, rounded, split = sem("turned"), sem("gained"), sem("rounded"), sem("split")
        squared, rooted, inverted, diagonal, summed = (sem(n) for n in ("squared", "rooted", "inverted", "diagonal",
                                                                        "summed"))
        chunk = lambda x, c: x[:, :, c * P:(c + 1) * P]
        with nc.Block() as block:
            @block.sync
            def _(sp):
                for c in range(nt):
                    if c >= 3:
                        sp.wait_ge(turned, c - 2)
                        sp.wait_ge(squared, c - 2)
                    sp.dma_start(tok[:, c % 3, :], rows[c]).then_inc(landed[c % 3], 16)
                    if c == min(4, nt - 1):
                        weights.start_loading(sp)

            @block.tensor
            def _(pe):
                for c in range(nt):
                    pe.wait_ge(landed[c % 3], 16 * (c // 3 + 1))
                    if c >= 2:
                        pe.wait_ge(gained, c - 1)
                    for f in range(KD):
                        mm = nc.tensor.transpose(bank[:, c % 2, f, :], tok[:, c % 3, f * P:(f + 1) * P],
                                                 k.const["ident"])
                    mm.then_inc(turned, 1)
                pe.wait_ge(diagonal, 1)
                for c in range(nt):
                    mm = nc.tensor.matmul(spread[:, c, :], k.const["ones"], diag[:, c, :], start=True, stop=True)
                mm.then_inc(summed, 1)

            @block.scalar
            def _(act):
                for c in range(nt):
                    act.wait_ge(landed[c % 3], 16 * (c // 3 + 1))
                    if c:
                        act.wait_ge(squared, c)
                    nc.scalar.activation(sq, tok[:, c % 3, :], ACT.Square,
                                         accum_out=total[:, c:c + 1]).then_inc(squared, 1)
                    act.wait_ge(gained, c + 1)
                    nc.scalar.copy(chunk(hi, c), full[:, c % 2]).then_inc(rounded, 1)
                act.wait_ge(squared, nt)
                nc.scalar.activation(root[:, :], total[:, :], ACT.Sqrt, scale=1.0 / D,
                                     bias=k.eps[:, 0:1]).then_inc(rooted, 1)
                weights.start_rounding(act)

            @block.gpsimd
            def _(pool):
                for c in range(nt):
                    pool.wait_ge(rounded, c + 1)
                    nc.gpsimd.tensor_tensor(chunk(lo, c), full[:, c % 2], chunk(hi, c).bitcast(F32),
                                            ALU.subtract).then_inc(split, 1)
                weights.start_splitting(pool)

            @block.vector
            def _(dve):
                for c in range(nt):
                    dve.wait_ge(turned, c + 1)
                    if c >= 2:
                        dve.wait_ge(split, c - 1)
                    nc.vector.tensor_tensor(full[:, c % 2], bank[:, c % 2], wide(gain, P),
                                            ALU.mult).then_inc(gained, 1)
                dve.wait_ge(rooted, 1)
                nc.vector.reciprocal(rstd_tok[:, :], root[:, :]).then_inc(inverted, 1)
                dve.wait_ge(inverted, 1)
                nc.vector.tensor_tensor(diag[:, :, :], k.const["ident"].unsqueeze(1).to_broadcast([P, nt, P]),
                                        wide(rstd_tok[:, :], P), ALU.mult).then_inc(diagonal, 1)
                dve.wait_ge(summed, 1)
                nc.vector.tensor_copy(rstd[:, :], spread[:, :, :].rearrange("p c t -> p (c t)"))


def turns(eng, n, body, first=0):
    if first:
        body(0, 1)
    with eng.Fori(first, n // 2) as i:
        body(i, 0)
        body(i, 1)
    if n % 2:
        body(n // 2, 0)


def weight_tiles(view, n):
    if isinstance(view, tuple):
        m, f0 = view
        even = m.rearrange("(kt p) (u i f) -> u i p kt f", p=P, u=2, f=P)[:, f0:f0 + n // 2]
        return lambda i, u: even[u, i]
    cols = view.rearrange("(kt p) (s f) -> s p kt f", p=P, f=P)
    even = cols[0:n // 2 * 2].rearrange("(i u) p kt f -> u i p kt f", u=2)
    return lambda i, u: cols[2 * i] if isinstance(i, int) and n % 2 and 2 * i + u == n - 1 else even[u, i]


class Job:

    def __init__(self, views, src, drain, tile_ready=None, norm=None, residual=None, halves=NH):
        self.views, self.src, self.drain, self.tile_ready, self.norm = views, src, drain, tile_ready, norm
        self.residual, self.halves = residual, halves
        self.steps = sum(n for n, _ in views)
        first = views[0][1]
        self.kt_n = (first[0] if isinstance(first, tuple) else first).shape[0] // P


class Residual:

    def __init__(self, nc, stack, name, x):
        self.nc = nc
        self.raw = stack.enter_context(nc.sbuf_tensor(name + "_raw", [P, 2, NC, P], F32))
        self.bank = stack.enter_context(nc.psum_tensor(name + "_bank", [P, NC, P], F32))
        self.landed = [stack.enter_context(nc.semaphore(f"{name}_landed{u}")) for u in range(2)]
        self.tiles = x.rearrange("(c p) (i u f) -> u i p c f", p=P, u=2, f=P)

    def load(self, sp, i, u):
        sp.dma_start(self.raw[:, u], self.tiles[u, i]).then_inc(self.landed[u], 16)

    def turn(self, pe, ident, i, u):
        pe.wait_ge(self.landed[u], 16 * i + 16)
        for c in range(NC):
            ins = self.nc.tensor.transpose(self.bank[:, c, :], self.raw[:, u, c, :], ident)
        return ins


class Weights:

    def __init__(self, nc, stack, name, side):
        self.nc = nc
        self.raw = stack.enter_context(nc.sbuf_tensor(name + "_raw", [P, 2, KD, P], F32, side=side))
        self.hi, self.lo = (stack.enter_context(nc.sbuf_tensor(f"{name}_{p}", [P, 2, KD, P], F32R, side=side))
                            for p in ("hi", "lo"))
        self.landed = [stack.enter_context(nc.semaphore(f"{name}_landed{u}")) for u in range(2)]
        self.rounded, self.split, self.used = (stack.enter_context(nc.semaphore(f"{name}_{n}"))
                                               for n in ("rounded", "split", "used"))
        self.base = 0
        self.next = None

    def load(self, sp, tile, u, kt_n):
        sp.dma_start(self.raw[:, u, 0:kt_n], tile).then_inc(self.landed[u], 16)

    def round(self, u, kt_n):
        self.nc.scalar.copy(self.hi[:, u, 0:kt_n], self.raw[:, u, 0:kt_n]).then_inc(self.rounded, 1)

    def rest(self, u, kt_n):
        self.nc.gpsimd.tensor_tensor(self.lo[:, u, 0:kt_n], self.raw[:, u, 0:kt_n], self.hi[:, u, 0:kt_n].bitcast(F32),
                                     ALU.subtract).then_inc(self.split, 1)

    def start_loading(self, sp):
        n, view = self.next.views[0]
        for u in range(2):
            self.load(sp, weight_tiles(view, n)(0, u), u, self.next.kt_n)

    def start_rounding(self, act):
        for u in range(2):
            act.wait_ge(self.landed[u], 16 * (self.base // 2 + 1))
            self.round(u, self.next.kt_n)

    def start_splitting(self, pool):
        for u in range(2):
            pool.wait_ge(self.rounded, self.base + u + 1)
            self.rest(u, self.next.kt_n)


def dense(nc, name, k, w, jobs):
    with ExitStack() as ctx:
        own = tiles(nc, ctx, name)
        _, ps, sem = own
        bank = ps("bank", [P, 2, NH, HALF])
        ready, free = sem("ready"), sem("banks_free")
        bases = [sum(job.steps for job in jobs[:n]) for n in range(len(jobs))]
        drains = [job.drain(own, bank, ready, free, base) for job, base in zip(jobs, bases)]
        for job in jobs:
            if job.norm:
                job.norm.open(own)
        past = w.base
        with nc.Block() as block:
            @block.sync
            def _(sp):
                base = past
                for job in jobs:
                    for n, view in job.views:
                        tile = weight_tiles(view, n)
                        for u in range(2):
                            if base > past:
                                sp.wait_ge(w.split, base + u - 1)
                                w.load(sp, tile(0, u), u, job.kt_n)
                            if job.residual:
                                job.residual.load(sp, 0, u)
                        if n > 3:
                            with sp.Fori(1, n // 2) as i:
                                for u in range(2):
                                    sp.wait_ge(w.split, 2 * i + (base + u - 1))
                                    w.load(sp, tile(i, u), u, job.kt_n)
                                    if job.residual:
                                        sp.wait_ge(ready, 2 * i + (base - past + u - 1))
                                        job.residual.load(sp, i, u)
                        if n % 2:
                            sp.wait_ge(w.split, base + n - 2)
                            w.load(sp, tile(n // 2, 0), 0, job.kt_n)
                        base += n

            @block.tensor
            def _(pe):
                for job, base in zip(jobs, bases):
                    def products(i, u, first=False):
                        pe.wait_ge(w.split, 2 * i + (past + base + u + 1))
                        pe.wait_ge(free, 2 * i + (base + u + 1))
                        for h in range(job.halves):
                            for kt in range(job.kt_n):
                                if first and h == 0 and job.tile_ready:
                                    job.tile_ready(pe, kt)
                                hi, lo = job.src(kt, h)
                                for n, (a, b) in enumerate(((w.hi, hi), (w.hi, lo), (w.lo, hi))):
                                    mm = nc.tensor.matmul(bank[:, u, h, 0:b.shape[1]], a[:, u, kt, :], b,
                                                          start=(kt == 0 and n == 0),
                                                          stop=(kt == job.kt_n - 1 and n == 2))
                            if first and h == 0 and job.norm:
                                job.norm.sum_up(pe, k)
                        if job.residual:
                            pe.wait_ge(free, 2 * i + (base + u + 2))
                            mm = job.residual.turn(pe, k.const["ident"], i, u)
                        mm.then_inc(ready, 1)

                    peel = bool(job.tile_ready or job.norm)
                    if peel:
                        products(0, 0, first=True)
                    turns(pe, job.steps, products, 1 if peel else 0)

            @block.scalar
            def _(act):
                def rounding(job, base):
                    def round_weights(i, u):
                        act.wait_ge(w.landed[u], 16 * i + 16 * ((past + base) // 2 + 1))
                        act.wait_ge(w.used, 2 * i + (past + base + u - 1))
                        w.round(u, job.kt_n)
                    return round_weights

                for n, (job, base, (drain, _, prologue, _)) in enumerate(zip(jobs, bases, drains)):
                    ahead = rounding(job, base)
                    body = drain or (lambda i, u: None)
                    last = (job.steps - 1) // 2
                    if prologue:
                        prologue(act)
                    if base:
                        ahead(0, 1)
                    if job.norm:
                        job.norm.take_root(act, k)
                    body(0, 0)
                    ahead(1, 0)
                    body(0, 1)
                    with act.Fori(1, last) as i:
                        ahead(i, 1)
                        body(i, 0)
                        ahead(i + 1, 0)
                        body(i, 1)
                    if job.steps % 2 == 0:
                        ahead(last, 1)
                    body(last, 0)
                    if n + 1 < len(jobs):
                        rounding(jobs[n + 1], bases[n + 1])(0, 0)
                    if job.steps % 2 == 0:
                        body(last, 1)

            @block.gpsimd
            def _(pool):
                for job, base in zip(jobs, bases):
                    def rest(i, u):
                        pool.wait_ge(w.rounded, 2 * i + (past + base + u + 1))
                        w.rest(u, job.kt_n)

                    if base:
                        rest(0, 0)
                        rest(0, 1)
                    with pool.Fori(1, job.steps // 2) as i:
                        rest(i, 0)
                        rest(i, 1)
                    if job.steps % 2:
                        rest(job.steps // 2, 0)

            @block.vector
            def _(dve):
                dve.sem_inc(free, 2)
                for job, base, (_, drain, _, prologue) in zip(jobs, bases, drains):
                    def step(i, u):
                        dve.wait_ge(ready, 2 * i + (base + u + 1))
                        dve.sem_inc(w.used, 1)
                        if drain:
                            drain(i, u)

                    if prologue:
                        prologue(dve)
                    if job.norm:
                        job.norm.invert(dve)
                    turns(dve, job.steps, step)
        w.base += bases[-1] + jobs[-1].steps


class Norm:

    def __init__(self, nc, stack, name, work, gain, parts):
        self.nc, self.gain, self.parts, self.name = nc, gain, parts, name
        self.full, self.squares, self.total = (work[:, n, :] for n in range(3))
        self.rstd = self.total
        self.stored, self.added, self.squared, self.gained, self.rounded, self.split = (
            stack.enter_context(nc.semaphore(f"{name}_{n}"))
            for n in ("stored", "added", "squared", "gained", "rounded", "split"))

    def add_out(self, dst, residual=None):
        nc, out, gains = self.nc, Steps(dst, KD), Steps(self.gain.unsqueeze(2), KD)
        hi, lo = (Steps(p, KD) for p in self.parts or (dst, dst))

        def drain(own, bank, ready, free, base):
            def act_step(i, u):
                nc.scalar.wait_ge(self.added, 2 * i + u + 1)
                nc.scalar.wait_ge(self.split, 2 * i + u + 1)
                nc.scalar.activation(self.squares, out(i, u), ACT.Square).then_inc(self.squared, 1)
                if self.parts:
                    nc.scalar.wait_ge(self.gained, 2 * i + u + 1)
                    nc.scalar.copy(hi(i, u), self.full).then_inc(self.rounded, 1)

            def dve_step(i, u):
                x = out(i, u)
                if residual:
                    rest = residual.bank[:, :, :].rearrange("p c t -> p (c t)")
                    nc.vector.tensor_copy(x, rest).then_inc(self.stored, 1)
                    nc.vector.wait_ge(self.stored, 2 * i + u + 1)
                nc.vector.tensor_tensor(halves(x), halves(x), bank[:, u], ALU.add).then_inc(self.added, 1)
                nc.vector.wait_ge(self.added, 2 * i + u + 1)
                nc.vector.sem_inc(free, 1)
                gain = gains(i, u).to_broadcast([P, T])
                if self.parts:
                    nc.vector.tensor_tensor(self.full, x, gain, ALU.mult).then_inc(self.gained, 1)
                nc.vector.wait_ge(self.squared, 2 * i + u + 1)
                nc.vector.tensor_tensor(self.total, self.total, self.squares, ALU.add)
                if self.parts:
                    nc.vector.wait_ge(self.rounded, 2 * i + u + 1)
                    nc.vector.tensor_tensor(lo(i, u), self.full, hi(i, u).bitcast(F32), ALU.subtract).then_inc(self.split, 1)
                else:
                    nc.vector.tensor_tensor(x, x, gain, ALU.mult).then_inc(self.split, 1)

            def clear(dve):
                nc.vector.memset(self.total, 0.0).then_inc(self.split, 1)

            return act_step, dve_step, None, clear
        return drain

    def tile_ready(self, pe, kt):
        pe.wait_ge(self.split, kt + 2)

    def open(self, own):
        _, ps, sem = own
        self.sum = ps(self.name + "_sum", [P, NH, HALF])
        self.summed, self.rooted, self.inverted = (sem(f"{self.name}_{n}") for n in ("summed", "rooted", "inverted"))

    def sum_up(self, pe, k):
        pe.wait_ge(self.split, KD + 1)
        for h in range(NH):
            mm = self.nc.tensor.matmul(self.sum[:, h, :], k.const["ones"], self.total[:, h * HALF:(h + 1) * HALF],
                                       start=True, stop=True)
        mm.then_inc(self.summed, 1)

    def take_root(self, act, k):
        act.wait_ge(self.summed, 1)
        self.nc.scalar.activation(halves(self.squares), self.sum[:, :, :], ACT.Sqrt, scale=1.0 / D,
                                  bias=k.eps[:, 0:1]).then_inc(self.rooted, 1)

    def invert(self, dve):
        dve.wait_ge(self.rooted, 1)
        self.nc.vector.reciprocal(self.rstd, self.squares).then_inc(self.inverted, 1)
        dve.wait_ge(self.inverted, 1)


def halves(x):
    return x.rearrange("p (h t) -> p h t", h=NH)


class Steps:

    def __init__(self, x, n):
        self.x, self.n = x, n
        self.pairs = x[:, 0:n // 2 * 2].rearrange("p (i u) t -> p i u t", u=2)

    def __call__(self, i, u):
        if isinstance(i, int):
            return self.x[:, 2 * i + u, :]
        return self.pairs[:, i, u, :]


def scaled_out(nc, dst, n, rstd):
    out = Steps(dst, n)
    few = rstd.shape[1]

    def drain(own, bank, ready, free, base):
        def dve_step(i, u):
            if few <= HALF:
                nc.vector.tensor_tensor(out(i, u), bank[:, u, 0, 0:few], rstd, ALU.mult).then_inc(free, 1)
                return
            nc.vector.tensor_tensor(halves(out(i, u)), bank[:, u], halves(rstd), ALU.mult).then_inc(free, 1)
        return None, dve_step, None, None
    return drain


def add_out(nc, dst):
    out = Steps(dst, KD)

    def drain(own, bank, ready, free, base):
        def dve_step(i, u):
            x = halves(out(i, u))
            nc.vector.tensor_tensor(x, x, bank[:, u], ALU.add).then_inc(free, 1)
        return None, dve_step, None, None
    return drain


def shift_mix_out(nc, dst, mu, rstd):
    out = Steps(dst, R_TILES)
    mus = Steps(mu.unsqueeze(2), R_TILES)

    def drain(own, bank, ready, free, base):
        sb, _, sem = own
        raw = sb("raw", [P, 2, T + 1])
        diff = sb("diff", [P, 2, T])
        mu_of = sb("mu_of", [P, 2])
        stored, mixed, chosen, subtracted = (sem(n) for n in ("stored", "mixed", "chosen", "subtracted"))

        def prologue(act):
            act.sem_inc(mixed, 2)
            nc.scalar.mul(raw[:, :, 0:1], mu[:, 0:2].unsqueeze(2), 0.0)

        def act_step(i, u):
            nc.scalar.wait_ge(mixed, 2 * i + u + 1)
            nc.scalar.copy(mu_of[:, u:u + 1], mus(i, u)).then_inc(chosen, 1)

        def dve_step(i, u):
            nc.vector.tensor_tensor(halves(raw[:, u, 1:T + 1]), bank[:, u], halves(rstd), ALU.mult).then_inc(stored, 1)
            nc.vector.wait_ge(stored, 2 * i + u + 1)
            nc.vector.sem_inc(free, 1)
            nc.vector.wait_ge(chosen, 2 * i + u + 1)
            nc.vector.tensor_tensor(diff[:, u, :], raw[:, u, 0:T], raw[:, u, 1:T + 1],
                                    ALU.subtract).then_inc(subtracted, 1)
            nc.vector.wait_ge(subtracted, 2 * i + u + 1)
            nc.vector.scalar_tensor_tensor(out=out(i, u), in0=diff[:, u, :], scalar=mu_of[:, u:u + 1],
                                           in1=raw[:, u, 1:T + 1], op0=ALU.mult, op1=ALU.add).then_inc(mixed, 1)
        return act_step, dve_step, prologue, None
    return drain


class Gate:

    def __init__(self, nc, stack, name, silu, prod, rstd, hidden):
        self.nc, self.silu, self.prod, self.rstd, self.hidden = nc, silu, prod, rstd, hidden
        self.scaled, self.activated, self.rounded, self.kept = (
            stack.enter_context(nc.semaphore(f"{name}_{n}")) for n in ("scaled", "activated", "rounded", "kept"))
        self.pairs = 0

    def group(self, width):
        nc, past = self.nc, self.pairs
        hi, lo = self.hidden
        self.pairs += width

        def drain(own, bank, ready, free, base):
            def act_step(i, u):
                if u == 0:
                    nc.scalar.wait_ge(self.scaled, 3 * i + (3 * past + 1))
                    nc.scalar.activation(self.silu, self.silu, ACT.Silu).then_inc(self.activated, 1)
                else:
                    nc.scalar.wait_ge(self.scaled, 3 * i + (3 * past + 3))
                    nc.scalar.copy(hi[:, i, :], self.prod).then_inc(self.rounded, 1)

            def dve_step(i, u):
                if u == 0:
                    nc.vector.tensor_tensor(halves(self.silu), bank[:, 0], halves(self.rstd),
                                            ALU.mult).then_inc(self.scaled, 1)
                    nc.vector.wait_ge(self.scaled, 3 * i + (3 * past + 1))
                    nc.vector.sem_inc(free, 1)
                else:
                    nc.vector.tensor_tensor(halves(self.prod), bank[:, 1], halves(self.rstd),
                                            ALU.mult).then_inc(self.scaled, 1)
                    nc.vector.wait_ge(self.scaled, 3 * i + (3 * past + 2))
                    nc.vector.sem_inc(free, 1)
                    nc.vector.wait_ge(self.activated, i + (past + 1))
                    nc.vector.tensor_tensor(self.prod, self.prod, self.silu, ALU.mult).then_inc(self.scaled, 1)
                    nc.vector.wait_ge(self.rounded, i + (past + 1))
                    nc.vector.tensor_tensor(lo[:, i, :], self.prod, hi[:, i, :].bitcast(F32),
                                            ALU.subtract).then_inc(self.kept, 1)
            return act_step, dve_step, None, None

        def tile_ready(pe, kt):
            pe.wait_ge(self.kept, past + kt + 1)
        return drain, tile_ready


def token_major(nc, name, src, kt_n, w_dram, dst, n_tok, width, rstd_tok, beside):
    nt = n_tok // P
    nb = width // HALF
    with ExitStack() as ctx:
        sb, ps, sem = tiles(nc, ctx, name)
        w = sb("w", [P, nb, kt_n, HALF])
        w_hi = ctx.enter_context(nc.sbuf_tensor(name + "_w_hi", [P, nb, kt_n, HALF], F32R))
        w_lo = ctx.enter_context(nc.sbuf_tensor(name + "_w_lo", [P, nb, kt_n, HALF], F32R))
        pairs = ((src[0], w_hi), (src[1], w_hi), (src[0], w_lo))
        bank = ps("bank", [P, 2, HALF])
        landed = [sem(f"landed{n}") for n in range(kt_n)]
        ready, copied, rounded, split = sem("ready"), sem("copied"), sem("rounded"), sem("split")
        rows = w_dram.rearrange("(kt p) (b f) -> kt p b f", p=P, f=HALF)
        beside.open((sb, ps, sem))
        with nc.Block() as block:
            @block.sync
            def _(sp):
                beside.load(sp)
                for kt in range(kt_n):
                    sp.dma_start(w[:, :, kt, :], rows[kt]).then_inc(landed[kt], 16)

            @block.tensor
            def _(pe):
                beside.logits(pe)
                for b in range(nb):
                    for c in range(nt):
                        n = b * nt + c
                        if n == 3:
                            beside.cumsums(pe)
                        if n >= 2:
                            pe.wait_ge(copied, n - 1)
                        for kt in range(kt_n):
                            if n == 0:
                                pe.wait_ge(split, kt + 1)
                            for m, (x, y) in enumerate(pairs):
                                mm = nc.tensor.matmul(bank[:, n % 2, :], x[:, kt, c * P:(c + 1) * P], y[:, b, kt, :],
                                                      start=(kt == 0 and m == 0),
                                                      stop=(kt == kt_n - 1 and m == len(pairs) - 1))
                        mm.then_inc(ready, 1)

            @block.scalar
            def _(act):
                for kt in range(kt_n):
                    act.wait_ge(landed[kt], 16)
                    nc.scalar.copy(w_hi[:, :, kt, :], w[:, :, kt, :]).then_inc(rounded, 1)
                beside.scalar(act)

            @block.gpsimd
            def _(pool):
                for kt in range(kt_n):
                    pool.wait_ge(rounded, kt + 1)
                    nc.gpsimd.tensor_tensor(w_lo[:, :, kt, :], w[:, :, kt, :], w_hi[:, :, kt, :].bitcast(F32),
                                            ALU.subtract).then_inc(split, 1)

            @block.vector
            def _(dve):
                beside.negatives(dve)
                for b in range(nb):
                    for c in range(nt):
                        n = b * nt + c
                        if n in (1, 2):
                            beside.log_decays(dve, n - 1)
                        if n in (4, 5):
                            beside.decayed(dve, n - 4)
                        dve.wait_ge(ready, n + 1)
                        out = dst[:, c, b * HALF:(b + 1) * HALF]
                        nc.vector.tensor_scalar(out, bank[:, n % 2, :], rstd_tok[:, c:c + 1], None,
                                                ALU.mult).then_inc(copied, 1)


def finish(nc, k, name, src, total, out):
    rows = out.rearrange("(c p) f -> c p f", p=P)
    with ExitStack() as ctx:
        sb, ps, sem = tiles(nc, ctx, name)
        tok = sb("tok", [P, 2, KD, P])
        root, rstd = sb("root", [P, NC]), sb("rstd", [P, NC])
        bank = ps("bank", [P, 2, KD, P])
        sums = ps("sums", [P, NC])
        summed, rooted, inverted, turned, copied = (sem(n) for n in ("summed", "rooted", "inverted", "turned", "copied"))
        written = [sem("written0"), sem("written1")]
        with nc.Block() as block:
            @block.tensor
            def _(pe):
                for c in range(NC):
                    mm = nc.tensor.matmul(sums[:, c:c + 1], total[:, c * P:(c + 1) * P], k.const["ones"][:, 0:1],
                                          start=True, stop=True)
                mm.then_inc(summed, 1)
                for c in range(NC):
                    if c >= 2:
                        pe.wait_ge(copied, c - 1)
                    for f in range(KD):
                        mm = nc.tensor.transpose(bank[:, c % 2, f, :], src[:, f, c * P:(c + 1) * P], k.const["ident"])
                    mm.then_inc(turned, 1)

            @block.scalar
            def _(act):
                act.wait_ge(summed, 1)
                nc.scalar.activation(root[:, :], sums[:, :], ACT.Sqrt, scale=1.0 / D, bias=k.eps[:, 0:1]).then_inc(rooted, 1)

            @block.vector
            def _(dve):
                dve.wait_ge(rooted, 1)
                nc.vector.reciprocal(rstd[:, :], root[:, :]).then_inc(inverted, 1)
                dve.wait_ge(inverted, 1)
                for c in range(NC):
                    dve.wait_ge(turned, c + 1)
                    if c >= 2:
                        dve.wait_ge(written[c % 2], 16 * (c // 2))
                    nc.vector.tensor_scalar(tok[:, c % 2], bank[:, c % 2], rstd[:, c:c + 1], None,
                                            ALU.mult).then_inc(copied, 1)

            @block.sync
            def _(sp):
                for c in range(NC):
                    sp.wait_ge(copied, c + 1)
                    sp.dma_start(rows[c], tok[:, c % 2].rearrange("p k f -> p (k f)")).then_inc(written[c % 2], 16)
                for u in range(2):
                    sp.wait_ge(written[u], 16 * (NC // 2))


class GlaDecays:

    def __init__(self, nc, k, stack, q_key, gate, lo, wa2, scratch):
        self.nc, self.k, self.gate, self.lo, self.wa2 = nc, k, gate, lo, wa2
        chunk = lambda x: x.rearrange("p h (c t) -> p c h t", t=P)
        self.q_key = chunk(q_key)
        self.q, self.key = self.q_key[:, :, 0:2, :], self.q_key[:, :, 2:4, :]
        self.soft = scratch[:, 0, :].rearrange("p (c j) -> p c j", c=NC)
        self.la = scratch[:, 1, :].rearrange("p (c j) -> p c j", c=NC)
        self.down, self.up = (x.rearrange("p c (f t) -> p c f t", t=P) for x in (self.soft, self.la))
        self.wa2_sb = stack.enter_context(nc.sbuf_tensor("gla_wa2_sb", [RANK, GH * GK], F32))
        self.mid, self.last = (stack.enter_context(nc.sbuf_tensor(f"gla_{n}", [P, NC, 2], F32)) for n in ("mid", "last"))
        self.half = lambda n: slice(n * NC // 2, (n + 1) * NC // 2)

    def open(self, own):
        _, ps, sem = own
        self.bank = ps("decays", [P, NC, GH * GK])
        self.cum = self.bank[:, :, :].rearrange("p c (f t) -> p c f t", t=P)
        self.mids = ps("mids", [P, NC, 2])
        self.loaded, self.multiplied, self.magnitude, self.exponential, self.softened = (
            sem(n) for n in ("wa2_loaded", "multiplied", "magnitude", "exponential", "softened"))
        self.negative, self.logged, self.summed, self.raised = (sem(n) for n in ("negative", "logged", "summed",
                                                                                  "raised"))

    def load(self, sp):
        sp.dma_start(self.wa2_sb[:, :], self.wa2).then_inc(self.loaded, 16)

    def logits(self, pe):
        k, mm = self.k, self.nc.tensor.matmul
        pe.wait_ge(self.loaded, 16)
        for c in range(NC):
            mm(self.bank[:, c, :], k.ones_row[0:1, 0:P], k.row["gla_ba"], start=True, stop=False)
            ins = mm(self.bank[:, c, :], self.lo[:, c * P:(c + 1) * P], self.wa2_sb[:, :], start=False, stop=True)
            if c % (NC // 2) == NC // 2 - 1:
                ins.then_inc(self.multiplied, 1)

    def cumsums(self, pe):
        k, mm = self.k, self.nc.tensor.matmul
        for n in range(2):
            pe.wait_ge(self.logged, n + 1)
            for c in range(NC)[self.half(n)]:
                for f in range(2):
                    x = self.la[:, c, f * P:(f + 1) * P]
                    mm(self.cum[:, c, f, :], x, k.const["cum_in"], start=True, stop=True)
                    ins = mm(self.mids[:, c, f:f + 1], x, k.const["cum_ex"][:, 0:1], start=True, stop=True)
            ins.then_inc(self.summed, 1)

    def scalar(self, act):
        fn = self.nc.scalar.activation
        for n in range(2):
            act.wait_ge(self.multiplied, n + 1)
            fn(self.soft[:, self.half(n), :], self.bank[:, self.half(n), :], ACT.Abs).then_inc(self.magnitude, 1)
        for n in range(2):
            act.wait_ge(self.magnitude, n + 1)
            x = self.soft[:, self.half(n), :]
            fn(x, x, ACT.Exp, scale=-1.0).then_inc(self.exponential, 1)
        for n in range(2):
            act.wait_ge(self.exponential, n + 1)
            x = self.soft[:, self.half(n), :]
            fn(x, x, ACT.Ln, bias=1.0).then_inc(self.softened, 1)
        for n in range(2):
            act.wait_ge(self.summed, n + 1)
            s = self.half(n)
            fn(self.up[:, s], self.cum[:, s], ACT.Exp, scale=1.0 / 16)
            fn(self.last[:, s, :], self.cum[:, s, :, P - 1], ACT.Exp, scale=1.0 / 16)
            fn(self.down[:, s], self.cum[:, s], ACT.Exp, scale=-1.0 / 16).then_inc(self.raised, 1)
        fn(self.mid[:, :, :], self.mids[:, :, :], ACT.Exp, scale=-1.0 / 16)
        for h in range(GH):
            fn(self.gate[:, h, :], self.gate[:, h, :], ACT.Silu)

    def negatives(self, dve):
        for n in range(2):
            dve.wait_ge(self.magnitude, n + 1)
            self.nc.vector.tensor_scalar(self.la[:, self.half(n), :], self.bank[:, self.half(n), :], 0.0, None,
                                         ALU.min).then_inc(self.negative, 1)

    def log_decays(self, dve, n):
        dve.wait_ge(self.softened, n + 1)
        dve.wait_ge(self.negative, n + 1)
        x = self.la[:, self.half(n), :]
        self.nc.vector.tensor_tensor(x, x, self.soft[:, self.half(n), :], ALU.subtract).then_inc(self.logged, 1)

    def decayed(self, dve, n):
        s = self.half(n)
        dve.wait_ge(self.raised, n + 1)
        for f in range(2):
            self.nc.vector.scalar_tensor_tensor(out=self.q[:, s, f], in0=self.q[:, s, f], scalar=GK ** -0.5,
                                                in1=self.up[:, s, f], op0=ALU.mult, op1=ALU.mult)
            self.nc.vector.tensor_tensor(self.key[:, s, f], self.key[:, s, f], self.down[:, s, f], ALU.mult)


def pipelined(eng, turn, ahead, behind):
    first = (behind + 1) // 2
    end = (NC - ahead) // 2
    for c in range(2 * first):
        turn(c // 2, c % 2)
    with eng.Fori(first, end) as i:
        turn(i, 0)
        turn(i, 1)
    for c in range(2 * end, NC + behind):
        turn(c // 2, c % 2)


def near(i, u, d):
    c = 2 * i + (u + d)
    return not isinstance(i, int) or 0 <= c < NC, c


def pair_rows(h, n):
    return slice(n * (h % 2), n * (h % 2) + n)


def gla(nc, k, d, vtok, og, weights):
    with ExitStack() as ctx:
        sb, ps, sem = tiles(nc, ctx, "gla")
        cur, kt = sb("cur", [P, 2, 4, P]), sb("kt", [P, 2, 2, P])
        qcur, kcur = cur[:, :, 0:2, :], cur[:, :, 2:4, :]
        vcur = sb("vcur", [P, 2, GH * GV])
        sc = sb("sc", [P, 2, GH, P])
        state = sb("state", [P, 2, GV])
        entry = sb("entry", [P, 2, 2, GV])
        sq, root = sb("sq", [P, GH, P]), sb("root", [P, 2, GH, P])
        turn_b, kv_b, sum_b = ps("turn_b", [P, HALF]), ps("kv_b", [P, HALF]), ps("sum_b", [P, HALF])
        score_b, out_b = ps("score_b", [P, 2, HALF]), ps("out_b", [P, 2, HALF])
        copied, turned, kept_keys, scored, masked = (sem(n) for n in ("copied", "turned", "kept_keys", "scored", "masked"))
        added, entered, output, kept, squared = (sem(n) for n in ("added", "entered", "output", "kept", "squared"))
        summed, rooted, inverted, normed, stepped = (sem(n) for n in ("summed", "rooted", "inverted", "normed", "stepped"))
        cog, cgate = (x.rearrange("p h (c t) -> p c h t", t=P) for x in (og, d.gate))
        with nc.Block() as block:
            @block.sync
            def _(sp):
                weights.start_loading(sp)

            @block.gpsimd
            def _(pool):
                weights.start_splitting(pool)

            @block.tensor
            def _(pe):
                def keys_and_scores(c, u):
                    pe.wait_ge(copied, c + 1)
                    for f in range(2):
                        ins = nc.tensor.transpose(turn_b[:, f * P:(f + 1) * P], kcur[:, u, f, :], k.const["ident"])
                    ins.then_inc(turned, 1)
                    if not (isinstance(c, int) and c == 0):
                        pe.wait_ge(masked, c)
                    for h in range(GH):
                        r = pair_rows(h, GK)
                        ins = nc.tensor.matmul(score_b[:, h % 2, (h // 2) * P:(h // 2 + 1) * P], kcur[r, u, h // 2, :],
                                               qcur[r, u, h // 2, :], start=True, stop=True)
                    ins.then_inc(scored, 1)

                def add_state(c, u):
                    pe.wait_ge(kept_keys, c + 1)
                    if not (isinstance(c, int) and c == 0):
                        pe.wait_ge(stepped, 2 * c - 1)
                    for h in range(GH):
                        ins = nc.tensor.matmul(kv_b[pair_rows(h, GK), (h // 2) * GV:(h // 2 + 1) * GV],
                                               kt[:, u, h // 2, GK * (h % 2):GK * (h % 2) + GK],
                                               vcur[:, u, h * GV:(h + 1) * GV], start=True, stop=True)
                    ins.then_inc(added, 1)

                def outputs(c, u):
                    pe.wait_ge(masked, c + 1)
                    pe.wait_ge(entered, c + 1)
                    if not (isinstance(c, int) and c == 0):
                        pe.wait_ge(kept, c)
                    for h in range(GH):
                        o = out_b[:, h % 2, (h // 2) * P:(h // 2 + 1) * P]
                        r = pair_rows(h, GK)
                        nc.tensor.matmul(o, vcur[:, u, h * GV:(h + 1) * GV], sc[:, u, h, :], start=True, stop=False)
                        ins = nc.tensor.matmul(o, entry[r, u, h // 2, :], qcur[r, u, h // 2, :], start=False, stop=True)
                    ins.then_inc(output, 1)

                def norm_sums(c):
                    pe.wait_ge(squared, c + 1)
                    if not (isinstance(c, int) and c == 0):
                        pe.wait_ge(rooted, c)
                    nc.tensor.matmul(sum_b[:, :], k.const["ones"], sq[:, :, :].rearrange("p h t -> p (h t)"),
                                     start=True, stop=True).then_inc(summed, 1)

                def turn(i, u):
                    there, c = near(i, u, 0)
                    more, later = near(i, u, 1)
                    past, earlier = near(i, u, -1)
                    if more:
                        keys_and_scores(later, 1 - u)
                    if there:
                        outputs(c, u)
                    if more:
                        add_state(later, 1 - u)
                    if past:
                        norm_sums(earlier)

                keys_and_scores(0, 0)
                add_state(0, 0)
                pipelined(pe, turn, 2, 2)

            @block.scalar
            def _(act):
                def copy_in(c, u):
                    nc.scalar.copy(cur[:, u], d.q_key[:, c])
                    nc.scalar.copy(vcur[:, u, :], vtok[:, c, :]).then_inc(copied, 1)

                def keep_keys(c, u):
                    act.wait_ge(turned, c + 1)
                    nc.scalar.copy(kt[:, u].rearrange("p f t -> p (f t)"), turn_b[:, 0:2 * P]).then_inc(kept_keys, 1)

                def keep_outputs(c):
                    act.wait_ge(output, c + 1)
                    if not (isinstance(c, int) and c == 0):
                        act.wait_ge(summed, c)
                    out = out_b[:, :, 0:2 * P].rearrange("p e (n t) -> p e n t", t=P)
                    nc.scalar.activation(sq[:, :, :].rearrange("p (n e) t -> p e n t", e=2), out,
                                         ACT.Square).then_inc(squared, 1)
                    nc.scalar.copy(cog[:, c].rearrange("p (n e) t -> p e n t", e=2), out).then_inc(kept, 1)

                def roots(c, u):
                    act.wait_ge(summed, c + 1)
                    if not (isinstance(c, int) and c < 2):
                        act.wait_ge(inverted, c - 1)
                    nc.scalar.activation(root[:, u], sum_b[:, :].rearrange("p (h t) -> p h t", t=P), ACT.Sqrt,
                                         scale=1.0 / GV, bias=k.eps[:, 1:2]).then_inc(rooted, 1)

                def turn(i, u):
                    there, c = near(i, u, 0)
                    more, later = near(i, u, 1)
                    most, latest = near(i, u, 2)
                    past, earlier = near(i, u, -1)
                    if more:
                        keep_keys(later, 1 - u)
                    if there:
                        keep_outputs(c)
                    if most:
                        copy_in(latest, u)
                    if past:
                        roots(earlier, 1 - u)

                weights.start_rounding(act)
                copy_in(0, 0)
                copy_in(1, 1)
                keep_keys(0, 0)
                pipelined(act, turn, 2, 2)

            @block.vector
            def _(dve):
                def mask(c, u):
                    dve.wait_ge(scored, c + 1)
                    nc.vector.tensor_tensor(sc[:, u].rearrange("p (n e) t -> p e n t", e=2),
                                            score_b[:, :, 0:2 * P].rearrange("p e (n t) -> p e n t", t=P),
                                            k.const["up_incl"].unsqueeze(1).unsqueeze(1).to_broadcast([P, 2, 2, P]),
                                            ALU.mult).then_inc(masked, 1)

                def step_state(c, u):
                    dve.wait_ge(added, c + 1)
                    dve.wait_ge(entered, c + 1)
                    nc.vector.tensor_tensor(state[:, :, :], entry[:, u],
                                            kv_b[:, 0:2 * GV].rearrange("p (f v) -> p f v", f=2),
                                            ALU.add).then_inc(stepped, 1)
                    dve.wait_ge(stepped, 2 * c + 1)
                    nc.vector.tensor_tensor(state[:, :, :], state[:, :, :], wide(d.last[:, c, :], GV),
                                            ALU.mult).then_inc(stepped, 1)
                    dve.wait_ge(stepped, 2 * c + 2)
                    if not (isinstance(c, int) and c == 0):
                        dve.wait_ge(output, c)
                    nc.vector.tensor_tensor(entry[:, 1 - u], state[:, :, :], wide(d.mid[:, c + 1, :], GV),
                                            ALU.mult).then_inc(entered, 1)

                def finish_norm(c, u):
                    dve.wait_ge(rooted, c + 1)
                    nc.vector.reciprocal(root[:, u], root[:, u]).then_inc(normed, 1)
                    dve.wait_ge(normed, 2 * c + 1)
                    nc.vector.scalar_tensor_tensor(out=cog[:, c], in0=cog[:, c], scalar=k.par["gla_norm_g"][:, 0:1],
                                                   in1=root[:, u], op0=ALU.mult, op1=ALU.mult).then_inc(normed, 1)
                    dve.wait_ge(normed, 2 * c + 2)
                    nc.vector.tensor_tensor(cog[:, c], cog[:, c], cgate[:, c], ALU.mult).then_inc(inverted, 1)

                def turn(i, u):
                    more, later = near(i, u, 1)
                    past, earliest = near(i, u, -2)
                    if more:
                        step_state(2 * i + u, u)
                        mask(later, 1 - u)
                    if past:
                        finish_norm(earliest, u)

                nc.vector.memset(entry[:, 0], 0.0).then_inc(entered, 1)
                mask(0, 0)
                pipelined(dve, turn, 2, 2)


PREP_PE = ("decay_logits", "rate_logits", "gates", "key_norms", "turn_v", "cumsum", "bonus", "turn_a", "turn_b",
           "turn_k")
PREP_ACT = ("loras", "decays", "rates", "gates", "key_roots", "keep_v", "down", "ends", "up", "bonus", "keep_a",
            "keep_b", "keep_k")
PREP_DVE = ("raw_kk", "raw_sq", "decay_bias", "rate_bias", "root_max", "inv_norm0", "inv_norm1", "kk", "rate_k",
            "k_gain", "key", "b_vec", "key_r", "bonus_rk", "k_decayed", "decayed")
LEVELS = range(len(MERGES))
TURNS = tuple(f"{n}{lv}_{g}" for lv in LEVELS for g in "ab" for n in ("join", "turn"))
CORE_PE = ("gram_n", "gram0", "gram1", "gram2", "gram3") + tuple(
    name for lv in LEVELS for name in TURNS[4 * lv:4 * lv + 4] + (f"left{lv}_a", f"left{lv}_b")) + (
    "removal", "chunk_h", "removed", "state", "outputs")
CORE_ACT = ("keep_n",) + TURNS + ("keep_w", "keep_u", "keep_y")
CORE_DVE = ("gram0", "gram1", "gram2", "gram3") + tuple(f"left{lv}_{g}" for lv in LEVELS for g in "ab") + (
    "keep_h", "entered", "state_sum", "state")
CORE_POOL = ("merge0_a", "plus_a", "merge0_b", "plus_b") + tuple(
    f"merge{lv}_{g}" for lv in LEVELS[1:] for g in "ab")
CLOSE_PE = ("means", "variances")
CLOSE_ACT = ("centred_sq", "roots")
CLOSE_DVE = ("centred", "inv_std", "normed", "gained", "bonus_v", "with_bias", "with_bonus", "written")


class RwkvTiles:

    def __init__(self, nc, ctx, z):
        sb, ps, sem = tiles(nc, ctx, "rwkv")
        pair = lambda n, s: [sb(f"{n}{u}", s) for u in range(2)]
        self.z = z[:, :, :].rearrange("p f (c t) -> p c f t", t=P)
        self.w2, self.a2, self.g2 = sb("w2", [P, HALF]), sb("a2", [P, HALF]), sb("g2", [P, HALF])
        self.w0 = sb("w0", [P, HALF])
        self.lora = sb("lora", [P, 2, P])
        self.sig_w = sb("sig_w", [P, HALF])
        self.rate, self.kk, self.t1, self.t2, self.key = (sb(n, [P, RT, P]) for n in ("rate", "kk", "t1", "t2", "key"))
        self.gates, self.bonus = pair("gates", [P, RT, P]), pair("bonus", [P, RT, P])
        self.ar = pair("ar", [P, RT, 2, P])
        self.bt, self.kt = pair("bt", [P, RT, P]), pair("kt", [P, RT, P])
        self.mid, self.last = pair("mid", [P, RT]), pair("last", [P, RT])
        self.tok = {n: pair(f"tok_{n}", [P, RH * RN]) for n in "abkv"}
        self.gm = sb("gm", [P, RH, 4, P])
        self.nmat = sb("nmat", [P, RH, P])
        self.merge = sb("merge", [P, len(MERGES) - 1, RH, P])
        self.pt = sb("pt", [P, RH, P])
        self.q = sb("q", [P, RH, P // 2])
        self.hu = sb("hu", [P, RH, RN])
        self.wt = sb("wt", [P, RT, P])
        self.state, self.entry = sb("state", [P, RT, RN]), sb("entry", [P, RT, RN])
        self.p, self.rb, self.ak, self.rk = (self.gm[:, :, n, :] for n in range(4))
        self.y, self.ysq, self.yroot = sb("y", [P, RT, P]), sb("ysq", [P, RT, P]), sb("yroot", [P, RT, P])
        self.bank = ps("bank", [P, 8, HALF])
        self.prep_pe, self.prep_act, self.prep_dve = sem("prep_pe"), sem("prep_act"), sem("prep_dve")
        self.core_pe, self.core_act, self.core_dve = sem("core_pe"), sem("core_act"), sem("core_dve")
        self.core_pool = sem("core_pool")
        self.close_pe, self.close_act, self.close_dve = sem("close_pe"), sem("close_act"), sem("close_dve")
        self.loaded, self.zeroed = sem("loaded"), sem("zeroed")

    def half_flat(self, b):
        return self.bank[:, b, 0:HALF // 2].rearrange("p (h t) -> p h t", t=P // 2)

    def flat(self, b):
        return self.bank[:, b, :].rearrange("p (h t) -> p h t", t=P)


HEADS = {"a": range(0, RH // 2), "b": range(RH // 2, RH)}
HS = {"a": slice(0, RH // 2), "b": slice(RH // 2, RH)}
GROUP_BANK = {"a": 0, "b": 3}


def rows(h):
    return slice(RN * (h % 2), RN * (h % 2) + RN)


def masks(x, n):
    return x.unsqueeze(1).to_broadcast([P, n, x.shape[1]])


def odd_blocks(x, width):
    if len(x.shape) == 2:
        return x.rearrange("p (n e b) -> p n e b", e=2, b=width)[:, :, 1, :]
    return x.rearrange("p h (n e b) -> p h n e b", e=2, b=width)[:, :, :, 1, :]


def blocks(x, width):
    if len(x.shape) == 2:
        return x.rearrange("p (n b) -> p n b", b=width)
    return x.rearrange("p h (n b) -> p h n b", b=width)


def over_chunks(eng, prepare, core, close):
    prepare(0, 0)
    core(0, 0, (1, 1), None)
    with eng.Fori(0, (NC - 2) // 2) as j:
        core(2 * j + 1, 1, (2 * j + 2, 0), (2 * j, 0))
        core(2 * j + 2, 0, (2 * j + 3, 1), (2 * j + 1, 1))
    core(NC - 1, 1, None, (NC - 2, 0))
    close(NC - 1, 1)


def rwkv_tensor(nc, pe, k, t):
    mm, bank, const = nc.tensor.matmul, t.bank, k.const

    def flat2(x):
        return x.rearrange("p f t -> p (f t)")

    def logits(c, b):
        pe.wait_ge(t.prep_act, at(PREP_ACT, "loras", c))
        mm(bank[:, 6, :], t.lora[:, 0, :], t.w2[:, :], start=True, stop=True).then_inc(t.prep_pe, 1)
        for f in range(RT):
            s = slice(f * P, (f + 1) * P)
            ins = mm(bank[:, 7, s], t.a2[:, s], t.lora[:, 0, :], start=True, stop=True)
        ins.then_inc(t.prep_pe, 1)

    def gates(c, b):
        pe.wait_ge(t.prep_dve, at(PREP_DVE, "decay_bias", c))
        for f in range(RT):
            s = slice(f * P, (f + 1) * P)
            ins = mm(bank[:, 6, s], t.g2[:, s], t.lora[:, 1, :], start=True, stop=True)
        ins.then_inc(t.prep_pe, 1)
        pe.wait_ge(t.prep_dve, at(PREP_DVE, "rate_bias", c))
        mm(bank[:, 7, :], const["pair_ones"], flat2(t.t1[:, :, :]), start=True, stop=True).then_inc(t.prep_pe, 1)

    def turn_v(c, b):
        pe.wait_ge(t.prep_act, at(PREP_ACT, "gates", c))
        for f in range(RT):
            ins = nc.tensor.transpose(bank[:, 6, f * P:(f + 1) * P], t.key[:, f, :], const["ident"])
        ins.then_inc(t.prep_pe, 1)

    def cumsum(c, b):
        pe.wait_ge(t.prep_act, at(PREP_ACT, "keep_v", c))
        for f in range(RT):
            ins = mm(bank[:, 6 + f // 2, (f % 2) * 2 * P:(f % 2 + 1) * 2 * P], t.sig_w[:, f * P:(f + 1) * P],
                     k.cum_w[:, :], start=True, stop=True)
        ins.then_inc(t.prep_pe, 1)

    def bonus(c, b):
        pe.wait_ge(t.prep_act, at(PREP_ACT, "up", c))
        pe.wait_ge(t.prep_dve, at(PREP_DVE, "bonus_rk", c))
        mm(bank[:, 6, :], const["pair_ones"], flat2(t.t1[:, :, :]), start=True, stop=True).then_inc(t.prep_pe, 1)

    def turn_a(c, b):
        pe.wait_ge(t.prep_dve, at(PREP_DVE, "decayed", c))
        for f in range(RT):
            ins = nc.tensor.transpose(bank[:, 7, f * P:(f + 1) * P], t.ar[b][:, f, 0, :], const["ident"])
        ins.then_inc(t.prep_pe, 1)

    def turn_bk(c, b):
        for n, x, last_read in ((6, t.bt[b], "bonus"), (7, t.kt[b], "keep_a")):
            pe.wait_ge(t.prep_act, at(PREP_ACT, last_read, c))
            for f in range(RT):
                ins = nc.tensor.transpose(bank[:, n, f * P:(f + 1) * P], x[:, f, :], const["ident"])
            ins.then_inc(t.prep_pe, 1)

    def prepare(c, b):
        for stage in (logits, gates, turn_v, cumsum, bonus, turn_a, turn_bk):
            stage(c, b)

    def means(c, b):
        pe.wait_ge(t.core_act, at(CORE_ACT, "keep_y", c))
        mm(bank[:, 6, :], const["pair_ones"], flat2(t.y[:, :, :]), start=True, stop=True).then_inc(t.close_pe, 1)

    def variances(c, b):
        pe.wait_ge(t.close_act, at(CLOSE_ACT, "centred_sq", c))
        mm(bank[:, 7, :], const["pair_ones"], flat2(t.ysq[:, :, :]), start=True, stop=True).then_inc(t.close_pe, 1)

    def close(c, b):
        means(c, b)
        variances(c, b)

    def core(c, b, nxt, prev):
        ar, bt, kt = t.ar[b], t.bt[b], t.kt[b]
        tok = {n: x[b] for n, x in t.tok.items()}

        def act(name):
            pe.wait_ge(t.core_act, at(CORE_ACT, name, c))

        def dve(name):
            pe.wait_ge(t.core_dve, at(CORE_DVE, name, c))

        def done(ins):
            ins.then_inc(t.core_pe, 1)

        pe.wait_ge(t.prep_dve, at(PREP_DVE, "decayed", c))
        for h in range(RH):
            ins = mm(bank[:, 4 + h % 2, (h // 2) * P:(h // 2 + 1) * P], ar[rows(h), h // 2, 0, :], bt[rows(h), h // 2, :],
                     start=True, stop=True)
        done(ins)
        pe.wait_ge(t.prep_act, at(PREP_ACT, "keep_k", c))
        if prev:
            pe.wait_ge(t.core_dve, before(CORE_DVE, c))
            means(*prev)
        for n in range(RH // 2):
            b0 = 2 * n % 6
            if n == 2:
                act("keep_n")
            if n == 3:
                dve("gram0")
            for w, x in enumerate((bt, kt)):
                for h in (2 * n, 2 * n + 1):
                    ins = mm(bank[:, b0 + h % 2, w * 2 * P:(w + 1) * 2 * P], x[rows(h), n, :],
                             ar[rows(h), n, :, :].rearrange("p w t -> p (w t)"), start=True, stop=True)
            done(ins)
        if prev:
            variances(*prev)
        beside = {0: logits, 1: gates, 3: turn_v, 4: cumsum}
        for lv, width in enumerate(MERGES):
            for g in "ab":
                b0 = GROUP_BANK[g]
                pe.wait_ge(t.core_pool, at(CORE_POOL, f"merge{lv}_{g}" if lv else "plus_" + g, c))
                dve(f"left{lv - 1}_{g}" if lv else {"a": "gram3", "b": "gram2"}[g])
                for n, h in enumerate(HEADS[g]):
                    m = t.merge[:, lv, h, :] if lv < len(MERGES) - 1 else t.nmat[:, h, :]
                    ins = mm(blocks(bank[:, b0 + 1, n * P // 2:(n + 1) * P // 2], width), m,
                             odd_blocks(t.p[:, h, :], width), start=True, stop=True)
                done(ins)
                for n, h in enumerate(HEADS[g]):
                    ins = nc.tensor.transpose(bank[:, b0, n * P:(n + 1) * P], t.p[:, h, :], const["ident"])
                done(ins)
            if nxt and lv in beside:
                if lv == 0 and prev:
                    pe.wait_ge(t.close_act, at(CLOSE_ACT, "roots", prev[0]))
                beside[lv](*nxt)
            for g in "ab":
                b0 = GROUP_BANK[g]
                act(f"turn{lv}_{g}")
                for n, h in enumerate(HEADS[g]):
                    ins = mm(bank[:, b0 + 2, n * P // 2:(n + 1) * P // 2], t.pt[:, h, :], t.q[:, h, :],
                             start=True, stop=True)
                done(ins)
        p7 = t.p
        dve(f"left{LEVELS[-1]}_b")
        for h in range(RH):
            ins = mm(bank[rows(h), 0, (h // 2) * P:(h // 2 + 1) * P], tok["a"][:, h * RN:(h + 1) * RN], p7[:, h, :],
                     start=True, stop=True)
        done(ins)
        for h in range(RH):
            s = slice(h * RN, (h + 1) * RN)
            ins = mm(bank[:, 1, s], t.ak[:, h, :], tok["v"][:, s], start=True, stop=True)
        done(ins)
        if nxt:
            bonus(*nxt)
        act("keep_w")
        dve("entered")
        for h in range(RH):
            o = bank[:, 3 + h % 2, (h // 2) * RN:(h // 2 + 1) * RN]
            mm(o, p7[:, h, :], t.hu[:, h, :], start=True, stop=False)
            ins = mm(o, t.wt[rows(h), h // 2, :], t.entry[rows(h), h // 2, :], start=False, stop=True)
        done(ins)
        if nxt:
            turn_a(*nxt)
        act("keep_u")
        for h in range(RH):
            o = bank[rows(h), 0, (h // 2) * RN:(h // 2 + 1) * RN]
            s = slice(h * RN, (h + 1) * RN)
            mm(o, tok["k"][:, s], tok["v"][:, s], start=True, stop=False)
            ins = mm(o, tok["b"][:, s], t.hu[:, h, :], start=False, stop=True)
        done(ins)
        if nxt:
            turn_bk(*nxt)
        for h in range(RH):
            o = bank[rows(h), 1, (h // 2) * P:(h // 2 + 1) * P]
            mm(o, t.entry[rows(h), h // 2, :], ar[rows(h), h // 2, 1, :], start=True, stop=False)
            mm(o, tok["v"][:, h * RN:(h + 1) * RN], t.rk[:, h, :], start=False, stop=False)
            ins = mm(o, t.hu[:, h, :], t.rb[:, h, :], start=False, stop=True)
        done(ins)

    pe.wait_ge(t.loaded, 64)
    pe.wait_ge(t.zeroed, 1)
    pe.sem_inc(t.prep_pe, 1)
    pe.sem_inc(t.core_pe, 1)
    pe.sem_inc(t.close_pe, 1)
    over_chunks(pe, prepare, core, close)


def rwkv_scalar(nc, act, k, t):
    bank, copy, fn = t.bank, nc.scalar.copy, nc.scalar.activation

    def pe_prep(c, name):
        act.wait_ge(t.prep_pe, at(PREP_PE, name, c))

    def done(ins):
        ins.then_inc(t.prep_act, 1)

    def loras(c, b):
        act.wait_ge(t.prep_dve, before(PREP_DVE, c))
        fn(t.lora[0:64, 0, :], t.z[0:64, c, 12, :], ACT.Tanh)
        copy(t.lora[64:128, 0, :], t.z[64:128, c, 12, :])
        copy(t.key[:, :, :], t.z[:, c, 8:12, :])
        done(fn(t.lora[:, 1, :], t.z[:, c, 13, :], ACT.Sigmoid))

    def sigmoids(c, b):
        act.wait_ge(t.prep_dve, at(PREP_DVE, "decay_bias", c))
        done(fn(t.sig_w[:, :], t.sig_w[:, :], ACT.Sigmoid))
        act.wait_ge(t.prep_dve, at(PREP_DVE, "rate_bias", c))
        done(fn(t.rate[:, :, :], t.rate[:, :, :], ACT.Sigmoid))

    def gates(c, b):
        pe_prep(c, "gates")
        if not (isinstance(c, int) and c < 2):
            act.wait_ge(t.close_dve, before(CLOSE_DVE, c - 1))
        done(copy(t.gates[b][:, :, :], t.flat(6)))
        pe_prep(c, "key_norms")
        done(fn(t.t2[:, :, :], t.flat(7), ACT.Sqrt))

    def keep_v(c, b):
        pe_prep(c, "turn_v")
        done(copy(t.tok["v"][b][:, :], bank[:, 6, :]))

    def decays(c, b):
        pe_prep(c, "cumsum")
        cum = bank[:, 6:8, :].rearrange("p b (f w t) -> p (b f) w t", f=2, w=2)
        done(fn(t.bt[b][:, :, :], cum[:, :, 0, :], ACT.Exp, scale=-1.0))
        fn(t.mid[b][:, :], cum[:, :, 1, 0], ACT.Exp, scale=-1.0)
        done(fn(t.last[b][:, :], cum[:, :, 0, P - 1], ACT.Exp))
        fn(t.ar[b][:, :, 0, :], cum[:, :, 1, :], ACT.Exp)
        done(fn(t.ar[b][:, :, 1, :], cum[:, :, 0, :], ACT.Exp))

    def bonus(c, b):
        pe_prep(c, "bonus")
        done(copy(t.bonus[b][:, :, :], t.flat(6)))

    def keep_a(c, b):
        pe_prep(c, "turn_a")
        done(copy(t.tok["a"][b][:, :], bank[:, 7, :]))

    def keep_bk(c, b):
        pe_prep(c, "turn_b")
        done(copy(t.tok["b"][b][:, :], bank[:, 6, :]))
        pe_prep(c, "turn_k")
        done(copy(t.tok["k"][b][:, :], bank[:, 7, :]))

    def prepare(c, b):
        for stage in (loras, sigmoids, gates, keep_v, decays, bonus, keep_a, keep_bk):
            stage(c, b)

    def squares(c, b):
        act.wait_ge(t.close_dve, at(CLOSE_DVE, "centred", c))
        fn(t.ysq[:, :, :], t.y[:, :, :], ACT.Square).then_inc(t.close_act, 1)

    def roots(c, b):
        act.wait_ge(t.close_pe, at(CLOSE_PE, "variances", c))
        fn(t.yroot[:, :, :], t.flat(7), ACT.Sqrt, scale=1.0 / RN, bias=k.eps[:, 2:3]).then_inc(t.close_act, 1)

    def close(c, b):
        squares(c, b)
        roots(c, b)

    def core(c, b, nxt, prev):
        def pe(name):
            act.wait_ge(t.core_pe, at(CORE_PE, name, c))

        def done(ins):
            ins.then_inc(t.core_act, 1)

        pe("gram_n")
        done(copy(t.nmat[:, :, :].rearrange("p (n e) t -> p e n t", e=2),
                  bank[:, 4:6, :].rearrange("p e (n t) -> p e n t", t=P)))
        if nxt:
            loras(*nxt)
        if prev:
            squares(*prev)
            roots(*prev)
        beside = {1: (sigmoids,), 2: (gates,), 3: (keep_v,), 4: (decays,)}
        for lv in LEVELS:
            for g in "ab":
                pe(f"join{lv}_{g}")
                done(copy(t.q[:, HS[g], :], t.half_flat(GROUP_BANK[g] + 1)))
                pe(f"turn{lv}_{g}")
                done(copy(t.pt[:, HS[g], :], t.flat(GROUP_BANK[g])))
            for stage in beside.get(lv, ()) if nxt else ():
                stage(*nxt)
        pe("removal")
        done(copy(t.wt[:, :, :], t.flat(0)))
        if nxt:
            bonus(*nxt)
        pe("removed")
        done(copy(t.hu[:, :, :].rearrange("p (n e) i -> p e n i", e=2),
                  bank[:, 3:5, 0:RT * RN].rearrange("p e (n i) -> p e n i", i=RN)))
        if nxt:
            keep_a(*nxt)
            keep_bk(*nxt)
        pe("outputs")
        act.wait_ge(t.close_dve, before(CLOSE_DVE, c))
        done(copy(t.y[:, :, :], t.flat(1)))

    act.sem_inc(t.prep_act, 1)
    act.sem_inc(t.core_act, 1)
    act.sem_inc(t.close_act, 1)
    over_chunks(act, prepare, core, close)


def rwkv_gpsimd(nc, pool, k, t):
    tt, const = nc.gpsimd.tensor_tensor, k.const

    def core(c, b, nxt, prev):
        def done(ins):
            ins.then_inc(t.core_pool, 1)

        pool.wait_ge(t.core_act, at(CORE_ACT, "keep_n", c))
        for lv, width in enumerate(MERGES):
            for g, last_pair in (("a", "gram1"), ("b", "gram3")):
                m = t.merge[:, lv, HS[g], :] if lv < len(MERGES) - 1 else t.nmat[:, HS[g], :]
                done(tt(m, t.nmat[:, HS[g], :], masks(const[f"merge{width}"], 4), ALU.mult))
                if lv == 0:
                    pool.wait_ge(t.core_dve, at(CORE_DVE, last_pair, c))
                    done(tt(t.p[:, HS[g], :], t.p[:, HS[g], :], masks(const["ident"], 4), ALU.add))

    pool.sem_inc(t.core_pool, 1)
    over_chunks(pool, lambda c, b: None, core, lambda c, b: None)


def rwkv_vector(nc, dve, k, t):
    tt, stt, recip = nc.vector.tensor_tensor, nc.vector.scalar_tensor_tensor, nc.vector.reciprocal
    bank, par, const = t.bank, k.par, k.const

    def own(c, name):
        dve.wait_ge(t.prep_dve, at(PREP_DVE, name, c))

    def act_prep(c, name):
        dve.wait_ge(t.prep_act, at(PREP_ACT, name, c))

    def done(ins):
        ins.then_inc(t.prep_dve, 1)

    def squares(c, b):
        done(tt(t.kk[:, :, :], t.z[:, c, 4:8, :], wide(par["rwkv_k_k"], P), ALU.mult))
        own(c, "raw_kk")
        done(tt(t.t1[:, :, :], t.kk[:, :, :], t.kk[:, :, :], ALU.mult))

    def biases(c, b):
        dve.wait_ge(t.prep_pe, at(PREP_PE, "decay_logits", c))
        done(tt(t.sig_w[:, :], bank[:, 6, :], t.w0[:, :], ALU.add))
        dve.wait_ge(t.prep_pe, at(PREP_PE, "rate_logits", c))
        done(tt(t.rate[:, :, :], t.flat(7), wide(par["rwkv_a0"], P), ALU.add))

    def roots(c, b):
        act_prep(c, "key_roots")
        done(nc.vector.tensor_scalar(t.t2[:, :, :], t.t2[:, :, :], 1e-12, None, ALU.max))
        own(c, "root_max")
        done(recip(t.t2[:, 0:RT // 2, :], t.t2[:, 0:RT // 2, :]))

    def norms(c, b):
        done(recip(t.t2[:, RT // 2:RT, :], t.t2[:, RT // 2:RT, :]))
        own(c, "inv_norm1")
        done(tt(t.kk[:, :, :], t.kk[:, :, :], t.t2[:, :, :], ALU.mult))

    def keys(c, b):
        k_in = t.z[:, c, 4:8, :]
        dve.wait_ge(t.prep_pe, at(PREP_PE, "turn_v", c))
        done(stt(out=t.key[:, :, :], in0=t.rate[:, :, :], scalar=-1.0, in1=k_in, op0=ALU.add, op1=ALU.mult))
        own(c, "rate_k")
        done(tt(t.key[:, :, :], t.key[:, :, :], wide(par["rwkv_k_a"], P), ALU.mult))
        own(c, "k_gain")
        done(tt(t.key[:, :, :], t.key[:, :, :], k_in, ALU.add))

    def key_products(c, b):
        own(c, "key")
        done(tt(t.rate[:, :, :], t.rate[:, :, :], t.kk[:, :, :], ALU.mult))
        done(tt(t.t2[:, :, :], t.key[:, :, :], t.z[:, c, 0:4, :], ALU.mult))
        own(c, "key_r")
        done(tt(t.t1[:, :, :], t.t2[:, :, :], wide(par["rwkv_r_k"], P), ALU.mult))

    def decays(c, b):
        ar, bt, kt = t.ar[b], t.bt[b], t.kt[b]
        act_prep(c, "up")
        done(tt(kt[:, :, :], t.key[:, :, :], bt[:, :, :], ALU.mult))
        tt(bt[:, :, :], t.rate[:, :, :], bt[:, :, :], ALU.mult)
        stt(out=ar[:, :, 0, :], in0=t.kk[:, :, :], scalar=-1.0, in1=ar[:, :, 0, :], op0=ALU.mult, op1=ALU.mult)
        done(tt(ar[:, :, 1, :], t.z[:, c, 0:4, :], ar[:, :, 1, :], ALU.mult))

    def prepare(c, b):
        for stage in (squares, biases, roots, norms, keys, key_products, decays):
            stage(c, b)

    def centre(c, b):
        dve.wait_ge(t.close_pe, at(CLOSE_PE, "means", c))
        stt(out=t.y[:, :, :], in0=t.flat(6), scalar=-1.0 / RN, in1=t.y[:, :, :], op0=ALU.mult,
            op1=ALU.add).then_inc(t.close_dve, 1)

    def invert(c, b):
        dve.wait_ge(t.close_act, at(CLOSE_ACT, "roots", c))
        recip(t.yroot[:, :, :], t.yroot[:, :, :]).then_inc(t.close_dve, 1)

    def normalise(c, b):
        y = t.y[:, :, :]
        dve.wait_ge(t.close_dve, at(CLOSE_DVE, "inv_std", c))
        tt(y, y, t.yroot[:, :, :], ALU.mult).then_inc(t.close_dve, 1)
        dve.wait_ge(t.close_dve, at(CLOSE_DVE, "normed", c))
        tt(y, y, wide(par["rwkv_ln_g"], P), ALU.mult).then_inc(t.close_dve, 1)
        tt(t.bonus[b][:, :, :], t.bonus[b][:, :, :], t.z[:, c, 8:12, :], ALU.mult).then_inc(t.close_dve, 1)

    def finish_y(c, b):
        y = t.y[:, :, :]
        dve.wait_ge(t.close_dve, at(CLOSE_DVE, "bonus_v", c))
        tt(y, y, wide(par["rwkv_ln_b"], P), ALU.add).then_inc(t.close_dve, 1)
        dve.wait_ge(t.close_dve, at(CLOSE_DVE, "with_bias", c))
        tt(y, y, t.bonus[b][:, :, :], ALU.add).then_inc(t.close_dve, 1)
        dve.wait_ge(t.close_dve, at(CLOSE_DVE, "with_bonus", c))
        tt(t.z[:, c, 0:4, :], y, t.gates[b][:, :, :], ALU.mult).then_inc(t.close_dve, 1)

    def close(c, b):
        for stage in (centre, invert, normalise, finish_y):
            stage(c, b)

    def core(c, b, nxt, prev):
        def pe(name):
            dve.wait_ge(t.core_pe, at(CORE_PE, name, c))

        def done(ins):
            ins.then_inc(t.core_dve, 1)

        def add_blocks(g, width):
            p = odd_blocks(t.p[:, HS[g], :], width)
            done(tt(p, blocks(t.half_flat(GROUP_BANK[g] + 2), width), p, ALU.add))

        if prev:
            centre(*prev)
        for n in range(RH // 2):
            pe(f"gram{n}")
            b0 = 2 * n % 6
            done(tt(t.gm[:, 2 * n:2 * n + 2, :, :].rearrange("p h w t -> p h (w t)"), bank[:, b0:b0 + 2, :],
                    masks(k.gram_masks, 2), ALU.mult))
        if nxt:
            squares(*nxt)
        if prev:
            invert(*prev)
        beside = {0: biases, 2: roots, 3: norms, 4: keys, 5: key_products}
        closing = {0: normalise, 1: finish_y}
        for lv, width in enumerate(MERGES):
            for g in "ab":
                pe(f"left{lv}_{g}")
                add_blocks(g, width)
            if nxt and lv in beside:
                beside[lv](*nxt)
            if prev and lv in closing:
                closing[lv](*prev)
        pe("chunk_h")
        done(nc.vector.tensor_copy(t.hu[:, :, :].rearrange("p h n -> p (h n)"), bank[:, 1, :]))
        dve.wait_ge(t.core_dve, before(CORE_DVE, c))
        done(tt(t.entry[:, :, :], t.state[:, :, :], wide(t.mid[b][:, :], RN), ALU.mult))
        if nxt:
            decays(*nxt)
        pe("state")
        done(tt(t.state[:, :, :], t.entry[:, :, :], bank[:, 0, 0:RT * RN].rearrange("p (f n) -> p f n", n=RN), ALU.add))
        dve.wait_ge(t.core_dve, at(CORE_DVE, "state_sum", c))
        done(tt(t.state[:, :, :], t.state[:, :, :], wide(t.last[b][:, :], RN), ALU.mult))

    nc.vector.memset(t.state[:, :, :], 0.0)
    nc.vector.memset(t.a2[0:64, :], 0.0)
    nc.vector.memset(t.w2[64:128, :], 0.0).then_inc(t.zeroed, 1)
    dve.wait_ge(t.zeroed, 1)
    dve.wait_ge(t.loaded, 64)
    dve.sem_inc(t.prep_dve, 1)
    dve.sem_inc(t.core_dve, 1)
    dve.sem_inc(t.close_dve, 1)
    over_chunks(dve, prepare, core, close)


def rwkv(nc, k, z, w2, a2, g2, w0):
    with ExitStack() as ctx:
        t = RwkvTiles(nc, ctx, z)
        with nc.Block() as block:
            @block.sync
            def _(sp):
                sp.dma_start(t.w2[0:64, :], w2).then_inc(t.loaded, 16)
                sp.dma_start(t.a2[64:128, :], a2).then_inc(t.loaded, 16)
                sp.dma_start(t.g2[:, :], g2).then_inc(t.loaded, 16)
                sp.dma_start(t.w0[:, :], w0.to_broadcast([P, HALF])).then_inc(t.loaded, 16)

            @block.tensor
            def _(pe):
                rwkv_tensor(nc, pe, k, t)

            @block.scalar
            def _(act):
                rwkv_scalar(nc, act, k, t)

            @block.gpsimd
            def _(pool):
                rwkv_gpsimd(nc, pool, k, t)

            @block.vector
            def _(dve):
                rwkv_vector(nc, dve, k, t)


def block_kernel(nc, x, mem, w_in, gla_wa2, rwkv_w2, rwkv_a2, rwkv_g2, w_out, wq_mem, wkv_mem, wo_mem, w_gate_up,
                 w_down, consts, params, rows, out):
    k = Kept()
    n_par = sum(n for _, n in PARAMS)
    keep = ExitStack()

    def hold(stack, name, shape, side="left"):
        return stack.enter_context(nc.sbuf_tensor(name, shape, F32, side=side))

    with keep:
        early = ExitStack()
        con_keep = hold(keep, "consts", [P, 2 * P])
        par = hold(keep, "params", [P, n_par])
        k.eps = hold(keep, "eps", [P, 3])
        con_early = hold(early, "consts_early", [P, (len(CONSTS) - 2) * P])
        row = hold(early, "rows", [1, GH * GK])
        k.cum_w = hold(early, "cum_w", [P, 2 * P])
        for n, name in enumerate(CONSTS):
            k.const[name] = con_keep[:, n * P:(n + 1) * P] if n < 2 else con_early[:, (n - 2) * P:(n - 1) * P]
        first = (CONSTS.index("cum_in") - 2) * P
        k.cum = con_early[:, first:first + 2 * P]
        first = (CONSTS.index("diag_up") - 2) * P
        k.gram_masks = con_early[:, first:first + 4 * P]
        k.ones_row = k.const["ones"][0:1, :]
        at_col = 0
        for name, n in PARAMS:
            k.par[name] = par[:, at_col:at_col + n]
            at_col += n
        k.row["gla_ba"] = row[0:1, :]
        loaded = keep.enter_context(nc.semaphore("consts_loaded"))
        with nc.Block() as block:
            @block.sync
            def _(sp):
                sp.dma_start(con_keep[:, :], consts[:, 0:2 * P]).then_inc(loaded, 16)
                sp.dma_start(con_early[:, :], consts[:, 2 * P:]).then_inc(loaded, 16)
                sp.dma_start(par[:, :], params).then_inc(loaded, 16)
                sp.dma_start(row[:, :], rows[:, 0:GH * GK]).then_inc(loaded, 16)

            @block.vector
            def _(dve):
                for n, e in enumerate((EPS, G_EPS, R_EPS)):
                    nc.vector.memset(k.eps[:, n:n + 1], e)

            @block.scalar
            def _(act):
                act.wait_ge(loaded, 64)
                nc.scalar.mul(k.cum_w[:, :], k.cum, -float(np.exp(-0.5)))

        def parts(stack, name, n, side="left"):
            return tuple(stack.enter_context(nc.sbuf_tensor(f"{name}_{p}", [P, n, T], F32R, side=side))
                         for p in ("hi", "lo"))

        def moving(pair):
            return lambda kt, h: tuple(x[:, kt, h * HALF:(h + 1) * HALF] for x in pair)

        h_stack = ExitStack()
        og = hold(early, "og", [P, GH, T])
        h = parts(h_stack, "h", KD, "right")
        rstd = hold(h_stack, "rstd", [P, T], "right")
        rstd_tok = hold(h_stack, "rstd_tok", [P, NC], "right")

        with ExitStack() as gl:
            gz = hold(gl, "gla_z", [P, 9, T])
            in_gla = Job([(4, w_in[:, 0:512]), (5, w_in[:, 1024:1536 + P])], moving(h), scaled_out(nc, gz, 9, rstd[:, :]))
            with ExitStack() as s2:
                weights = Weights(nc, s2, "gla_w", "left")
                weights.next = in_gla
                with ExitStack() as s3:
                    room = hold(s3, "norm_mix_room", [P, 7, D])
                    first_norm(nc, k, "norm_mix", x, k.par["norm_mix_g"], h, rstd, rstd_tok, room[:, :, :], weights)
                dense(nc, "proj_gla", k, weights, [in_gla])
            vtok = hold(gl, "gla_v", [P, NC, GH * GV])
            decays = GlaDecays(nc, k, gl, gz[:, 0:4, :], gz[:, 4:8, :], gz[0:RANK, 8, :], gla_wa2,
                               og[:, :, :].rearrange("p (n h) t -> p n (h t)", n=2))
            token_major(nc, "proj_v", h, KD, w_in[:, 512:1024], vtok, T, GH * GV, rstd_tok, decays)
            weights = Weights(nc, h_stack, "rwkv_w", "right")
            in_rwkv = Job([(R_TILES, w_in[:, G_COLS:])], moving(h), None)
            weights.next = in_rwkv
            gla(nc, k, decays, vtok, og[:, :, :], weights)

        z = hold(early, "rwkv_z", [P, R_TILES, T])
        in_rwkv.drain = shift_mix_out(nc, z, k.par["rwkv_mu"], rstd[:, :])
        dense(nc, "proj_rwkv", k, weights, [in_rwkv])
        h_stack.close()
        rwkv(nc, k, z, rwkv_w2, rwkv_a2, rwkv_g2, rows[:, GH * GK:])

        late = ExitStack()
        xT = hold(late, "xT", [P, KD, T], "right")
        weights = Weights(nc, late, "w", "right")
        mix_stack = ExitStack()
        mix = parts(mix_stack, "mix", KD, "right")
        out_job = Job([(KD, w_out)], moving(mix), None)
        weights.next = out_job
        halves_of = [og[:, n, :] for n in range(GH)] + [z[:, n, :] for n in range(RT)]
        split_tiles(nc, "split_mix", [(v, mix[0][:, n, :], mix[1][:, n, :]) for n, v in enumerate(halves_of)], weights)
        early.close()

        a = parts(late, "a", KD)
        work = hold(late, "work", [P, 3, T])
        norm_x = Norm(nc, late, "norm_mem_x", work, k.par["norm_mem_x_g"], a)
        with ExitStack() as st:
            out_job.residual = Residual(nc, st, "x_again", x)
            out_job.drain = norm_x.add_out(xT, out_job.residual)
            dense(nc, "proj_out", k, weights, [out_job])
        mix_stack.close()
        with ExitStack() as st:
            kT = hold(st, "mem_k", [P, KD, M])
            vT = hold(st, "mem_v", [P, KD, M])
            v_tok = hold(st, "mem_v_tok", [P, M // P, D])
            q_sb = hold(st, "q_sb", [P, KD, T])
            with ExitStack() as s2:
                mem_h = tuple(s2.enter_context(nc.sbuf_tensor(f"mem_h_{n}", [P, KD, M], F32R)) for n in ("hi", "lo"))
                mem_rstd = hold(s2, "mem_rstd", [P, M])
                mem_rstd_tok = hold(s2, "mem_rstd_tok", [P, M // P])
                kv_jobs = [Job([(KD, wkv_mem[:, n * D:(n + 1) * D])], lambda kt, h: tuple(p[:, kt, :] for p in mem_h),
                               scaled_out(nc, dst, KD, mem_rstd[:, :]), halves=1) for n, dst in enumerate((kT, vT))]
                q_job = Job([(KD, wq_mem)], moving(a), scaled_out(nc, q_sb, KD, norm_x.rstd), norm=norm_x)
                weights.next = kv_jobs[0]
                first_norm(nc, k, "norm_mem", mem, k.par["norm_mem_g"], mem_h, mem_rstd, mem_rstd_tok,
                           q_sb[:, 0:7, :], weights)
                dense(nc, "proj_mem", k, weights, kv_jobs + [q_job])
            clear_semaphores(nc, PAST)

            norm_f = Norm(nc, late, "norm_ffn", work, k.par["norm_ffn_g"], None)
            o_job = Job([(KD, wo_mem)], moving(a), None)
            weights.next = o_job
            attention(nc, k, q_sb, kT, vT, v_tok, a, work[:, 0, :], weights)

        f_stack = ExitStack()
        norm_f.parts = f = parts(f_stack, "f", KD, "right")
        norm_last = Norm(nc, late, "norm_final", work, k.par["norm_final_g"], None)
        o_job.drain = norm_f.add_out(xT)
        gate = Gate(nc, late, "gate", norm_f.full, norm_f.squares, norm_f.rstd, a)
        jobs = [o_job]
        first = 0
        for n, width in enumerate(FF_GROUPS):
            gate_drain, hidden_ready = gate.group(width)
            jobs.append(Job([(2 * width, (w_gate_up, first))], moving(f), gate_drain,
                            tile_ready=norm_f.tile_ready if n == 0 else None, norm=norm_f if n == 0 else None))
            first += width
            cols = slice((first - width) * P, first * P)
            jobs.append(Job([(KD, w_down[cols, :])], moving(a),
                            norm_last.add_out(xT) if first == FT else add_out(nc, xT), tile_ready=hidden_ready))
        dense(nc, "ffn", k, weights, jobs)
        f_stack.close()
        finish(nc, k, "store", xT, norm_last.total, out)
        late.close()


def attention(nc, k, q_sb, kT, vT, vm, o_sb, room, weights):
    scale = float(AD) ** -0.5
    with ExitStack() as ctx:
        sb, ps, sem = tiles(nc, ctx, "attn")
        q_c = sb("q_c", [P, 2, KD, P])
        top, bias, total, inv = (sb(n, [P, 2, AH]) for n in ("top", "bias", "total", "inv"))
        e = sb("e", [P, 2, AH, M])
        pT = room.rearrange("p (h m t) -> p h m t", h=AH, m=2)
        score_b, turn_b, out_b = ps("score_b", [P, 2, AH, M]), ps("turn_b", [P, AH, 2, P]), ps("out_b", [P, KD, P])
        q_copied, scored, topped, biased, raised = (sem(n) for n in ("q_copied", "scored", "topped", "biased", "raised"))
        inverted, weighed, turned, p_copied = (sem(n) for n in ("inverted", "weighed", "turned", "p_copied"))
        output, rounded, split = sem("output"), sem("rounded"), sem("split")
        values_turned, values_kept = sem("values_turned"), sem("values_kept")
        cq = q_sb[:, :, :].rearrange("p f (c t) -> p c f t", t=P)
        co, co_lo = (x[:, :, :].rearrange("p f (c t) -> p c f t", t=P) for x in o_sb)
        with nc.Block() as block:
            @block.sync
            def _(sp):
                weights.start_loading(sp)

            @block.gpsimd
            def _(pool):
                weights.start_splitting(pool)

            @block.tensor
            def _(pe):
                def scores(c, u):
                    pe.wait_ge(q_copied, c + 1)
                    for h in range(AH):
                        for n in range(2):
                            ins = nc.tensor.matmul(score_b[:, u, h, :], q_c[:, u, 2 * h + n, :], kT[:, 2 * h + n, :],
                                                   start=(n == 0), stop=(n == 1))
                    ins.then_inc(scored, 1)

                def turn(i, u):
                    c = 2 * i + u
                    most, latest = near(i, u, 2)
                    pe.wait_ge(weighed, c + 1)
                    for h in range(AH):
                        for m in range(2):
                            ins = nc.tensor.transpose(turn_b[:, h, m, :], e[:, u, h, m * P:(m + 1) * P], k.const["ident"])
                    ins.then_inc(turned, 1)
                    if most:
                        scores(latest, u)
                    pe.wait_ge(p_copied, c + 1)
                    if not (isinstance(c, int) and c == 0):
                        pe.wait_ge(split, c)
                    for f in range(KD):
                        for m in range(2):
                            ins = nc.tensor.matmul(out_b[:, f, :], vm[:, m, f * P:(f + 1) * P], pT[:, f // 2, m, :],
                                                   start=(m == 0), stop=(m == 1))
                    ins.then_inc(output, 1)

                for m, b in enumerate((turn_b[:, :, :, :].rearrange("p h m t -> p (h m) t"), out_b)):
                    for f in range(KD):
                        ins = nc.tensor.transpose(b[:, f, :], vT[:, f, m * P:(m + 1) * P], k.const["ident"])
                    ins.then_inc(values_turned, 1)
                scores(0, 0)
                scores(1, 1)
                pe.wait_ge(values_kept, 2)
                pipelined(pe, turn, 3, 0)

            @block.scalar
            def _(act):
                def copy_q(c, u):
                    nc.scalar.copy(q_c[:, u], cq[:, c]).then_inc(q_copied, 1)

                def raise_e(c, u):
                    act.wait_ge(biased, c + 1)
                    for h in range(AH):
                        ins = nc.scalar.activation(e[:, u, h, :], score_b[:, u, h, :], ACT.Exp, bias=bias[:, u, h:h + 1],
                                                   scale=scale, accum_out=total[:, u, h:h + 1])
                    ins.then_inc(raised, 1)

                def turn(i, u):
                    c = 2 * i + u
                    more, later = near(i, u, 1)
                    most, latest = near(i, u, 3)
                    act.wait_ge(turned, c + 1)
                    if not (isinstance(c, int) and c == 0):
                        act.wait_ge(output, c)
                    nc.scalar.copy(pT[:, :, :, :], turn_b[:, :, :, :]).then_inc(p_copied, 1)
                    if more:
                        raise_e(later, 1 - u)
                    if most:
                        copy_q(latest, 1 - u)
                    act.wait_ge(output, c + 1)
                    nc.scalar.copy(co[:, c], out_b[:, :, :]).then_inc(rounded, 1)

                weights.start_rounding(act)
                copy_q(0, 0)
                copy_q(1, 1)
                act.wait_ge(values_turned, 1)
                nc.scalar.copy(vm[:, 0, :], turn_b[:, :, :, :].rearrange("p h m t -> p (h m t)")).then_inc(values_kept, 1)
                raise_e(0, 0)
                copy_q(2, 0)
                pipelined(act, turn, 3, 0)

            @block.vector
            def _(dve):
                def softmax(c, u):
                    dve.wait_ge(scored, c + 1)
                    nc.vector.tensor_reduce(top[:, u, :], score_b[:, u], mybir.AxisListType.X, ALU.max).then_inc(topped, 1)
                    dve.wait_ge(topped, c + 1)
                    nc.vector.tensor_scalar(bias[:, u, :], top[:, u, :], -scale, None, ALU.mult).then_inc(biased, 1)
                    dve.wait_ge(raised, c + 1)
                    nc.vector.reciprocal(inv[:, u, :], total[:, u, :]).then_inc(inverted, 1)
                    dve.wait_ge(inverted, c + 1)
                    nc.vector.tensor_tensor(e[:, u], e[:, u], wide(inv[:, u, :], M), ALU.mult).then_inc(weighed, 1)

                def turn(i, u):
                    c = 2 * i + u
                    more, later = near(i, u, 1)
                    if more:
                        softmax(later, 1 - u)
                    dve.wait_ge(rounded, c + 1)
                    nc.vector.tensor_tensor(co_lo[:, c], out_b[:, :, :], co[:, c].bitcast(F32),
                                            ALU.subtract).then_inc(split, 1)

                dve.wait_ge(values_turned, 2)
                nc.vector.tensor_copy(vm[:, 1, :], out_b[:, :, :].rearrange("p f t -> p (f t)")).then_inc(values_kept, 1)
                softmax(0, 0)
                pipelined(dve, turn, 3, 0)


WEIGHTS = ["w_in", "gla_wa2", "rwkv_w2", "rwkv_a2", "rwkv_g2", "w_out", "wq_mem", "wkv_mem", "wo_mem", "w_gate_up",
           "w_down"]


def kernel(**inputs):
    import concourse.bacc as bacc
    from concourse.bass_utils import run_bass_kernel_spmd

    nc = bacc.Bacc("TRN2", target_bir_lowering=False, num_devices=1)
    a = {name: np.ascontiguousarray(value) for name, value in inputs.items()}
    arrays = {"x": a["x"][0], "mem": a["mem"][0]}
    arrays.update({name: a[name][0] for name in WEIGHTS})
    arrays["consts"] = constants()
    arrays["params"] = np.concatenate([a[name].reshape(n, P).T for name, n in PARAMS], axis=1)
    arrays["rows"] = np.concatenate([a[name].reshape(1, n) for name, n in ROWS], axis=1)
    arrays = {name: np.ascontiguousarray(value) for name, value in arrays.items()}
    args = [nc.dram_tensor(f"in_{name}", value.shape, F32, kind="ExternalInput").ap()
            for name, value in arrays.items()]
    args.append(nc.dram_tensor("out_0", (T, D), F32, kind="ExternalOutput").ap())
    block_kernel(nc, *args)
    r = run_bass_kernel_spmd(nc, [{f"in_{name}": value for name, value in arrays.items()}], core_ids=[0])
    return r.results[0]["out_0"].reshape(1, T, D)
```
